# Optimizing a Trainium2 kernel written in Bass

```python
import jax, jax.numpy as jnp
from jax import lax
import numpy as np

D_MODEL = 1024
BATCH = 1
SEQ = 256
DEPTH = 1

PLE_DIM = 256
HEAD_DIM = 64
RWKV_HEADS = 8
RWKV_DIM = RWKV_HEADS * HEAD_DIM
W_LORA = 64
A_LORA = 64
G_LORA = 128
ATTN_GROUPS = ((128, 1), (512, 4), (2048, 16))
HEADS_PER_GROUP = 8
ATTN_HEADS = HEADS_PER_GROUP * len(ATTN_GROUPS)
ATTN_DIM = ATTN_HEADS * HEAD_DIM
ATTN_OUT_DIM = HEADS_PER_GROUP * HEAD_DIM
Q_BLOCK = 128
N_BRANCHES = 2
RWKV_COLS = 3 * RWKV_DIM + W_LORA + A_LORA + G_LORA
ATTN_COLS = 3 * ATTN_DIM
GATE_COLS = N_BRANCHES * D_MODEL
IN_COLS = RWKV_COLS + ATTN_COLS + GATE_COLS
N_EXPERT_GROUPS = 4
EXPERTS_PER_GROUP = 8
TOP_K_EXPERT = 2
D_FF_EXPERT = 256
NORM_EPS = 1e-6
RWKV_GN_EPS = 64e-5

kernel_name = "hybrid_rwkv7_dilated_alibi_hmoe_block"

def rmsnorm(x, gain):
    x32 = x.astype(jnp.float32)
    return x32 * lax.rsqrt(jnp.mean(x32 * x32, axis=-1, keepdims=True) + NORM_EPS) * gain

def token_shift(t, mu):
    prev = jnp.pad(t[:, :-1], ((0, 0), (1, 0), (0, 0)))
    return t + (prev - t) * mu

def wkv7_scan(r, decay, k, v, kk, a):
    b, s, h, n = r.shape

    def step(state, inp):
        r_t, w_t, k_t, v_t, kk_t, a_t = inp
        sa = jnp.einsum('bhij,bhj->bhi', state, -kk_t)
        state = (state * w_t[:, :, None, :]
                 + sa[..., :, None] * (kk_t * a_t)[:, :, None, :]
                 + v_t[..., :, None] * k_t[:, :, None, :])
        y = jnp.einsum('bhij,bhj->bhi', state, r_t)
        return state, y

    xs = tuple(jnp.moveaxis(t, 1, 0) for t in (r, decay, k, v, kk, a))
    state0 = jnp.zeros((b, h, n, n), jnp.float32)
    _, ys = lax.scan(step, state0, xs)
    return jnp.moveaxis(ys, 0, 1)

def rwkv7_time_mix(z, w0, w2, a0, a2, g2, k_k, k_a, r_k, ln_w, ln_b):
    z = z.astype(jnp.float32)
    b, s, _ = z.shape
    o1, o2, o3 = RWKV_DIM, 2 * RWKV_DIM, 3 * RWKV_DIM
    o4, o5 = o3 + W_LORA, o3 + W_LORA + A_LORA
    r, k, v = z[..., :o1], z[..., o1:o2], z[..., o2:o3]
    w_d, a_d, g_d = z[..., o3:o4], z[..., o4:o5], z[..., o5:]
    w_log = -jax.nn.softplus(-(w0 + jnp.tanh(w_d) @ w2)) - 0.5
    decay = jnp.exp(-jnp.exp(w_log))
    a = jax.nn.sigmoid(a0 + a_d @ a2)
    g = jax.nn.sigmoid(g_d) @ g2
    heads = lambda t: t.reshape(b, s, RWKV_HEADS, HEAD_DIM)
    kk = heads(k * k_k)
    kk = kk * lax.rsqrt(jnp.sum(kk * kk, axis=-1, keepdims=True) + 1e-12)
    k = k * (1.0 + (a - 1.0) * k_a)
    rh, kh, vh = heads(r), heads(k), heads(v)
    y = wkv7_scan(rh, heads(decay), kh, vh, kk, heads(a))
    mean = jnp.mean(y, axis=-1, keepdims=True)
    var = jnp.mean(jnp.square(y - mean), axis=-1, keepdims=True)
    y = ((y - mean) * lax.rsqrt(var + RWKV_GN_EPS)).reshape(b, s, RWKV_DIM) * ln_w + ln_b
    y = y + (jnp.sum(rh * kh * r_k, axis=-1, keepdims=True) * vh).reshape(b, s, RWKV_DIM)
    return y * g

def alibi_slopes(n_heads):
    return jnp.asarray(2.0 ** (-8.0 * np.arange(1, n_heads + 1) / n_heads), dtype=jnp.float32)

def dilated_window_attention(q, k, v, slopes, window, dilation):
    b, s, h, hd = q.shape
    d = dilation
    n_back = window // dilation
    span = d * Q_BLOCK
    s_pad = -(-s // span) * span
    L = s_pad // d
    nb = L // Q_BLOCK

    def to_blocks(t):
        t = jnp.pad(t.astype(jnp.float32), ((0, 0), (0, s_pad - s), (0, 0), (0, 0)))
        t = t.reshape(b, L, d, h, hd).transpose(0, 2, 1, 3, 4)
        return t.reshape(b * d, nb, Q_BLOCK, h, hd)

    def with_prev(t):
        prev = jnp.pad(t[:, :-1], ((0, 0), (1, 0), (0, 0), (0, 0), (0, 0)))
        return jnp.concatenate([prev, t], axis=2)

    qb = to_blocks(q)
    kc, vc = with_prev(to_blocks(k)), with_prev(to_blocks(v))
    scores = jnp.einsum('znqhd,znkhd->znhqk', qb, kc) * (HEAD_DIM ** -0.5)
    delta = (jnp.arange(Q_BLOCK)[:, None] + Q_BLOCK) - jnp.arange(2 * Q_BLOCK)[None, :]
    key_idx = jnp.arange(nb)[:, None, None] * Q_BLOCK + jnp.arange(2 * Q_BLOCK)[None, None, :] - Q_BLOCK
    valid = (delta >= 0)[None] & (delta <= n_back)[None] & (key_idx >= 0)
    alibi = -slopes[:, None, None] * (d * delta).astype(jnp.float32)[None]
    scores = jnp.where(valid[None, :, None], scores + alibi[None, None], -jnp.inf)
    lse = jax.nn.logsumexp(scores, axis=-1)
    probs = jnp.exp(scores - lse[..., None])
    out = jnp.einsum('znhqk,znkhd->znqhd', probs, vc)
    out = out.reshape(b, d, L, h, hd).transpose(0, 2, 1, 3, 4).reshape(b, s_pad, h, hd)[:, :s]
    lse = lse.transpose(0, 1, 3, 2).reshape(b, d, L, h).transpose(0, 2, 1, 3).reshape(b, s_pad, h)[:, :s]
    return out, lse

def dilated_mixture_attention(qkv, slopes):
    b, s, _ = qkv.shape
    qkv = qkv.reshape(b, s, 3, ATTN_HEADS, HEAD_DIM)
    q, k, v = qkv[:, :, 0], qkv[:, :, 1], qkv[:, :, 2]
    outs, lses = [], []
    for g, (window, dilation) in enumerate(ATTN_GROUPS):
        sl = slice(g * HEADS_PER_GROUP, (g + 1) * HEADS_PER_GROUP)
        o, l = dilated_window_attention(q[:, :, sl], k[:, :, sl], v[:, :, sl], slopes[sl], window, dilation)
        outs.append(o)
        lses.append(l)
    outs = jnp.stack(outs, axis=0)
    alpha = jax.nn.softmax(jnp.stack(lses, axis=0), axis=0)
    return jnp.sum(alpha[..., None] * outs, axis=0).reshape(b, s, ATTN_OUT_DIM)

def hierarchical_moe(h, w_router_group, w_router_expert, w_exp_gate, w_exp_up, w_exp_down):
    b, s, dm = h.shape
    ht = h.reshape(b * s, dm)
    grp_probs = jax.nn.softmax((ht @ w_router_group).astype(jnp.float32), axis=-1)
    grp_w, grp_idx = lax.top_k(grp_probs, 1)
    exp_logits = jnp.einsum('td,gde->tge', ht, w_router_expert).astype(jnp.float32)
    sel = jnp.take_along_axis(exp_logits, grp_idx[:, :, None], axis=1)[:, 0]
    top_v, top_i = lax.top_k(sel, TOP_K_EXPERT)
    top_w = jax.nn.softmax(top_v, axis=-1) * grp_w
    within = jnp.sum(jax.nn.one_hot(top_i, EXPERTS_PER_GROUP, dtype=jnp.float32) * top_w[..., None], axis=1)
    combine = jax.nn.one_hot(grp_idx[:, 0], N_EXPERT_GROUPS, dtype=jnp.float32)[:, :, None] * within[:, None, :]
    y = jnp.zeros((b * s, dm), jnp.float32)
    for g in range(N_EXPERT_GROUPS):
        hg = jnp.einsum('td,edf->tef', ht, w_exp_gate[g])
        hu = jnp.einsum('td,edf->tef', ht, w_exp_up[g])
        act = jax.nn.silu(hg) * hu * combine[:, g, :, None]
        y = y + jnp.einsum('tef,efd->td', act, w_exp_down[g])
    return y.reshape(b, s, dm)

def setup_inputs(seed: int = 0) -> dict:
    key = jax.random.key(seed)
    ks = jax.random.split(key, 28)
    f32 = jnp.float32
    nrm = lambda k, shape, scale: jax.random.normal(k, shape, f32) * scale
    gain = lambda k, shape: 1.0 + 0.05 * jax.random.normal(k, shape, f32)
    E, G, F = EXPERTS_PER_GROUP, N_EXPERT_GROUPS, D_FF_EXPERT
    return {
        "x": nrm(ks[0], (BATCH, SEQ, D_MODEL), 1.0),
        "p": nrm(ks[1], (DEPTH, BATCH, SEQ, PLE_DIM), 1.0),
        "norm_mix": gain(ks[2], (DEPTH, D_MODEL)),
        "w_in": nrm(ks[3], (DEPTH, D_MODEL, IN_COLS), D_MODEL ** -0.5),
        "rwkv_mu": jax.random.uniform(ks[4], (DEPTH, RWKV_COLS), f32),
        "rwkv_w0": jax.random.uniform(ks[5], (DEPTH, RWKV_DIM), f32, -6.0, 1.0),
        "rwkv_w2": nrm(ks[6], (DEPTH, W_LORA, RWKV_DIM), 0.5 * W_LORA ** -0.5),
        "rwkv_a0": nrm(ks[7], (DEPTH, RWKV_DIM), 0.5),
        "rwkv_a2": nrm(ks[8], (DEPTH, A_LORA, RWKV_DIM), 0.5 * A_LORA ** -0.5),
        "rwkv_g2": nrm(ks[9], (DEPTH, G_LORA, RWKV_DIM), G_LORA ** -0.5),
        "rwkv_k_k": 0.85 + nrm(ks[10], (DEPTH, RWKV_DIM), 0.05),
        "rwkv_k_a": 1.0 + nrm(ks[11], (DEPTH, RWKV_DIM), 0.05),
        "rwkv_r_k": nrm(ks[12], (DEPTH, RWKV_HEADS, HEAD_DIM), 0.1),
        "rwkv_ln_w": gain(ks[13], (DEPTH, RWKV_DIM)),
        "rwkv_ln_b": nrm(ks[14], (DEPTH, RWKV_DIM), 0.02),
        "w_proj_a": nrm(ks[15], (DEPTH, RWKV_DIM, D_MODEL), RWKV_DIM ** -0.5),
        "w_proj_b": nrm(ks[16], (DEPTH, ATTN_OUT_DIM, D_MODEL), ATTN_OUT_DIM ** -0.5),
        "w_out": nrm(ks[17], (DEPTH, D_MODEL, D_MODEL), D_MODEL ** -0.5),
        "norm_moe": gain(ks[18], (DEPTH, D_MODEL)),
        "w_router_group": nrm(ks[19], (DEPTH, D_MODEL, G), D_MODEL ** -0.5),
        "w_router_expert": nrm(ks[20], (DEPTH, G, D_MODEL, E), D_MODEL ** -0.5),
        "w_exp_gate": nrm(ks[21], (DEPTH, G, E, D_MODEL, F), D_MODEL ** -0.5),
        "w_exp_up": nrm(ks[22], (DEPTH, G, E, D_MODEL, F), D_MODEL ** -0.5),
        "w_exp_down": nrm(ks[23], (DEPTH, G, E, F, D_MODEL), F ** -0.5),
        "norm_ple": gain(ks[24], (DEPTH, D_MODEL)),
        "w_ple_gate": nrm(ks[25], (DEPTH, D_MODEL, D_MODEL), D_MODEL ** -0.5),
        "w_ple_proj": nrm(ks[26], (DEPTH, PLE_DIM, D_MODEL), PLE_DIM ** -0.5),
        "norm_final": gain(ks[27], (D_MODEL,)),
    }

def reference(x, p, norm_mix, w_in, rwkv_mu, rwkv_w0, rwkv_w2, rwkv_a0, rwkv_a2, rwkv_g2,
              rwkv_k_k, rwkv_k_a, rwkv_r_k, rwkv_ln_w, rwkv_ln_b, w_proj_a, w_proj_b, w_out,
              norm_moe, w_router_group, w_router_expert, w_exp_gate, w_exp_up, w_exp_down,
              norm_ple, w_ple_gate, w_ple_proj, norm_final):
    slopes = alibi_slopes(ATTN_HEADS)
    b, s, _ = x.shape
    x = x.astype(jnp.float32)
    for i in range(DEPTH):
        h = rmsnorm(x, norm_mix[i])
        proj = h @ w_in[i]
        z_rwkv = token_shift(proj[..., :RWKV_COLS], rwkv_mu[i])
        qkv = proj[..., RWKV_COLS:RWKV_COLS + ATTN_COLS]
        gates = jax.nn.sigmoid(proj[..., RWKV_COLS + ATTN_COLS:].astype(jnp.float32))
        gates = gates.reshape(b, s, N_BRANCHES, D_MODEL)
        y_a = rwkv7_time_mix(z_rwkv, rwkv_w0[i], rwkv_w2[i], rwkv_a0[i], rwkv_a2[i], rwkv_g2[i],
                             rwkv_k_k[i], rwkv_k_a[i], rwkv_r_k[i], rwkv_ln_w[i], rwkv_ln_b[i])
        y_b = dilated_mixture_attention(qkv, slopes)
        merged = gates[:, :, 0] * (y_a @ w_proj_a[i]) + gates[:, :, 1] * (y_b @ w_proj_b[i])
        x = x + merged @ w_out[i]
        x = x + hierarchical_moe(rmsnorm(x, norm_moe[i]), w_router_group[i], w_router_expert[i],
                                 w_exp_gate[i], w_exp_up[i], w_exp_down[i])
        ple_gate = jax.nn.sigmoid(rmsnorm(x, norm_ple[i]) @ w_ple_gate[i])
        x = x + ple_gate * (p[i] @ w_ple_proj[i])
    return rmsnorm(x, norm_final)


_drawn_inputs = setup_inputs


def setup_inputs(seed=0):
    import zlib

    import numpy as np

    out = dict(_drawn_inputs(seed))
    spreads = {}
    factors = {'rwkv_w2': 4.077, 'rwkv_k_k': 4.062, 'rwkv_ln_b': 8.0, 'norm_ple': 6.568}
    for name, (base, spread) in spreads.items():
        noise = np.random.default_rng([zlib.crc32(name.encode()), seed]).standard_normal(out[name].shape)
        drawn = base * np.exp(spread * noise) if base else spread * noise
        out[name] = __import__('jax').numpy.asarray(drawn.astype(out[name].dtype))
    for name, factor in factors.items():
        out[name] = (out[name] * factor).astype(out[name].dtype)
    return out
```

```python
import concourse.bass as bass
from concourse import mybir
from contextlib import ExitStack

F32 = mybir.dt.float32
I32 = mybir.dt.int32
ACT = mybir.ActivationFunctionType
ALU = mybir.AluOpType
AX = mybir.AxisListType.X

P = 128
D = 1024
T = 256
KD = D // P
NT = T // P
RW = 512
NPAIR = RW // P
HD = 64
W_LORA = 64
NH = 8
CH = 64
NG_ATT = 3
E = 32
EG = 4
F = 256
SLOTS = 32
BATCH = P // SLOTS
NBATCH = E // BATCH
NPASS = T // SLOTS
UNIT = 2048
RING = 3
LEVELS = 6
DECAY = 0.6065306597126334
EPS = 1e-6
GN_EPS = 64e-5
FAR = -1.0e30

CST = {}
CVEC = {}


def _columns(table, spec, at=0):
    for name, n in spec:
        table[name] = (at, n)
        at += n
    return at


N_CST = _columns(CST, [("ident", P), ("ones", P), ("before", P), ("slot", T), ("key_g", EG), ("key_e", E),
                       ("full", NPASS), ("eps", 4)])
N_CRW = _columns(CST, [("block", P), ("causal", 4 * P), ("level", LEVELS * P), ("level0T", P), ("reset", NPAIR * T)], N_CST)
N_CVEC = _columns(CVEC, [("norm_mix", KD), ("mu", 14), ("w0", NPAIR), ("a0", NPAIR), ("k_k", NPAIR), ("k_a", NPAIR),
                         ("r_k", NPAIR), ("ln_w", NPAIR), ("ln_b", NPAIR)])
SLOPES = [2.0 ** (-8.0 * (i + 1) / 24) for i in range(24)]


def program(nc, xT, xtok, pT, cst, crw, neg, cvec, lora, g2, stream, gain3, router, wgu, wd, wpg, wpp, out):
    ctx = ExitStack()
    with ctx:
        def sem(name):
            return ctx.enter_context(nc.semaphore(name))

        COLS = 53000
        mem = ctx.enter_context(nc.sbuf_tensor("mem", [P, COLS], F32))
        npass_i = ctx.enter_context(nc.sbuf_tensor("npass_i", [1, 1], I32))
        ps = ctx.enter_context(nc.psum_tensor("ps", [P, 8, 512], F32))

        def region(lo, hi):
            at = [lo]

            def take(*dims):
                n = 1
                for d in dims:
                    n *= d
                v = mem[:, at[0]:at[0] + n]
                at[0] += n
                assert at[0] <= hi, (at[0], hi)
                names = "abcd"[:len(dims)]
                if len(dims) > 1:
                    v = v.rearrange(f"p ({' '.join(names)}) -> p {' '.join(names)}",
                                    **{m: d for m, d in zip(names[1:], dims[1:])})
                return v
            return take

        GU0, GU1, DN, HIGH = 0, 16384, 32768, 40960
        take = region(GU0, DN)
        gu_w = [[take(KD, 2 * F) for _ in range(BATCH)] for _ in range(2)]
        take = region(DN, HIGH)
        dn_w = [take(F // P, D) for _ in range(BATCH)]
        ring_at = DN - RING * UNIT
        ring = [mem[:, ring_at + i * UNIT:ring_at + (i + 1) * UNIT] for i in range(RING)]

        take = region(HIGH, COLS)
        c_all = take(N_CST)
        cv = take(N_CVEC)
        small = take(320)
        high_pre = HIGH + N_CST + N_CVEC + 320
        x1 = take(NT, D)
        h2 = take(NT, D)
        sel = take(NT, E * SLOTS)
        hg = take(KD, P)
        selw = take(NT, P)
        silu = take(F)
        act = take(F)
        actT = take(F // P, P)
        ysb = take(D)
        selwT = take(NT, P)
        zero = take(512)
        take = region(HIGH + N_CST + N_CVEC, high_pre)
        rmask = take(NT, E)
        comb = take(NT, E)
        posm = take(NT, E)
        stat = take(64)
        stat_a = take(32)
        st_max = stat[:, 0:16]

        take = region(high_pre, COLS)
        hT = take(KD, T)
        yaT = take(NPAIR, T)
        ybT = take(NPAIR, T)
        crw_sb = take(N_CRW - N_CST)
        lora_sb = take(2, RW)
        g2_sb = take(RW)
        take = region(GU0, ring_at)
        prep = take(8, NPAIR, T)
        rT, kT, aT_, kkT, swT, cumT, wexT, winvT = [prep[:, i] for i in range(8)]
        mats = prep[:, 0:4].rearrange("p s n t -> p (s n t)").rearrange("p (n b c) -> p n b c", n=NPAIR, b=2)
        M_sb, X_sb, Z_sb, T1_sb = [prep[:, 4 + i].rearrange("p n t -> p (n t)").rearrange("p (h t) -> p h t", h=NH)
                                   for i in range(4)]
        vT = take(NPAIR, T)
        gT = take(NPAIR, T)
        bonus = take(NPAIR, T)
        wincT = take(NPAIR, T)
        arz = take(NPAIR, 2, 2, T)
        bT = take(NPAIR, T)
        kaT = take(NPAIR, T)
        rhoT = take(NPAIR, T)
        mlev = take(2, NH, P)
        alT = mlev[:, 0].rearrange("p h t -> p (h t)").rearrange("p (n t) -> p n t", n=NPAIR)
        tok = take(4, NT, RW)
        Atok, Btok, Ktok, Vtok = [tok[:, i] for i in range(4)]
        take = region(DN, HIGH)
        NV = take(RW)
        XNV = take(RW)
        XAT = take(NPAIR, P)
        U_sb = take(RW)
        Th = take(5, NPAIR, P)
        yc = take(NH, HD)
        ysq = take(NH, HD)
        shift = take(2, T + 1)
        lin = take(2, T)
        tmpT = take(NPAIR, P)
        dlt = ysq.rearrange("p h d -> p (h d)").rearrange("p (c t) -> p c t", c=2)
        take = region(GU0, ring_at)
        xT_sb = take(KD, T)
        sq = take(KD, T)
        rstd_bc = take(T)
        take = region(GU1, ring_at)
        qT = take(NG_ATT * NPAIR, T)
        kz = take(NG_ATT * NPAIR, 2, T)
        take = region(DN, HIGH)
        vtok = take(NT, NG_ATT * RW)
        Ssb = take(2, 2, NG_ATT * 384)
        take = region(high_pre + 4096, COLS)
        neg_sb = take(NG_ATT, 384)
        PT = take(2, 384)
        take = region(GU1, ring_at)
        mT = take(KD, T)
        sga = take(512)
        sgb = take(512)
        ma = take(512)
        mb = take(512)
        xt_sb = take(NT, D)
        h2T = take(KD, T)
        gmoe = take(D)
        wr = take(KD, 36)
        rt = take(NT, 36)
        take = region(GU0, GU1)
        wpg_sb = take(KD, D)
        wpp_sb = take(T // P, D)
        pT_sb = take(T // P, T)
        gple = take(D)
        gfin = take(D)
        take = region(GU1, DN)
        h3T = take(KD, T)
        gate = take(NT, D)
        h3 = h2

        def C(name):
            at, n = CST[name]
            return c_all[:, at:at + n] if at < N_CST else crw_sb[:, at - N_CST:at - N_CST + n]

        def V(name, i):
            at = CVEC[name][0] + i
            return cv[:, at:at + 1]

        ident = C("ident")

        sems = {}

        def S(name):
            if name not in sems:
                sems[name] = ctx.enter_context(nc.semaphore("s_" + name))
            return sems[name]

        class Chain:

            def __init__(self, eng, own):
                self.eng, self.own, self.n = eng, own, {}

            def __call__(self, ins, signal=None):
                name = signal or self.own
                self.n[name] = self.n.get(name, 0) + 1
                ins.then_inc(S(name), 1)
                self.eng.wait_ge(S(name), self.n[name])

        class LoopChain:

            def __init__(self, eng, own, trip, per):
                self.eng, self.own, self.trip, self.per, self.n = eng, own, trip, per, 0

            def __call__(self, ins):
                self.n += 1
                ins.then_inc(S(self.own), 1)
                self.eng.wait_ge(S(self.own), self.trip * self.per + self.n)

            def close(self):
                assert self.n == self.per, (self.own, self.n)

        block = ctx.enter_context(nc.Block())
        W0 = N_CRW - N_CST

        @block.sync
        def _(sp):
            sp.dma_start(c_all, cst).then_inc(S("ld_cst"), 16)
            sp.dma_start(cv, cvec).then_inc(S("ld_cvec"), 16)
            sp.dma_start(xT_sb, xT).then_inc(S("ld_xT"), 16)

            def unit(n, slot, first=False):
                if not first:
                    sp.wait_ge(S("unit_used"), n - RING + 1)
                sp.dma_start(ring[slot], stream[bass.ds(n, 1)].rearrange("a p n -> p (a n)")).then_inc(
                    S(f"unit_landed{slot}"), 16)

            for n in range(RING):
                unit(n, n, first=True)
            sp.dma_start(crw_sb, crw).then_inc(S("ld_crw"), 16)
            sp.dma_start(lora_sb, lora).then_inc(S("ld_lora"), 16)
            sp.dma_start(g2_sb, g2).then_inc(S("ld_g2"), 16)
            for n in range(RING, 7):
                unit(n, n % RING)

            def load_gate_up(trip, i, q, fresh):
                for e in range(BATCH):
                    which = i * (2 * BATCH) + q * BATCH + e
                    if not fresh and e == 0:
                        sp.wait_ge(S("gu_used"), 2 * trip + q)
                    sp.dma_start(gu_w[q][e], wgu[bass.ds(which, 1)].rearrange("a p k f -> p (a k) f")).then_inc(
                        S(f"gu_landed{q}{e}"), 16)

            def load_down(trip, i, q, fresh):
                for e in range(BATCH):
                    which = i * (2 * BATCH) + q * BATCH + e
                    if not fresh and e == 0:
                        sp.wait_ge(S("dn_out"), 2 * (2 * trip + q))
                    sp.dma_start(dn_w[e], wd[bass.ds(which, 1)].rearrange("a p k f -> p (a k) f")).then_inc(
                        S(f"dn_landed{e}"), 16)

            def load(trip, i, q, fresh):
                load_gate_up(trip, i, q, fresh)
                load_down(trip, i, q, fresh)

            with sp.Fori(0, 6) as i:
                for j in range(RING):
                    unit(7 + RING * i + j, (7 + j) % RING)
            sp.wait_ge(S("ya_out"), NT)
            sp.dma_start(neg_sb, neg).then_inc(S("ld_neg"), 16)
            load_gate_up(0, 0, 0, True)
            sp.wait_ge(S("scores_out"), NPAIR)
            sp.dma_start(xt_sb, xtok).then_inc(S("ld_x"), 16)
            sp.dma_start(gmoe, gain3[0]).then_inc(S("ld_gmoe"), 16)
            sp.dma_start(wr, router).then_inc(S("ld_wr"), 16)
            with sp.Fori(0, 4) as i:
                for j in range(RING):
                    unit(25 + RING * i + j, (25 + j) % RING)
            for n in range(37, 41):
                unit(n, n % RING)
            sp.wait_ge(S("PV_done"), 6 * NPAIR)
            load_down(0, 0, 0, True)
            sp.wait_ge(S("unit_used"), 41)
            sp.wait_ge(S("mask_ready"), 2)
            load_gate_up(0, 0, 1, True)
            load_down(0, 0, 1, False)
            with sp.Fori(1, NBATCH // 2) as i:
                load(i, i, 0, False)
                load(i, i, 1, False)
            passes = sp.value_load(npass_i[0:1, 0:1], min_val=1, max_val=NPASS)
            with sp.If(passes > 1):
                with sp.Fori(1, passes) as b:
                    with sp.Fori(0, NBATCH // 2) as i:
                        load(b * (NBATCH // 2) + i, i, 0, False)
                        load(b * (NBATCH // 2) + i, i, 1, False)
            sp.wait_ge(S("gu_used"), passes * NBATCH)
            sp.dma_start(wpp_sb, wpp).then_inc(S("ld_wpp"), 16)
            sp.dma_start(pT_sb, pT).then_inc(S("ld_pT"), 16)
            sp.dma_start(wpg_sb, wpg).then_inc(S("ld_wpg"), 16)
            sp.dma_start(gple, gain3[1]).then_inc(S("ld_gple"), 16)
            sp.dma_start(gfin, gain3[2]).then_inc(S("ld_gfin"), 16)
            for t in range(NT):
                sp.wait_ge(S("out_ready"), t + 1)
                sp.dma_start(out[0, t * P:(t + 1) * P, :], x1[:, t]).then_inc(S(f"out_stored{t}"), 16)
            for t in range(NT):
                sp.wait_ge(S(f"out_stored{t}"), 16)

        @block.tensor
        def _(pe):
            mm = nc.tensor.matmul

            def tr(o, i):
                return nc.tensor.transpose(o, i, ident)

            pe.wait_ge(S("ld_cst"), 16)
            pe.wait_ge(S("sq_ready"), 1)
            for k in range(KD):
                m = mm(ps[:, 7, 0:T], C("ones"), sq[:, k], start=k == 0, stop=k == KD - 1)
            m.then_inc(S("ssq_done"), 1)
            pe.wait_ge(S("hT_ready"), 1)

            def landed(n, slot):
                pe.wait_ge(S(f"unit_landed{slot}"), 16 * (n // RING) + 16)

            def project(n, slot, free=True):
                landed(n, slot)
                if free:
                    pe.wait_ge(S("proj_read"), n - RING + 1)
                w = ring[slot].rearrange("p (k c) -> p k c", k=KD)
                for c in range(2):
                    for k in range(KD):
                        m = mm(ps[:, slot, c * T:(c + 1) * T], w[:, k, c * P:(c + 1) * P], hT[:, k],
                               start=k == 0, stop=k == KD - 1)
                m.then_inc(S("unit_used"), 1)

            for n in range(7):
                project(n, n % RING, free=n >= RING)

            pe.wait_ge(S("ld_lora"), 16)
            pe.wait_ge(S("ld_g2"), 16)
            pe.wait_ge(S("lora_in"), 2)
            pe.wait_ge(S("proj_read"), 7)
            for kind in range(3):
                for c in range(NPAIR):
                    w = g2_sb if kind == 2 else lora_sb[:, kind]
                    m = mm(ps[:, 2 * kind + c // 2, (c % 2) * T:(c % 2 + 1) * T], w[:, c * P:(c + 1) * P],
                           lin[:, 1] if kind == 2 else lin[:, 0], start=True, stop=True)
                m.then_inc(S("lora_out"), 1)
            pe.wait_ge(S("ld_crw"), 16)
            pe.wait_ge(S("kksq_ready"), 1)
            for src, bank in ((bT, 6), (rhoT, 0)):
                if bank == 0:
                    pe.wait_ge(S("lora_read"), 1)
                    pe.wait_ge(S("rk_ready"), 1)
                for c in range(2):
                    m = mm(ps[:, bank + c], C("block"), src[:, 2 * c:2 * c + 2].rearrange("p n t -> p (n t)"),
                           start=True, stop=True)
                m.then_inc(S("headsum"), 1)

            for i, (src, ready) in enumerate(((vT, "z_ready"), (bT, "b_ready"), (kaT, "ka_ready"), (alT, "al_ready"))):
                pe.wait_ge(S(ready), 7 if ready == "z_ready" else 1)
                for t in range(NT):
                    bank = 2 + 2 * (i % 2) + t
                    if i == 0:
                        pe.wait_ge(S("lora_read"), 3)
                    if i >= 2:
                        pe.wait_ge(S("tok_read"), 2 * i - 4 + t + 1)
                    for c in range(NPAIR):
                        m = tr(ps[:, bank, c * P:(c + 1) * P], src[:, c, t * P:(t + 1) * P])
                    m.then_inc(S("tok_out"), 1)

            pe.wait_ge(S("arz_ready"), 1)
            for t in range(NT):
                tt = slice(t * P, (t + 1) * P)
                for n in range(NPAIR):
                    for i, src in enumerate((bT, kaT)):
                        bank = 2 * (n % 2) + i
                        if t == 0 and n < 2:
                            pe.wait_ge(S("headsum_read"), 2)
                            pe.wait_ge(S("tok_read"), 8)
                        elif n < 2:
                            pe.wait_ge(S("ya_out"), t)
                        else:
                            pe.wait_ge(S("mats_read"), 8 * t + 2 * (n - 2) + i + 1)
                        m = mm(ps[:, bank].rearrange("p (a t) -> p a t", a=4), src[:, n, tt],
                               arz[:, n].rearrange("p a b t -> p (a b) t")[:, :, tt], start=True, stop=True)
                        m.then_inc(S("mats_out"), 1)
                for g in range(2):
                    pe.wait_ge(S("mats_read"), 8 * t + 4 * g + 4)
                    for h in range(4):
                        m = tr(ps[:, 4 + g, h * P:(h + 1) * P], mats[:, 2 * g + h // 2, 0, (h % 2) * P:(h % 2 + 1) * P])
                    m.then_inc(S("M_out"), 1)
                for l in range(1, LEVELS):
                    for g in range(2):
                        pe.wait_ge(S("mlev_ready"), (LEVELS - 1) * 2 * t + 2 * (l - 1) + g + 1)
                        pe.wait_ge(S("Z_ready"), LEVELS * 2 * t + 2 * (l - 1) + g + 1)
                        for h in range(4 * g, 4 * g + 4):
                            m = mm(ps[:, g, (h % 4) * P:(h % 4 + 1) * P], mlev[:, l % 2, h], Z_sb[:, h], start=True, stop=True)
                        m.then_inc(S("T1_out"), 1)
                    for g in range(2):
                        pe.wait_ge(S("T1_ready"), (LEVELS - 1) * 2 * t + 2 * (l - 1) + g + 1)
                        pe.wait_ge(S("X_ready"), (LEVELS - 1) * 2 * t + 2 * (l - 1) + g + 1)
                        for h in range(4 * g, 4 * g + 4):
                            m = mm(ps[:, 2 + g, (h % 4) * P:(h % 4 + 1) * P], X_sb[:, h], T1_sb[:, h], start=True, stop=True)
                        m.then_inc(S("D_out"), 1)
                        if l < LEVELS - 1:
                            for h in range(4 * g, 4 * g + 4):
                                m = mm(ps[:, 4 + g, (h % 4) * P:(h % 4 + 1) * P], T1_sb[:, h], X_sb[:, h], start=True, stop=True)
                            m.then_inc(S("DT_out"), 1)
                pe.wait_ge(S("Z_ready"), LEVELS * 2 * (t + 1))
                for h in range(NH):
                    m = mm(ps[:, 6, h * HD:(h + 1) * HD], mats[:, h // 2, 1, (h % 2) * P:(h % 2 + 1) * P],
                           Vtok[:, t, h * HD:(h + 1) * HD], start=True, stop=True)
                m.then_inc(S("NV_out"), 1)
                for h in range(NH):
                    m = mm(ps[(h % 2) * HD:(h % 2 + 1) * HD, 7, (h // 2) * P:(h // 2 + 1) * P],
                           Atok[:, t, h * HD:(h + 1) * HD], Z_sb[:, h], start=True, stop=True)
                m.then_inc(S("XAT_out"), 1)
                pe.wait_ge(S("NV_ready"), t + 1)
                for h in range(NH):
                    m = mm(ps[:, 0, h * HD:(h + 1) * HD], Z_sb[:, h], NV[:, h * HD:(h + 1) * HD], start=True, stop=True)
                m.then_inc(S("XNV_out"), 1)
                pe.wait_ge(S("XAT_ready"), t + 1)
                pe.wait_ge(S("XNV_ready"), t + 1)
                for c in range(2):
                    cc = 2 * t + c
                    rows = slice(c * CH, (c + 1) * CH)
                    pe.wait_ge(S("state_ready"), 1 + cc)
                    for n in range(NPAIR):
                        m = mm(ps[rows, 1, n * P:(n + 1) * P], XAT[:, n, rows], Th[:, cc, n], start=True, stop=True)
                    m.then_inc(S("U_out"), 1)
                    pe.wait_ge(S("U_ready"), cc + 1)
                    for n in range(NPAIR):
                        mm(ps[:, 2, n * P:(n + 1) * P], Ktok[rows, t, n * P:(n + 1) * P],
                           Vtok[rows, t, n * P:(n + 1) * P], start=True, stop=False)
                        m = mm(ps[:, 2, n * P:(n + 1) * P], Btok[rows, t, n * P:(n + 1) * P],
                               U_sb[rows, n * P:(n + 1) * P], start=False, stop=True)
                    m.then_inc(S("dT_out"), 1)
                pe.wait_ge(S("U_ready"), 2 * t + 2)
                for c in range(2):
                    rows = slice(c * CH, (c + 1) * CH)
                    for n in range(NPAIR):
                        mm(ps[rows, 3, n * P:(n + 1) * P], rhoT[:, n, t * P + c * CH:t * P + (c + 1) * CH],
                           Th[:, 2 * t + c, n], start=n == 0, stop=False, skip_group_check=True)
                for h in range(NH):
                    cols = slice(h * HD, (h + 1) * HD)
                    hh = slice(2 * P + (h % 2) * P, 2 * P + (h % 2 + 1) * P)
                    mm(ps[:, 3, cols], mats[:, h // 2, 0, hh], U_sb[:, cols], start=False, stop=False, skip_group_check=True)
                    m = mm(ps[:, 3, cols], mats[:, h // 2, 1, hh], Vtok[:, t, cols], start=False,
                           stop=h == NH - 1, skip_group_check=True)
                m.then_inc(S("Y_out"), 1)
                pe.wait_ge(S("yn_ready"), t + 1)
                for n in range(NPAIR):
                    m = tr(ps[:, 4, n * P:(n + 1) * P], yc[:, 2 * n:2 * n + 2].rearrange("p h d -> p (h d)"))
                m.then_inc(S("ynT_out"), 1)

            pe.wait_ge(S("ya_out"), NT)
            with pe.Fori(0, 4) as i:
                for j in range(RING):
                    project(7 + RING * i + j, (7 + j) % RING)
            with pe.Fori(0, 2) as i:
                for j in range(RING):
                    n, slot = 19 + RING * i + j, (19 + j) % RING
                    landed(n, slot)
                    pe.wait_ge(S("proj_read"), n - RING + 1)
                    w = ring[slot].rearrange("p (k c) -> p k c", k=KD)
                    for t in range(NT):
                        for k in range(KD):
                            m = mm(ps[:, slot, t * T:(t + 1) * T], hT[:, k, t * P:(t + 1) * P], w[:, k],
                                   start=k == 0, stop=k == KD - 1)
                    m.then_inc(S("unit_used"), 1)

            def scores(n):
                if n == 0:
                    pe.wait_ge(S("proj_read"), 25)
                else:
                    pe.wait_ge(S("scores_read"), 12 * n)
                for g in range(NG_ATT):
                    c = g * NPAIR + n
                    m = mm(ps[:, g].rearrange("p (h t) -> p h t", h=2), qT[:, c, P:T], kz[:, c], start=True, stop=True)
                    m = mm(ps[:, 3 + g // 2, (g % 2) * T:(g % 2 + 1) * T].rearrange("p (h t) -> p h t", h=2),
                           qT[:, c, 0:P], kz[:, c, :, 0:P], start=True, stop=True)
                m.then_inc(S("scores_out"), 1)

            scores(0)
            for n in range(NPAIR):
                if n + 1 < NPAIR:
                    scores(n + 1)
                for h in range(2):
                    hd = 2 * n + h
                    pe.wait_ge(S("probs_ready"), 2 * hd + 2)
                    for g in range(NG_ATT):
                        i = hd * NG_ATT + g
                        if i >= 2:
                            pe.wait_ge(S("PT_ready"), i - 1)
                        src = Ssb[:, n % 2, h]
                        tr(ps[:, 5 + i % 2, 0:P], src[:, g * P:(g + 1) * P])
                        tr(ps[:, 5 + i % 2, P:2 * P], src[:, 384 + g * T:384 + g * T + P])
                        m = tr(ps[:, 5 + i % 2, 2 * P:3 * P], src[:, 384 + g * T + P:384 + (g + 1) * T])
                        m.then_inc(S("PT_out"), 1)
                        if g == 0 and h == 0 and n >= 1:
                            pe.wait_ge(S("yb_read"), n)
                        pe.wait_ge(S("PT_ready"), i + 1)
                        rows = slice(h * HD, (h + 1) * HD)
                        vc = slice(g * RW + hd * HD, g * RW + (hd + 1) * HD)
                        mm(ps[rows, 7, 0:T], vtok[:, 0, vc], PT[:, i % 2, 0:T], start=g == 0, stop=False,
                           skip_group_check=True)
                        m = mm(ps[rows, 7, P:T], vtok[:, 1, vc], PT[:, i % 2, T:T + P], start=False, stop=g == 2,
                               skip_group_check=True)
                        m.then_inc(S("PV_done"), 1)

            pe.wait_ge(S("yb_read"), NPAIR)
            pe.sem_inc(S("gates_read"), 1)
            pe.sem_inc(S("merged"), 1)
            with pe.Fori(0, 4) as i:
                for j in range(2):
                    n, slot = 25 + RING * i + j, (25 + j) % RING
                    landed(n, slot)
                    if j == 0:
                        pe.wait_ge(S("gates_read"), i * 2 + 1)
                    w = ring[slot].rearrange("p (k c) -> p k c", k=KD)
                    for c in range(2):
                        for k in range(KD):
                            m = mm(ps[:, j, c * T:(c + 1) * T], w[:, k, c * P:(c + 1) * P], hT[:, k],
                                   start=k == 0, stop=k == KD - 1)
                    m.then_inc(S("unit_used"), 1)
                n, slot = 25 + RING * i + 2, 27 % RING
                landed(n, slot)
                pe.wait_ge(S("merged"), i + 1)
                w = ring[slot].rearrange("p (b k c) -> p b k c", b=2, k=NPAIR)
                for b, y in enumerate((yaT, ybT)):
                    for c in range(2):
                        for k in range(NPAIR):
                            m = mm(ps[:, 2 + b, c * T:(c + 1) * T], w[:, b, k, c * P:(c + 1) * P], y[:, k],
                                   start=k == 0, stop=k == NPAIR - 1)
                m.then_inc(S("unit_used"), 1)

            pe.wait_ge(S("merged"), 5)
            for u in range(4):
                n = 37 + u
                landed(n, n % RING)
                w = ring[n % RING].rearrange("p (k c) -> p k c", k=2)
                for k in range(2):
                    kk = 2 * u + k
                    for t in range(NT):
                        for hf in range(2):
                            m = mm(ps[:, 4 + 2 * t + hf], mT[:, kk, t * P:(t + 1) * P], w[:, k, hf * 512:(hf + 1) * 512],
                                   start=kk == 0, stop=kk == KD - 1)
                m.then_inc(S("unit_used"), 1)
            for t in range(NT):
                pe.wait_ge(S("h2_ready"), t + 1)
                for hf in range(2):
                    for k in range(4):
                        m = tr(ps[:, 2 * t + hf, k * P:(k + 1) * P], h2[:, t, (4 * hf + k) * P:(4 * hf + k + 1) * P])
                    m.then_inc(S("h2T_out"), 1)
            pe.wait_ge(S("ld_wr"), 16)
            for t in range(NT):
                pe.wait_ge(S("h2T_ready"), 2 * t + 2)
                for k in range(KD):
                    m = mm(ps[:, 4 + t, 0:36], h2T[:, k, t * P:(t + 1) * P], wr[:, k], start=k == 0, stop=k == KD - 1)
                m.then_inc(S("logits_out"), 1)
            pe.wait_ge(S("mask_ready"), 2)
            mm(ps[:, 6, 0:E], C("before"), rmask[:, 0], start=True, stop=True)
            mm(ps[:, 6, E:2 * E], C("ones"), rmask[:, 0], start=True, stop=False)
            mm(ps[:, 6, E:2 * E], C("before"), rmask[:, 1], start=False, stop=True)
            mm(ps[:, 6, 2 * E:3 * E], C("ones"), rmask[:, 0], start=True, stop=False)
            mm(ps[:, 6, 2 * E:3 * E], C("ones"), rmask[:, 1], start=False, stop=True).then_inc(S("pos_out"), 1)

            pe.wait_ge(S("passes_ready"), 1)
            passes = pe.value_load(npass_i[0:1, 0:1], min_val=1, max_val=NPASS)
            pe.wait_ge(S("zero_ready"), 1)
            for j in range(4):
                mm(ps[:, j], zero[:, 0:P], zero, start=True, stop=False, skip_group_check=True)
            for name in ("ysb0_ready", "ysb1_ready", "batch_done", "gu_used"):
                pe.sem_inc(S(name), 1)
            with pe.Fori(0, passes) as b:
                with pe.Fori(0, NBATCH // 2) as i:
                    for q in range(2):
                        trip = b * (NBATCH // 2) + i
                        done = 2 * trip + q
                        if q == 0:
                            pe.wait_ge(S("sel_ready"), 2 * b + 2)
                        pe.wait_ge(S("ysb0_ready"), done + 1)
                        pe.wait_ge(S("ysb1_ready"), done + 1)
                        for k in range(KD):
                            for t in range(NT):
                                m = mm(ps[:, 4 + k // 4, (k % 4) * P:(k % 4 + 1) * P], h2[:, t, k * P:(k + 1) * P],
                                       sel[:, t, bass.ds(i * (2 * P) + q * P, P)], start=t == 0, stop=t == NT - 1)
                            if k % 4 == 3:
                                m.then_inc(S("gath_out"), 1)
                        for e in range(BATCH):
                            pe.wait_ge(S(f"gu_landed{q}{e}"), 16 * trip + 16)
                        pe.wait_ge(S("gath0_ready"), done + 1)
                        pe.wait_ge(S("gath1_ready"), done + 1)
                        for k in range(KD):
                            for e in range(BATCH):
                                m = mm(ps[e * SLOTS:(e + 1) * SLOTS, 6], hg[:, k, e * SLOTS:(e + 1) * SLOTS],
                                       gu_w[q][e][:, k], start=k == 0, stop=k == KD - 1)
                        m.then_inc(S("gu_used"), 1)
                        pe.wait_ge(S("selw_ready"), done + 1)
                        for t in range(NT):
                            m = tr(ps[:, 7, t * P:(t + 1) * P], selw[:, t])
                        m.then_inc(S("selwT_out"), 1)
                        pe.wait_ge(S("act_ready"), done + 1)
                        for f in range(F // P):
                            m = tr(ps[:, 7, T + f * P:T + (f + 1) * P], act[:, f * P:(f + 1) * P])
                        m.then_inc(S("actT_out"), 1)
                        for e in range(BATCH):
                            pe.wait_ge(S(f"dn_landed{e}"), 32 * trip + 16 * q + 16)
                        pe.wait_ge(S("actT_ready"), done + 1)
                        for hf in range(2):
                            for f in range(F // P):
                                for e in range(BATCH):
                                    m = mm(ps[e * SLOTS:(e + 1) * SLOTS, 4 + hf], actT[:, f, e * SLOTS:(e + 1) * SLOTS],
                                           dn_w[e][:, f, hf * 512:(hf + 1) * 512], start=f == 0, stop=f == F // P - 1)
                            m.then_inc(S("dn_out"), 1)
                        pe.wait_ge(S("selwT_ready"), done + 1)
                        for hf in range(2):
                            pe.wait_ge(S(f"ysb{hf}_ready"), done + 2)
                            for t in range(NT):
                                m = mm(ps[:, 2 * t + hf], selwT[:, t], ysb[:, hf * 512:(hf + 1) * 512],
                                       start=False, stop=False, skip_group_check=True)
                        m.then_inc(S("batch_done"), 1)
            for j in range(4):
                m = mm(ps[:, j], zero[:, 0:P], zero, start=False, stop=True, skip_group_check=True)
            m.then_inc(S("moe_done"), 1)

            pe.wait_ge(S("ld_wpp"), 16)
            pe.wait_ge(S("ld_pT"), 16)
            for t in range(NT):
                for hf in range(2):
                    for k in range(2):
                        m = mm(ps[:, 4 + 2 * t + hf], pT_sb[:, k, t * P:(t + 1) * P], wpp_sb[:, k, hf * 512:(hf + 1) * 512],
                               start=k == 0, stop=k == 1)
            for t in range(NT):
                pe.wait_ge(S("h3_ready"), t + 1)
                pe.wait_ge(S("x2_ready"), 2)
                for hf in range(2):
                    for k in range(4):
                        m = tr(ps[:, 2 * t + hf, k * P:(k + 1) * P], h3[:, t, (4 * hf + k) * P:(4 * hf + k + 1) * P])
                    m.then_inc(S("h3T_out"), 1)
            pe.wait_ge(S("ld_wpg"), 16)
            pe.wait_ge(S("h3T_ready"), 4)
            for t in range(NT):
                for hf in range(2):
                    for k in range(KD):
                        m = mm(ps[:, 2 * t + hf], h3T[:, k, t * P:(t + 1) * P], wpg_sb[:, k, hf * 512:(hf + 1) * 512],
                               start=k == 0, stop=k == KD - 1)
                m.then_inc(S("gate_out"), 1)

        @block.scalar
        def _(a):
            do = Chain(a, "act")
            A = nc.scalar.activation
            eps = C("eps")

            def copy(o, i, scale=1.0):
                return A(o, i, ACT.Copy, scale=scale)

            a.wait_ge(S("ld_xT"), 16)
            A(sq, xT_sb, ACT.Square).then_inc(S("sq_ready"), 1)
            a.wait_ge(S("ld_cst"), 16)
            a.wait_ge(S("ld_cvec"), 16)
            a.wait_ge(S("ssq_done"), 1)
            A(rstd_bc, ps[:, 7, 0:T], ACT.Sqrt, scale=1.0 / D, bias=eps[:, 0:1]).then_inc(S("rms_ready"), 1)
            a.wait_ge(S("zeroed"), 1)
            for n in range(7):
                a.wait_ge(S("unit_used"), n + 1)
                if n:
                    a.wait_ge(S("z_ready"), n)
                copy(shift[:, :, 1:T + 1], ps[:, n % RING].rearrange("p (c t) -> p c t", c=2)).then_inc(S("proj_read"), 1)
                if n == 0:
                    a.wait_ge(S("z_ready"), 1)
                    A(lin[0:W_LORA, 0], lin[0:W_LORA, 0], ACT.Tanh).then_inc(S("lora_in"), 1)
                    A(lin[:, 1], lin[:, 1], ACT.Sigmoid).then_inc(S("lora_in"), 1)
            for kind, dst, name in ((0, swT, "w0"), (1, aT_, "a0")):
                a.wait_ge(S("lora_out"), kind + 1)
                for c in range(NPAIR):
                    ins = A(dst[:, c], ps[:, 2 * kind + c // 2, (c % 2) * T:(c % 2 + 1) * T], ACT.Sigmoid, bias=V(name, c))
                    if c == NPAIR - 1:
                        ins.then_inc(S("lora_read"), 1)
                    else:
                        do(ins)
            a.wait_ge(S("lora_out"), 3)
            copy(gT.rearrange("p n t -> p (n t)"), ps[:, 4:6].rearrange("p b t -> p (b t)")).then_inc(S("lora_read"), 1)
            a.wait_ge(S("cum_ready"), 1)
            A(wincT, cumT, ACT.Exp, scale=-DECAY).then_inc(S("winc_ready"), 1)
            A(winvT, cumT, ACT.Exp, scale=DECAY).then_inc(S("winv_ready"), 1)
            a.wait_ge(S("cumx_ready"), 1)
            A(wexT, wexT, ACT.Exp, scale=-DECAY).then_inc(S("wex_ready"), 1)
            a.wait_ge(S("headsum"), 1)
            A(alT.rearrange("p n t -> p (n t)"), ps[:, 6:8].rearrange("p b t -> p (b t)"), ACT.Sqrt, bias=eps[:, 2:3])\
                .then_inc(S("kknorm"), 1)
            for i, dst in enumerate((Vtok, Btok, Ktok, Atok)):
                for t in range(NT):
                    a.wait_ge(S("tok_out"), 2 * i + t + 1)
                    copy(dst[:, t], ps[:, 2 + 2 * (i % 2) + t]).then_inc(S("tok_read"), 1)
            for t in range(NT):
                for g in range(2):
                    if t:
                        a.wait_ge(S("mlev_ready"), 2 * (LEVELS - 1) * t)
                        a.wait_ge(S("X_ready"), 2 * (LEVELS - 1) * t)
                    a.wait_ge(S("M_out"), 2 * t + g + 1)
                    copy(M_sb[:, 4 * g:4 * g + 4].rearrange("p h t -> p (h t)"), ps[:, 4 + g]).then_inc(S("M_ready"), 1)
                for l in range(1, LEVELS):
                    for g in range(2):
                        i = 2 * (LEVELS - 1) * t + 2 * (l - 1) + g + 1
                        a.wait_ge(S("T1_out"), i)
                        copy(T1_sb[:, 4 * g:4 * g + 4].rearrange("p h t -> p (h t)"), ps[:, g]).then_inc(S("T1_ready"), 1)
                a.wait_ge(S("NV_out"), t + 1)
                copy(NV, ps[:, 6]).then_inc(S("NV_ready"), 1)
                a.wait_ge(S("XAT_out"), t + 1)
                copy(XAT.rearrange("p n t -> p (n t)"), ps[:, 7]).then_inc(S("XAT_ready"), 1)
                a.wait_ge(S("XNV_out"), t + 1)
                copy(XNV, ps[:, 0]).then_inc(S("XNV_ready"), 1)
                a.wait_ge(S("var_ready"), t + 1)
                A(stat_a[:, 0:8], stat_a[:, 0:8], ACT.Sqrt, scale=1.0 / HD, bias=eps[:, 1:2]).then_inc(S("sd_ready"), 1)

            with a.Fori(0, 2) as i:
                for j in range(RING):
                    a.wait_ge(S("unit_used"), 7 + RING * i + j + 1)
                    copy(qT[:, bass.ds(2 * RING * i + 2 * j, 2)], ps[:, (7 + j) % RING].rearrange("p (c t) -> p c t", c=2),
                         scale=HD ** -0.5).then_inc(S("proj_read"), 1)
            a.wait_ge(S("kz_zeroed"), 2)
            with a.Fori(0, 2) as i:
                for j in range(RING):
                    a.wait_ge(S("unit_used"), 13 + RING * i + j + 1)
                    for h in range(2):
                        rows = slice(h * HD, (h + 1) * HD)
                        ins = copy(kz[rows, bass.ds(2 * RING * i + 2 * j, 2), h],
                                   ps[rows, (13 + j) % RING].rearrange("p (c t) -> p c t", c=2))
                        ins.then_inc(S("proj_read") if h else S("kz_half"), 1)
            with a.Fori(0, 2) as i:
                for j in range(RING):
                    a.wait_ge(S("unit_used"), 19 + RING * i + j + 1)
                    copy(vtok[:, :, bass.ds((RING * i + j) * T, T)], ps[:, (19 + j) % RING].rearrange("p (c t) -> p c t", c=2)
                         ).then_inc(S("proj_read"), 1)

            def exps(n):
                for h in range(2):
                    for b in range(2):
                        i = 4 * n + 2 * h + b
                        v = Ssb[:, n % 2, h, 0:384] if b == 0 else Ssb[:, n % 2, h, 384:1152]
                        a.wait_ge(S("max_ready"), i + 1)
                        A(v, v, ACT.Exp, bias=st_max[:, i:i + 1], accum_out=stat_a[:, i:i + 1]).then_inc(S("exp_ready"), 1)

            exps(0)
            for n in range(NPAIR):
                if n + 1 < NPAIR:
                    exps(n + 1)
                for i in range(6 * n, 6 * n + 6):
                    a.wait_ge(S("PT_out"), i + 1)
                    if i >= 2:
                        a.wait_ge(S("PV_done"), i - 1)
                    copy(PT[:, i % 2], ps[:, 5 + i % 2, 0:384]).then_inc(S("PT_ready"), 1)
                a.wait_ge(S("PV_done"), 6 * n + 6)
                copy(ybT[:, n], ps[:, 7, 0:T]).then_inc(S("yb_read"), 1)
            with a.Fori(0, 4) as i:
                for j, dst in enumerate((sga, sgb)):
                    a.wait_ge(S("unit_used"), 25 + RING * i + j + 1)
                    if j == 0:
                        a.wait_ge(S("merged"), i + 1)
                    A(dst, ps[:, j], ACT.Sigmoid).then_inc(S("gates_read"), 1)

            def sd(src, i, junk):
                do(A(junk, src, ACT.Square, accum_out=stat_a[:, 16 + i:17 + i]))
                A(stat_a[:, i:i + 1], stat_a[:, 16 + i:17 + i], ACT.Sqrt, scale=1.0 / D, bias=eps[:, 0:1])\
                    .then_inc(S("rms_ready"), 1)

            junk = hg.rearrange("p k t -> p (k t)")
            for t in range(NT):
                a.wait_ge(S("x1_ready"), t + 1)
                sd(x1[:, t], t, junk)
            for i in range(4):
                a.wait_ge(S("h2T_out"), i + 1)
                t, hf = i // 2, i % 2
                copy(h2T[:, 4 * hf:4 * hf + 4, t * P:(t + 1) * P], ps[:, i].rearrange("p (k t) -> p k t", k=4))\
                    .then_inc(S("h2T_ready"), 1)
            for t in range(NT):
                a.wait_ge(S("route_max"), t + 1)
                A(rt[:, t, 0:EG], rt[:, t, 0:EG], ACT.Exp, bias=stat[:, 16 + t:17 + t], accum_out=stat_a[:, 4 + t:5 + t])\
                    .then_inc(S("route_exp"), 1)
                a.wait_ge(S("route_second"), t + 1)
                A(stat_a[:, 6 + t:7 + t], stat[:, 20 + t:21 + t], ACT.Exp).then_inc(S("route_exp"), 1)
            a.wait_ge(S("passes_ready"), 1)
            passes = a.value_load(npass_i[0:1, 0:1], min_val=1, max_val=NPASS)
            with a.Fori(0, passes) as b:
                with a.Fori(0, NBATCH // 2) as i:
                    for q in range(2):
                        done = 2 * (b * (NBATCH // 2) + i) + q
                        a.wait_ge(S("gath_out"), 2 * done + 1)
                        copy(hg[:, 0:4].rearrange("p k t -> p (k t)"), ps[:, 4]).then_inc(S("gath0_ready"), 1)
                        a.wait_ge(S("gu_used"), done + 2)
                        A(silu, ps[:, 6, 0:F], ACT.Silu).then_inc(S("silu_ready"), 1)
                        a.wait_ge(S("actT_out"), done + 1)
                        copy(actT.rearrange("p f t -> p (f t)"), ps[:, 7, T:2 * T]).then_inc(S("actT_ready"), 1)
                        a.wait_ge(S("batch_done"), done + 1)
                        a.wait_ge(S("dn_out"), 2 * done + 1)
                        copy(ysb[:, 0:512], ps[:, 4]).then_inc(S("ysb0_ready"), 1)

            for t in range(NT):
                a.wait_ge(S("x2_ready"), t + 1)
                sd(x1[:, t], 8 + t, junk)
            for i in range(4):
                a.wait_ge(S("h3T_out"), i + 1)
                t, hf = i // 2, i % 2
                copy(h3T[:, 4 * hf:4 * hf + 4, t * P:(t + 1) * P], ps[:, i].rearrange("p (k t) -> p k t", k=4))\
                    .then_inc(S("h3T_ready"), 1)
            for t in range(NT):
                a.wait_ge(S("gate_out"), t + 1)
                A(gate[:, t], ps[:, 2 * t:2 * t + 2].rearrange("p b n -> p (b n)"), ACT.Sigmoid).then_inc(S("gate_ready"), 1)
            for t in range(NT):
                a.wait_ge(S("x3_ready"), t + 1)
                sd(x1[:, t], 10 + t, junk)

        @block.gpsimd
        def _(g_):
            do = Chain(g_, "pool")
            Pg = nc.gpsimd
            do(Pg.memset(shift[:, :, 0:1], 0.0))
            Pg.memset(Th.rearrange("p a n t -> p (a n t)"), 0.0).then_inc(S("zeroed"), 1)
            g_.wait_ge(S("hT_ready"), 1)
            do(Pg.memset(arz.rearrange("p n a h t -> p (n a h t)"), 0.0))
            for kind, (src, ready) in enumerate(((alT, "al_ready"), (rhoT, "rho_ready"))):
                g_.wait_ge(S(ready), 1)
                for h in range(2):
                    rows = slice(h * HD, (h + 1) * HD)
                    do(Pg.tensor_copy(arz[rows, :, kind, h], src[rows]))
            g_.sem_inc(S("arz_ready"), 1)
            g_.wait_ge(S("ld_crw"), 16)
            g_.wait_ge(S("tok_out"), 8)
            for t in range(NT):
                for l in range(1, LEVELS):
                    for g in range(2):
                        n = 2 * (LEVELS - 1) * t + 2 * (l - 1) + g
                        if l == 1:
                            g_.wait_ge(S("M_ready"), 2 * t + g + 1)
                        if n >= 4:
                            g_.wait_ge(S("T1_out"), n - 3)
                        Pg.tensor_tensor(mlev[:, l % 2, 4 * g:4 * g + 4], M_sb[:, 4 * g:4 * g + 4],
                                         C("level")[:, l * P:(l + 1) * P].unsqueeze(1).broadcast_to([P, 4, P]), ALU.mult)\
                            .then_inc(S("mlev_ready"), 1)
            g_.wait_ge(S("merged"), 5)
            Pg.memset(zero, 0.0).then_inc(S("zero_ready"), 1)

        @block.vector
        def _(v):
            do = Chain(v, "dve")
            N = nc.vector
            tt, ts, stt = N.tensor_tensor, N.tensor_scalar, N.scalar_tensor_tensor

            def bc(x, n):
                return x.unsqueeze(2).broadcast_to([x.shape[0], x.shape[1], n])

            def bc1(x, n):
                return x.unsqueeze(1).broadcast_to([x.shape[0], n, x.shape[1]])

            v.wait_ge(S("rms_ready"), 1)
            do(N.reciprocal(rstd_bc, rstd_bc))
            for k in range(KD):
                ins = stt(hT[:, k], xT_sb[:, k], V("norm_mix", k), rstd_bc, ALU.mult, ALU.mult)
                do(ins, "hT_ready" if k == KD - 1 else None)
            zdst = [lin, kT[:, 0:2], kT[:, 2:4], rT[:, 0:2], rT[:, 2:4], vT[:, 0:2], vT[:, 2:4]]
            for n in range(7):
                v.wait_ge(S("proj_read"), n + 1)
                do(tt(dlt, shift[:, :, 0:T], shift[:, :, 1:T + 1], ALU.subtract))
                do(stt(zdst[n][:, 0], dlt[:, 0], V("mu", 2 * n), shift[:, 0, 1:T + 1], ALU.mult, ALU.add))
                do(stt(zdst[n][:, 1], dlt[:, 1], V("mu", 2 * n + 1), shift[:, 1, 1:T + 1], ALU.mult, ALU.add), "z_ready")
            v.wait_ge(S("ld_crw"), 16)
            v.wait_ge(S("lora_read"), 1)
            flat = lambda x: x.rearrange("p n t -> p (n t)")
            do(N.tensor_tensor_scan(flat(cumT), C("reset"), flat(swT), 0.0, ALU.mult, ALU.add), "cum_ready")
            do(tt(wexT, cumT, swT, ALU.subtract), "cumx_ready")
            for c in range(NPAIR):
                do(ts(kkT[:, c], kT[:, c], V("k_k", c), None, ALU.mult))
            do(tt(bT, kkT, kkT, ALU.mult), "kksq_ready")
            v.wait_ge(S("lora_read"), 2)
            for c in range(NPAIR):
                do(ts(kaT[:, c], aT_[:, c], 1.0, V("k_a", c), ALU.subtract, ALU.mult))
            do(stt(kaT, kaT, 1.0, kT, ALU.add, ALU.mult))
            for c in range(NPAIR):
                do(stt(rhoT[:, c], rT[:, c], V("r_k", c), kaT[:, c], ALU.mult, ALU.mult),
                   "rk_ready" if c == NPAIR - 1 else None)
            v.wait_ge(S("kknorm"), 1)
            do(N.reciprocal(alT, alT), "headsum_read")
            do(tt(kkT, kkT, alT, ALU.mult))
            v.wait_ge(S("winv_ready"), 1)
            do(tt(bT, kkT, aT_, ALU.mult))
            do(tt(bT, bT, winvT, ALU.mult), "b_ready")
            do(tt(kaT, kaT, winvT, ALU.mult), "ka_ready")
            v.wait_ge(S("wex_ready"), 1)
            do(stt(alT, wexT, -1.0, kkT, ALU.mult, ALU.mult), "al_ready")
            v.wait_ge(S("headsum"), 2)
            do(tt(bonus, ps[:, 0:2].rearrange("p b (c t) -> p (b c) t", c=2), vT, ALU.mult), "headsum_read")
            v.wait_ge(S("winc_ready"), 1)
            do(tt(rhoT, rT, wincT, ALU.mult), "rho_ready")
            for t in range(NT):
                for n in range(NPAIR):
                    for i in range(2):
                        v.wait_ge(S("mats_out"), 8 * t + 2 * n + i + 1)
                        if t == 0 and n == 0 and i == 0:
                            v.wait_ge(S("tok_out"), 8)
                            v.wait_ge(S("arz_ready"), 1)
                        do(tt(mats[:, n, i], ps[:, 2 * (n % 2) + i], C("causal"), ALU.mult), "mats_read")
                for g in range(2):
                    hh = slice(4 * g, 4 * g + 4)
                    mt = mats[:, 2 * g:2 * g + 2, 0, 0:2 * P].rearrange("p n (h t) -> p n h t", h=2)
                    v.wait_ge(S("M_ready"), 2 * t + g + 1)
                    z4 = Z_sb[:, hh].rearrange("p (n h) t -> p n h t", n=2)
                    for n in range(2):
                        do(tt(z4[:, n], mt[:, n], bc1(C("level0T"), 2), ALU.mult))
                    do(tt(X_sb[:, hh], M_sb[:, hh], bc1(C("level")[:, 0:P], 4), ALU.mult))
                    do(tt(Z_sb[:, hh], Z_sb[:, hh], bc1(ident, 4), ALU.add), "Z_ready")
                    do(tt(X_sb[:, hh], X_sb[:, hh], bc1(ident, 4), ALU.add), "X_ready")
                for l in range(1, LEVELS):
                    for g in range(2):
                        hh = slice(4 * g, 4 * g + 4)
                        i = 2 * (LEVELS - 1) * t + 2 * (l - 1) + g + 1
                        v.wait_ge(S("D_out"), i)
                        do(tt(Z_sb[:, hh], Z_sb[:, hh], ps[:, 2 + g].rearrange("p (h t) -> p h t", h=4), ALU.add), "Z_ready")
                        if l < LEVELS - 1:
                            v.wait_ge(S("DT_out"), 2 * (LEVELS - 2) * t + 2 * (l - 1) + g + 1)
                            do(tt(X_sb[:, hh], X_sb[:, hh], ps[:, 4 + g].rearrange("p (h t) -> p h t", h=4), ALU.add),
                               "X_ready")
                v.wait_ge(S("XNV_ready"), t + 1)
                if t == 0:
                    v.wait_ge(S("zeroed"), 1)
                    v.sem_inc(S("state_ready"), 1)
                    do.n["state_ready"] = 1
                for c in range(2):
                    cc = 2 * t + c
                    rows = slice(c * CH, (c + 1) * CH)
                    v.wait_ge(S("U_out"), cc + 1)
                    do(tt(U_sb[rows], ps[rows, 1], XNV[rows], ALU.add), "U_ready")
                    v.wait_ge(S("dT_out"), cc + 1)
                    for h in range(2):
                        hr = slice(h * HD, (h + 1) * HD)
                        do(tt(Th[hr, cc + 1, :, hr], ps[hr, 2].rearrange("p (n t) -> p n t", n=NPAIR)[:, :, hr],
                              Th[hr, cc, :, hr], ALU.add))
                    for h in range(2):
                        hr = slice(h * HD, (h + 1) * HD)
                        last = (cc + 1) * CH - 1
                        do(tt(Th[hr, cc + 1, :, hr], Th[hr, cc + 1, :, hr], bc(wincT[hr, :, last], HD), ALU.mult),
                           "state_ready" if h else None)
                v.wait_ge(S("Y_out"), t + 1)
                y8 = ps[:, 3].rearrange("p (h d) -> p h d", h=NH)
                do(N.tensor_reduce(stat[:, 0:8], y8, AX, ALU.add))
                do(ts(stat[:, 0:8], stat[:, 0:8], -1.0 / HD, None, ALU.mult))
                do(tt(yc, y8, bc(stat[:, 0:8], HD), ALU.add))
                do(tt(ysq, yc, yc, ALU.mult))
                do(N.tensor_reduce(stat_a[:, 0:8], ysq, AX, ALU.add), "var_ready")
                v.wait_ge(S("sd_ready"), t + 1)
                do(N.reciprocal(stat[:, 8:16], stat_a[:, 0:8]))
                do(tt(yc, yc, bc(stat[:, 8:16], HD), ALU.mult), "yn_ready")
                v.wait_ge(S("ynT_out"), t + 1)
                cols = slice(t * P, (t + 1) * P)
                for n in range(NPAIR):
                    do(ts(tmpT[:, n], ps[:, 4, n * P:(n + 1) * P], V("ln_w", n), V("ln_b", n), ALU.mult, ALU.add))
                do(tt(tmpT, tmpT, bonus[:, :, cols], ALU.add))
                do(tt(yaT[:, :, cols], tmpT, gT[:, :, cols], ALU.mult), "ya_out")

            do(N.memset(kz[0:HD, :, 1], 0.0), "kz_zeroed")
            do(N.memset(kz[HD:P, :, 0], 0.0), "kz_zeroed")
            v.wait_ge(S("ld_neg"), 16)

            def score(n):
                v.wait_ge(S("scores_out"), n + 1)
                if n >= 2:
                    v.wait_ge(S("PT_out"), 6 * (n - 1))
                for h in range(2):
                    for b in range(2):
                        i = 4 * n + 2 * h + b
                        base, w = (0, P) if b == 0 else (384, T)
                        for g in range(NG_ATT):
                            if b:
                                src = ps[:, g, h * T:(h + 1) * T]
                                bias = neg_sb[:, g, P:384]
                            else:
                                at = (g % 2) * T + h * P
                                src = ps[:, 3 + g // 2, at:at + P]
                                bias = neg_sb[:, g, 0:P]
                            do(stt(Ssb[:, n % 2, h, base + g * w:base + (g + 1) * w], bias, SLOPES[g * 8 + 2 * n + h], src,
                                   ALU.mult, ALU.add), "scores_read")
                        do(N.tensor_reduce(st_max[:, i:i + 1], Ssb[:, n % 2, h, base:base + 3 * w], AX, ALU.max, negate=True),
                           "max_ready")

            def normalise(n):
                for h in range(2):
                    for b in range(2):
                        i = 4 * n + 2 * h + b
                        sl = Ssb[:, n % 2, h, 0:384] if b == 0 else Ssb[:, n % 2, h, 384:1152]
                        v.wait_ge(S("exp_ready"), i + 1)
                        do(N.reciprocal(stat[:, 16 + i:17 + i], stat_a[:, i:i + 1]))
                        do(ts(sl, sl, stat[:, 16 + i:17 + i], None, ALU.mult), "probs_ready")

            score(0)
            normalise(0)
            for n in range(1, NPAIR):
                score(n)
                normalise(n)
            link = None
            with v.Fori(0, 4) as i:
                link = LoopChain(v, "dve_merge", i, 2)
                v.wait_ge(S("gates_read"), 2 * i + 3)
                v.wait_ge(S("unit_used"), 28 + RING * i)
                link(tt(ma, sga, ps[:, 2], ALU.mult))
                link(tt(mb, sgb, ps[:, 3], ALU.mult))
                tt(mT[:, bass.ds(2 * i, 2)], ma.rearrange("p (c t) -> p c t", c=2), mb.rearrange("p (c t) -> p c t", c=2),
                   ALU.add).then_inc(S("merged"), 1)
                v.wait_ge(S("merged"), i + 2)
                link.close()
            two = lambda b: ps[:, b:b + 2].rearrange("p b n -> p (b n)")
            v.wait_ge(S("unit_used"), 41)
            v.wait_ge(S("ld_x"), 16)
            for t in range(NT):
                do(tt(x1[:, t], two(4 + 2 * t), xt_sb[:, t], ALU.add), "x1_ready")
            v.wait_ge(S("ld_gmoe"), 16)
            for t in range(NT):
                v.wait_ge(S("rms_ready"), 2 + t)
                do(N.reciprocal(stat[:, t:t + 1], stat_a[:, t:t + 1]))
                do(stt(h2[:, t], x1[:, t], stat[:, t:t + 1], gmoe, ALU.mult, ALU.mult), "h2_ready")

            def first_max(dst, logits, keys, top, scratch):
                do(ts(scratch, logits, top, None, ALU.is_equal))
                do(tt(scratch, scratch, keys, ALU.mult))
                do(N.tensor_reduce(stat[:, 24:25], scratch, AX, ALU.max))
                do(ts(dst, scratch, stat[:, 24:25], None, ALU.is_equal))

            for t in range(NT):
                L = rt[:, t]
                m1, m2, nd, gw, w1, w2 = [stat[:, c + t:c + t + 1] for c in (26, 28, 20, 30, 32, 34)]
                gm = stat[:, 40:40 + EG]
                pen = stat[:, 44:44 + EG]
                other = comb[:, t]
                e32 = posm[:, t]
                v.wait_ge(S("logits_out"), t + 1)
                do(N.tensor_copy(L, ps[:, 4 + t, 0:36]))
                do(N.tensor_reduce(stat[:, 22:23], L[:, 0:EG], AX, ALU.max))
                do(ts(stat[:, 48:52], L[:, 0:EG], stat[:, 22:23], None, ALU.is_equal))
                do(tt(stat[:, 48:52], stat[:, 48:52], C("key_g"), ALU.mult))
                do(N.tensor_reduce(stat[:, 24:25], stat[:, 48:52], AX, ALU.max))
                do(ts(gm, stat[:, 48:52], stat[:, 24:25], None, ALU.is_equal))
                do(ts(pen, gm, 1.0, -FAR, ALU.subtract, ALU.mult))
                do(tt(L[:, EG:36].rearrange("p (g e) -> p g e", g=EG), L[:, EG:36].rearrange("p (g e) -> p g e", g=EG),
                      bc(pen, E // EG), ALU.add))
                do(ts(stat[:, 16 + t:17 + t], stat[:, 22:23], -1.0, None, ALU.mult), "route_max")
                ex = L[:, EG:36]
                do(N.tensor_reduce(m1, ex, AX, ALU.max))
                first_max(rmask[:, t], ex, C("key_e"), m1, e32)
                do(stt(ex, rmask[:, t], 3.0 * FAR, ex, ALU.mult, ALU.add))
                do(N.tensor_reduce(m2, ex, AX, ALU.max))
                first_max(other, ex, C("key_e"), m2, e32)
                do(tt(nd, m2, m1, ALU.subtract), "route_second")
                v.wait_ge(S("route_exp"), 2 * t + 2)
                do(N.reciprocal(gw, stat_a[:, 4 + t:5 + t]))
                do(ts(w1, stat_a[:, 6 + t:7 + t], 1.0, None, ALU.add))
                do(N.reciprocal(w1, w1))
                do(tt(w2, stat_a[:, 6 + t:7 + t], w1, ALU.mult))
                do(tt(w1, w1, gw, ALU.mult))
                do(tt(w2, w2, gw, ALU.mult))
                do(ts(e32, other, w2, None, ALU.mult))
                do(tt(ex, rmask[:, t], other, ALU.add))
                do(stt(other, rmask[:, t], w1, e32, ALU.mult, ALU.add))
                do(N.tensor_copy(rmask[:, t], ex), "mask_ready")
            v.wait_ge(S("pos_out"), 1)
            for t in range(NT):
                do(ts(posm[:, t], rmask[:, t], -4096.0, 4096.0, ALU.mult, ALU.add))
                do(tt(posm[:, t], posm[:, t], ps[:, 6, t * E:(t + 1) * E], ALU.add))
            do(N.tensor_reduce(stat[:, 0:1], ps[:, 6, 2 * E:3 * E], AX, ALU.max))
            do(ts(stat[:, 48:48 + NPASS], C("full"), stat[:, 0:1], None, ALU.is_lt))
            do(N.tensor_reduce(stat[:, 1:2], stat[:, 48:48 + NPASS], AX, ALU.add))
            do(N.tensor_copy(npass_i[0:1, 0:1], stat[0:1, 1:2]), "passes_ready")
            passes = v.value_load(npass_i[0:1, 0:1], min_val=1, max_val=NPASS)
            e4 = lambda x: x.rearrange("p (e s) -> p e s", s=SLOTS)
            with v.Fori(0, passes) as b:
                v.wait_ge(S("batch_done"), NBATCH * b + 1)
                for t in range(NT):
                    tt(e4(sel[:, t]), C("slot")[:, bass.ds(SLOTS * b, SLOTS)].unsqueeze(1).broadcast_to([P, E, SLOTS]),
                       bc(posm[:, t], SLOTS), ALU.is_equal).then_inc(S("sel_ready"), 1)
                with v.Fori(0, NBATCH // 2) as i:
                    for q in range(2):
                        done = 2 * (b * (NBATCH // 2) + i) + q
                        if q == 0:
                            v.wait_ge(S("sel_ready"), 2 * b + 2)
                        for t in range(NT):
                            ins = tt(e4(selw[:, t]), e4(sel[:, t, bass.ds(i * 2 * P + q * P, P)]),
                                     bc(comb[:, t, bass.ds(i * 2 * BATCH + q * BATCH, BATCH)], SLOTS), ALU.mult)
                            ins.then_inc(S("selw_ready"), 1)
                        v.wait_ge(S("gath_out"), 2 * done + 2)
                        N.tensor_copy(hg[:, 4:8].rearrange("p k t -> p (k t)"), ps[:, 5]).then_inc(S("gath1_ready"), 1)
                        v.wait_ge(S("batch_done"), done + 1)
                        v.wait_ge(S("selwT_out"), done + 1)
                        N.tensor_copy(selwT.rearrange("p a t -> p (a t)"), ps[:, 7, 0:T]).then_inc(S("selwT_ready"), 1)
                        v.wait_ge(S("silu_ready"), done + 1)
                        tt(act, silu, ps[:, 6, F:2 * F], ALU.mult).then_inc(S("act_ready"), 1)
                        v.wait_ge(S("dn_out"), 2 * done + 2)
                        N.tensor_copy(ysb[:, 512:1024], ps[:, 5]).then_inc(S("ysb1_ready"), 1)
            v.wait_ge(S("moe_done"), 1)
            for t in range(NT):
                do(tt(x1[:, t], x1[:, t], two(2 * t), ALU.add), "x2_ready")
            v.wait_ge(S("ld_gple"), 16)
            for t in range(NT):
                v.wait_ge(S("rms_ready"), 4 + t)
                do(N.reciprocal(stat[:, 8 + t:9 + t], stat_a[:, 8 + t:9 + t]))
                do(stt(h3[:, t], x1[:, t], stat[:, 8 + t:9 + t], gple, ALU.mult, ALU.mult), "h3_ready")
            for t in range(NT):
                v.wait_ge(S("gate_ready"), t + 1)
                do(tt(gate[:, t], gate[:, t], two(4 + 2 * t), ALU.mult))
                do(tt(x1[:, t], x1[:, t], gate[:, t], ALU.add), "x3_ready")
            v.wait_ge(S("ld_gfin"), 16)
            for t in range(NT):
                v.wait_ge(S("rms_ready"), 6 + t)
                do(N.reciprocal(stat[:, 10 + t:11 + t], stat_a[:, 10 + t:11 + t]))
                do(stt(x1[:, t], x1[:, t], stat[:, 10 + t:11 + t], gfin, ALU.mult, ALU.mult), "out_ready")


def _constants(np):
    f = np.float32
    i = np.arange(P)
    c = np.zeros((P, N_CRW), f)

    def put(name, a):
        at, n = CST[name]
        c[:, at:at + n] = a

    s, t = i[:, None], i[None, :]
    same = (s // CH) == (t // CH)
    put("ident", np.eye(P))
    put("ones", 1.0)
    put("before", s < t)
    put("slot", np.arange(T))
    put("key_g", np.arange(EG, 0, -1))
    put("key_e", np.arange(E, 0, -1))
    put("full", np.arange(NPASS) * SLOTS)
    put("eps", np.array([EPS, GN_EPS, 1e-12, 0.0]))
    put("block", (s // HD) == (t // HD))
    put("causal", np.concatenate([(s < t) & same] * 2 + [(s <= t) & same] * 2, 1))
    lev = [((s // (2 * b)) == (t // (2 * b))) & ((s // b) % 2 == 1) & ((t // b) % 2 == 0) for b in (2 ** l for l in range(LEVELS))]
    put("level", np.concatenate(lev, 1))
    put("level0T", lev[0].T)
    put("reset", np.tile((np.arange(T) % CH != 0), NPAIR))
    neg = np.zeros((P, NG_ATT, 384), f)
    for g, (window, d) in enumerate(((128, 1), (512, 4), (2048, 16))):
        for b in range(2):
            keys = np.arange(P * (b + 1))
            dist = (b * P + i)[:, None] - keys[None, :]
            ok = (dist >= 0) & (dist % d == 0) & (dist <= window)
            neg[:, g, (0 if b == 0 else P):(P if b == 0 else 384)] = np.where(ok, -dist, FAR)
    return c[:, :N_CST].copy(), c[:, N_CST:].copy(), neg


def kernel(**inp):
    import numpy as np
    import concourse.bacc as bacc
    from concourse.bass_utils import run_bass_kernel_spmd as run

    w = {k: np.asarray(v) for k, v in inp.items()}
    con = np.ascontiguousarray

    def kp(a):
        return con(a.reshape(-1, P, a.shape[-1]).transpose(1, 0, 2))

    def col(a):
        return a.reshape(-1, P).T

    x = w["x"][0]
    win = w["w_in"][0]
    RC = 3 * RW + 256
    AC = 3 * NG_ATT * RW
    units = []

    def cols(at, n):
        for c in range(0, n, T):
            units.append(kp(win[:, at + c:at + c + T]).reshape(P, UNIT))

    cols(3 * RW, 256)
    cols(RW, RW)
    cols(0, RW)
    cols(2 * RW, RW)
    cols(RC, AC)
    pa, pb = w["w_proj_a"][0], w["w_proj_b"][0]
    for m in range(4):
        cols(RC + AC + m * T, T)
        cols(RC + AC + D + m * T, T)
        units.append(np.concatenate([kp(pa[:, m * T:(m + 1) * T]).reshape(P, -1), kp(pb[:, m * T:(m + 1) * T]).reshape(P, -1)], 1))
    wo = kp(w["w_out"][0])
    for u in range(4):
        units.append(wo[:, 2 * u:2 * u + 2].reshape(P, UNIT))
    mu = w["rwkv_mu"][0]
    mu = np.concatenate([mu[3 * RW:], mu[RW:2 * RW], mu[:RW], mu[2 * RW:3 * RW]])
    cvec = np.concatenate([col(w["norm_mix"][0]), col(mu)] + [col(w[n][0].reshape(-1)) for n in (
        "rwkv_w0", "rwkv_a0", "rwkv_k_k", "rwkv_k_a", "rwkv_r_k", "rwkv_ln_w", "rwkv_ln_b")], 1)
    lora = np.zeros((P, 2, RW), np.float32)
    lora[:64, 0] = w["rwkv_w2"][0]
    lora[64:, 1] = w["rwkv_a2"][0]
    gains = np.stack([np.broadcast_to(g, (P, D)) for g in (w["norm_moe"][0], w["norm_ple"][0], w["norm_final"])])
    wr = np.concatenate([w["w_router_group"][0], w["w_router_expert"][0].transpose(1, 0, 2).reshape(D, E)], 1)
    gu = np.concatenate([w["w_exp_gate"][0], w["w_exp_up"][0]], -1).reshape(E, KD, P, 2 * F).transpose(0, 2, 1, 3)
    dn = w["w_exp_down"][0].reshape(E, F // P, P, D).transpose(0, 2, 1, 3)
    cst, crw, neg = _constants(np)
    arrays = {
        "xT": kp(x.T), "xtok": kp(x), "pT": kp(w["p"][0, 0].T), "cst": cst, "crw": crw, "neg": neg, "cvec": cvec,
        "lora": lora, "g2": w["rwkv_g2"][0], "stream": np.stack(units), "gain3": gains, "router": kp(wr),
        "wgu": gu, "wd": dn, "wpg": kp(w["w_ple_gate"][0]), "wpp": kp(w["w_ple_proj"][0]),
    }
    nc = bacc.Bacc("TRN2", target_bir_lowering=False, num_devices=1)
    args = []
    for name, a in arrays.items():
        arrays[name] = con(a)
        args.append(nc.dram_tensor(name, a.shape, F32, kind="ExternalInput").ap())
    o = nc.dram_tensor("out", (1, T, D), F32, kind="ExternalOutput").ap()
    program(nc, *args, o)
    r = run(nc, [arrays], core_ids=[0])
    return r.results[0]["out"]
```

```python
import concourse.bass as bass
from concourse import mybir
from contextlib import ExitStack

F32 = mybir.dt.float32
I32 = mybir.dt.int32
ACT = mybir.ActivationFunctionType
ALU = mybir.AluOpType
AX = mybir.AxisListType.X

P = 128
D = 1024
T = 256
KD = D // P
NT = T // P
RW = 512
NPAIR = RW // P
HD = 64
W_LORA = 64
NH = 8
CH = 64
NG_ATT = 3
E = 32
EG = 4
F = 256
SLOTS = 32
BATCH = P // SLOTS
NBATCH = E // BATCH
NPASS = T // SLOTS
UNIT = 2048
RING = 3
LEVELS = 6
DECAY = 0.6065306597126334
EPS = 1e-6
GN_EPS = 64e-5
FAR = -1.0e30

CST = {}
CVEC = {}


def _columns(table, spec, at=0):
    for name, n in spec:
        table[name] = (at, n)
        at += n
    return at


N_CST = _columns(CST, [("ident", P), ("ones", P), ("before", P), ("slot", T), ("key_g", EG), ("key_e", E),
                       ("full", NPASS), ("eps", 4)])
N_CRW = _columns(CST, [("block", P), ("causal", 4 * P), ("level", LEVELS * P), ("level0T", P), ("reset", NPAIR * T)], N_CST)
N_CVEC = _columns(CVEC, [("norm_mix", KD), ("mu", 14), ("w0", NPAIR), ("a0", NPAIR), ("k_k", NPAIR), ("k_a", NPAIR),
                         ("r_k", NPAIR), ("ln_w", NPAIR), ("ln_b", NPAIR)])
SLOPES = [2.0 ** (-8.0 * (i + 1) / 24) for i in range(24)]


def program(nc, xT, xtok, pT, cst, crw, neg, cvec, lora, g2, stream, gain3, router, wgu, wd, wpg, wpp, out):
    ctx = ExitStack()
    with ctx:
        def sem(name):
            return ctx.enter_context(nc.semaphore(name))

        COLS = 53000
        mem = ctx.enter_context(nc.sbuf_tensor("mem", [P, COLS], F32))
        npass_i = ctx.enter_context(nc.sbuf_tensor("npass_i", [1, 1], I32))
        ps = ctx.enter_context(nc.psum_tensor("ps", [P, 8, 512], F32))

        def region(lo, hi):
            at = [lo]

            def take(*dims):
                n = 1
                for d in dims:
                    n *= d
                v = mem[:, at[0]:at[0] + n]
                at[0] += n
                assert at[0] <= hi, (at[0], hi)
                names = "abcd"[:len(dims)]
                if len(dims) > 1:
                    v = v.rearrange(f"p ({' '.join(names)}) -> p {' '.join(names)}",
                                    **{m: d for m, d in zip(names[1:], dims[1:])})
                return v
            return take

        GU0, GU1, DN, HIGH = 0, 16384, 32768, 40960
        take = region(GU0, DN)
        gu_w = [[take(KD, 2 * F) for _ in range(BATCH)] for _ in range(2)]
        take = region(DN, HIGH)
        dn_w = [take(F // P, D) for _ in range(BATCH)]
        ring_at = DN - RING * UNIT
        ring = [mem[:, ring_at + i * UNIT:ring_at + (i + 1) * UNIT] for i in range(RING)]

        take = region(HIGH, COLS)
        c_all = take(N_CST)
        cv = take(N_CVEC)
        small = take(320)
        high_pre = HIGH + N_CST + N_CVEC + 320
        x1 = take(NT, D)
        h2 = take(NT, D)
        sel = take(NT, E * SLOTS)
        hg = take(KD, P)
        selw = take(NT, P)
        silu = take(F)
        act = take(F)
        actT = take(F // P, P)
        ysb = take(D)
        selwT = take(NT, P)
        zero = take(512)
        take = region(HIGH + N_CST + N_CVEC, high_pre)
        rmask = take(NT, E)
        comb = take(NT, E)
        posm = take(NT, E)
        stat = take(64)
        stat_a = take(32)
        st_max = stat[:, 0:16]

        take = region(high_pre, COLS)
        hT = take(KD, T)
        yaT = take(NPAIR, T)
        ybT = take(NPAIR, T)
        crw_sb = take(N_CRW - N_CST)
        lora_sb = take(2, RW)
        g2_sb = take(RW)
        lin = take(2, T)
        mats_more = [take(2, 512) for _ in range(2)]
        take = region(GU0, GU1)
        prep = take(8, NPAIR, T)
        rT, kT, aT_, kkT, swT, cumT, wexT, winvT = [prep[:, i] for i in range(8)]
        mats0 = prep[:, 0:4].rearrange("p s n t -> p (s n t)").rearrange("p (n b c) -> p n b c", n=NPAIR, b=2)
        M_sb, X_sb, Z_sb, T1_sb = [prep[:, 4 + i].rearrange("p n t -> p (n t)").rearrange("p (h t) -> p h t", h=NH)
                                   for i in range(4)]
        vT = take(NPAIR, T)
        gT = take(NPAIR, T)
        bonus = take(NPAIR, T)
        wincT = take(NPAIR, T)
        bT = take(NPAIR, T)
        kaT = take(NPAIR, T)
        rhoT = take(NPAIR, T)
        mats_more.append(take(2, 512))
        mats_more.append(vT.rearrange("p n t -> p (n t)").rearrange("p (b c) -> p b c", b=2))
        take = region(GU1, ring_at)
        arz = take(NPAIR, 2, 2, T)
        mlev = take(2, NH, P)
        alT = mlev[:, 0].rearrange("p h t -> p (h t)").rearrange("p (n t) -> p n t", n=NPAIR)
        tok = take(4, NT, RW)
        Atok, Btok, Ktok, Vtok = [tok[:, i] for i in range(4)]
        take = region(DN, HIGH)
        NV = take(RW)
        XNV2 = [take(RW) for _ in range(NT)]
        XAT2 = [take(NPAIR, P) for _ in range(NT)]
        U_sb = take(RW)
        Th = take(5, NPAIR, P)
        yc = take(NH, HD)
        ysq = take(NH, HD)
        shift = take(2, T + 1)
        tmpT = take(NPAIR, P)
        dlt = ysq.rearrange("p h d -> p (h d)").rearrange("p (c t) -> p c t", c=2)

        def mats(t, n, i):
            return mats0[:, n, i] if t == 0 else mats_more[n][:, i]

        take = region(GU0, ring_at)
        xT_sb = take(KD, T)
        sq = take(KD, T)
        rstd_bc = take(T)
        take = region(GU1, ring_at)
        qT = take(NG_ATT * NPAIR, T)
        kz = take(NG_ATT * NPAIR, 2, T)
        take = region(DN, HIGH)
        vtok = take(NT, NG_ATT * RW)
        Ssb = take(2, 2, NG_ATT * 384)
        take = region(high_pre + 4096, COLS)
        neg_sb = take(NG_ATT, 384)
        PT = take(2, 384)
        gates = take(4, 2, 2 * T)
        take = region(GU1, ring_at)
        mT = take(KD, T)
        ma = take(512)
        mb = take(512)
        xt_sb = take(NT, D)
        h2T = take(KD, T)
        gmoe = take(D)
        wr = take(KD, 36)
        rt = take(NT, 36)
        take = region(GU0, GU1)
        wpg_sb = take(KD, D)
        wpp_sb = take(T // P, D)
        pT_sb = take(T // P, T)
        gple = take(D)
        gfin = take(D)
        take = region(GU1, DN)
        h3T = take(KD, T)
        gate = take(NT, D)
        h3 = h2

        def C(name):
            at, n = CST[name]
            return c_all[:, at:at + n] if at < N_CST else crw_sb[:, at - N_CST:at - N_CST + n]

        def V(name, i):
            at = CVEC[name][0] + i
            return cv[:, at:at + 1]

        ident = C("ident")

        sems = {}

        def S(name):
            if name not in sems:
                sems[name] = ctx.enter_context(nc.semaphore("s_" + name))
            return sems[name]

        class Chain:

            def __init__(self, eng, own):
                self.eng, self.own, self.n = eng, own, {}

            def __call__(self, ins, signal=None):
                name = signal or self.own
                self.n[name] = self.n.get(name, 0) + 1
                ins.then_inc(S(name), 1)
                self.eng.wait_ge(S(name), self.n[name])

        block = ctx.enter_context(nc.Block())
        W0 = N_CRW - N_CST

        @block.sync
        def _(sp):
            sp.dma_start(c_all, cst).then_inc(S("ld_cst"), 16)
            sp.dma_start(cv, cvec).then_inc(S("ld_cvec"), 16)
            sp.dma_start(xT_sb, xT).then_inc(S("ld_xT"), 16)

            def unit(n, slot, first=False):
                if not first:
                    sp.wait_ge(S("unit_used"), n - RING + 1)
                sp.dma_start(ring[slot], stream[bass.ds(n, 1)].rearrange("a p n -> p (a n)")).then_inc(
                    S(f"unit_landed{slot}"), 16)

            for n in range(RING):
                unit(n, n, first=True)
            sp.dma_start(crw_sb, crw).then_inc(S("ld_crw"), 16)
            sp.dma_start(lora_sb, lora).then_inc(S("ld_lora"), 16)
            sp.dma_start(g2_sb, g2).then_inc(S("ld_g2"), 16)
            for n in range(RING, 13):
                unit(n, n % RING)

            def load_gate_up(trip, i, q, fresh):
                for e in range(BATCH):
                    which = i * (2 * BATCH) + q * BATCH + e
                    if not fresh and e == 0:
                        sp.wait_ge(S("gu_used"), 2 * trip + q)
                    sp.dma_start(gu_w[q][e], wgu[bass.ds(which, 1)].rearrange("a p k f -> p (a k) f")).then_inc(
                        S(f"gu_landed{q}{e}"), 16)

            def load_down(trip, i, q, fresh):
                for e in range(BATCH):
                    which = i * (2 * BATCH) + q * BATCH + e
                    if not fresh and e == 0:
                        sp.wait_ge(S("dn_out"), 2 * (2 * trip + q))
                    sp.dma_start(dn_w[e], wd[bass.ds(which, 1)].rearrange("a p k f -> p (a k) f")).then_inc(
                        S(f"dn_landed{e}"), 16)

            def load(trip, i, q, fresh):
                load_gate_up(trip, i, q, fresh)
                load_down(trip, i, q, fresh)

            with sp.Fori(0, 4) as i:
                for j in range(RING):
                    unit(13 + RING * i + j, (13 + j) % RING)
            sp.wait_ge(S("ya_out"), NT)
            sp.dma_start(neg_sb, neg).then_inc(S("ld_neg"), 16)
            for n in range(25, 28):
                unit(n, n % RING)
            load_gate_up(0, 0, 0, True)
            for n in range(28, 36):
                unit(n, n % RING)
            sp.wait_ge(S("scores_out"), NPAIR)
            sp.dma_start(xt_sb, xtok).then_inc(S("ld_x"), 16)
            sp.dma_start(gmoe, gain3[0]).then_inc(S("ld_gmoe"), 16)
            sp.dma_start(wr, router).then_inc(S("ld_wr"), 16)
            for n in range(36, 41):
                unit(n, n % RING)
            sp.wait_ge(S("PV_done"), 6 * NPAIR)
            load_down(0, 0, 0, True)
            sp.wait_ge(S("unit_used"), 41)
            sp.wait_ge(S("mask_ready"), 2)
            load_gate_up(0, 0, 1, True)
            load_down(0, 0, 1, False)
            with sp.Fori(1, NBATCH // 2) as i:
                load(i, i, 0, False)
                load(i, i, 1, False)
            passes = sp.value_load(npass_i[0:1, 0:1], min_val=1, max_val=NPASS)
            with sp.If(passes > 1):
                with sp.Fori(1, passes) as b:
                    with sp.Fori(0, NBATCH // 2) as i:
                        load(b * (NBATCH // 2) + i, i, 0, False)
                        load(b * (NBATCH // 2) + i, i, 1, False)
            sp.wait_ge(S("gu_used"), passes * NBATCH)
            sp.dma_start(wpp_sb, wpp).then_inc(S("ld_wpp"), 16)
            sp.dma_start(pT_sb, pT).then_inc(S("ld_pT"), 16)
            sp.dma_start(wpg_sb, wpg).then_inc(S("ld_wpg"), 16)
            sp.dma_start(gple, gain3[1]).then_inc(S("ld_gple"), 16)
            sp.dma_start(gfin, gain3[2]).then_inc(S("ld_gfin"), 16)
            for t in range(NT):
                sp.wait_ge(S("out_ready"), t + 1)
                sp.dma_start(out[0, t * P:(t + 1) * P, :], x1[:, t]).then_inc(S(f"out_stored{t}"), 16)
            for t in range(NT):
                sp.wait_ge(S(f"out_stored{t}"), 16)

        @block.tensor
        def _(pe):
            mm = nc.tensor.matmul

            def tr(o, i):
                return nc.tensor.transpose(o, i, ident)

            pe.wait_ge(S("ld_cst"), 16)
            pe.wait_ge(S("sq_ready"), 1)
            for k in range(KD):
                m = mm(ps[:, 7, 0:T], C("ones"), sq[:, k], start=k == 0, stop=k == KD - 1)
            m.then_inc(S("ssq_done"), 1)
            pe.wait_ge(S("hT_ready"), 1)

            def landed(n, slot):
                pe.wait_ge(S(f"unit_landed{slot}"), 16 * (n // RING) + 16)

            def half(n, c, bank, w_slot=None):
                w = ring[n % RING if w_slot is None else w_slot].rearrange("p (k c) -> p k c", k=KD)
                for k in range(KD):
                    m = mm(ps[:, bank, c * T:(c + 1) * T], w[:, k, c * P:(c + 1) * P], hT[:, k],
                           start=k == 0, stop=k == KD - 1)
                if c:
                    m.then_inc(S("unit_used"), 1)

            def project(n):
                landed(n, n % RING)
                if n >= RING:
                    pe.wait_ge(S("proj_read"), n - RING + 1)
                for c in range(2):
                    half(n, c, n % RING)

            def headsum(src, bank):
                for c in range(2):
                    m = mm(ps[:, bank + c], C("block"), src[:, 2 * c:2 * c + 2].rearrange("p n t -> p (n t)"),
                           start=True, stop=True)
                m.then_inc(S("headsum"), 1)

            project(0)
            project(1)
            pe.wait_ge(S("ld_lora"), 16)
            pe.wait_ge(S("ld_g2"), 16)
            pe.wait_ge(S("lora_in"), 2)
            for kind in range(3):
                if kind == 2:
                    pe.wait_ge(S("lora_read"), 1)
                for c in range(NPAIR):
                    w = g2_sb if kind == 2 else lora_sb[:, kind]
                    m = mm(ps[:, (3, 5, 3)[kind] + c // 2, (c % 2) * T:(c % 2 + 1) * T], w[:, c * P:(c + 1) * P],
                           lin[:, 1] if kind == 2 else lin[:, 0], start=True, stop=True)
                m.then_inc(S("lora_out"), 1)
            project(2)
            project(3)
            project(4)
            pe.wait_ge(S("ld_crw"), 16)
            pe.wait_ge(S("kksq_ready"), 1)
            pe.wait_ge(S("lora_read"), 2)
            headsum(bT, 5)
            project(5)
            pe.wait_ge(S("rk_ready"), 1)
            pe.wait_ge(S("lora_read"), 3)
            headsum(rhoT, 3)
            project(6)

            for i, (src, ready) in enumerate(((vT, "z_ready"), (bT, "b_ready"), (kaT, "ka_ready"), (alT, "al_ready"))):
                pe.wait_ge(S(ready), 7 if i == 0 else 1)
                for t in range(NT):
                    j = NT * i + t
                    if j == 1:
                        pe.wait_ge(S("proj_read"), 7)
                    if j >= 4:
                        pe.wait_ge(S("tok_read"), j - 3)
                    for c in range(NPAIR):
                        m = tr(ps[:, (7, 0, 1, 2)[j % 4], c * P:(c + 1) * P], src[:, c, t * P:(t + 1) * P])
                    m.then_inc(S("tok_out"), 1)

            pe.wait_ge(S("arz_ready"), 1)
            def small_products(t):
                tt = slice(t * P, (t + 1) * P)
                if t == 0:
                    pe.wait_ge(S("headsum_read"), 2)
                    pe.wait_ge(S("tok_read"), 8)
                else:
                    pe.wait_ge(S("XAT_ready"), t)
                    pe.wait_ge(S("XNV_ready"), t)
                for n in range(NPAIR):
                    for i, src in enumerate((bT, kaT)):
                        if n >= 2:
                            pe.wait_ge(S("mats_read"), 8 * t + 2 * (n - 2) + i + 1)
                        mm(ps[:, 2 + 2 * (n % 2) + i].rearrange("p (a t) -> p a t", a=4), src[:, n, tt],
                           arz[:, n].rearrange("p a b t -> p (a b) t")[:, :, tt], start=True, stop=True)\
                            .then_inc(S("mats_out"), 1)
                for g in range(2):
                    pe.wait_ge(S("mats_read"), 8 * t + 4 * g + 4)
                    for h in range(4):
                        m = tr(ps[:, 6 + g, h * P:(h + 1) * P], mats(t, 2 * g + h // 2, 0)[:, (h % 2) * P:(h % 2 + 1) * P])
                    m.then_inc(S("M_out"), 1)

            def inverse_first(t, l):
                for g in range(2):
                    pe.wait_ge(S("mlev_ready"), (LEVELS - 1) * 2 * t + 2 * (l - 1) + g + 1)
                    pe.wait_ge(S("Z_ready"), LEVELS * 2 * t + 2 * (l - 1) + g + 1)
                    if l == 1:
                        pe.wait_ge(S("mats_read"), 8 * t + 8)
                    for h in range(4 * g, 4 * g + 4):
                        m = mm(ps[:, 2 + g, (h % 4) * P:(h % 4 + 1) * P], mlev[:, l % 2, h], Z_sb[:, h], start=True, stop=True)
                    m.then_inc(S("T1_out"), 1)

            def inverse_second(t, l):
                for g in range(2):
                    pe.wait_ge(S("T1_ready"), (LEVELS - 1) * 2 * t + 2 * (l - 1) + g + 1)
                    pe.wait_ge(S("X_ready"), (LEVELS - 1) * 2 * t + 2 * (l - 1) + g + 1)
                    for h in range(4 * g, 4 * g + 4):
                        m = mm(ps[:, 4 + g, (h % 4) * P:(h % 4 + 1) * P], X_sb[:, h], T1_sb[:, h], start=True, stop=True)
                    m.then_inc(S("D_out"), 1)
                    if l < LEVELS - 1:
                        for h in range(4 * g, 4 * g + 4):
                            m = mm(ps[:, 6 + g, (h % 4) * P:(h % 4 + 1) * P], T1_sb[:, h], X_sb[:, h], start=True, stop=True)
                        m.then_inc(S("DT_out"), 1)

            def apply_inverse(t, between=lambda: None):
                pe.wait_ge(S("Z_ready"), LEVELS * 2 * (t + 1))
                for h in range(NH):
                    m = mm(ps[:, 2, h * HD:(h + 1) * HD], mats(t, h // 2, 1)[:, (h % 2) * P:(h % 2 + 1) * P],
                           Vtok[:, t, h * HD:(h + 1) * HD], start=True, stop=True)
                m.then_inc(S("NV_out"), 1)
                for h in range(NH):
                    m = mm(ps[(h % 2) * HD:(h % 2 + 1) * HD, 3, (h // 2) * P:(h // 2 + 1) * P],
                           Atok[:, t, h * HD:(h + 1) * HD], Z_sb[:, h], start=True, stop=True)
                m.then_inc(S("XAT_out"), 1)
                between()
                pe.wait_ge(S("NV_ready"), t + 1)
                for h in range(NH):
                    m = mm(ps[:, 4, h * HD:(h + 1) * HD], Z_sb[:, h], NV[:, h * HD:(h + 1) * HD], start=True, stop=True)
                m.then_inc(S("XNV_out"), 1)

            def chain_bank(t):
                return 0 if t == 0 else 2

            def chunk_inputs(t, c):
                cc, rows = 2 * t + c, slice(c * CH, (c + 1) * CH)
                pe.wait_ge(S("XAT_ready"), t + 1)
                pe.wait_ge(S("state_ready"), 1 + cc)
                for n in range(NPAIR):
                    m = mm(ps[rows, chain_bank(t), n * P:(n + 1) * P], XAT2[t][:, n, rows], Th[:, cc, n], start=True, stop=True)
                m.then_inc(S("U_out"), 1)

            def chunk_state(t, c):
                cc, rows = 2 * t + c, slice(c * CH, (c + 1) * CH)
                pe.wait_ge(S("U_ready"), cc + 1)
                for n in range(NPAIR):
                    o = ps[:, chain_bank(t) + 1, n * P:(n + 1) * P]
                    mm(o, Ktok[rows, t, n * P:(n + 1) * P], Vtok[rows, t, n * P:(n + 1) * P], start=True, stop=False)
                    m = mm(o, Btok[rows, t, n * P:(n + 1) * P], U_sb[rows, n * P:(n + 1) * P], start=False, stop=True)
                m.then_inc(S("dT_out"), 1)

            def tile_outputs(t):
                bank = chain_bank(t)
                for c in range(2):
                    rows = slice(c * CH, (c + 1) * CH)
                    for n in range(NPAIR):
                        mm(ps[rows, bank, n * P:(n + 1) * P], rhoT[:, n, t * P + c * CH:t * P + (c + 1) * CH],
                           Th[:, 2 * t + c, n], start=n == 0, stop=False, skip_group_check=True)
                for h in range(NH):
                    cols = slice(h * HD, (h + 1) * HD)
                    hh = slice(2 * P + (h % 2) * P, 2 * P + (h % 2 + 1) * P)
                    mm(ps[:, bank, cols], mats(t, h // 2, 0)[:, hh], U_sb[:, cols], start=False, stop=False, skip_group_check=True)
                    m = mm(ps[:, bank, cols], mats(t, h // 2, 1)[:, hh], Vtok[:, t, cols], start=False,
                           stop=h == NH - 1, skip_group_check=True)
                m.then_inc(S("Y_out"), 1)

            def turn_outputs(t):
                pe.wait_ge(S("yn_ready"), t + 1)
                for n in range(NPAIR):
                    m = tr(ps[:, chain_bank(t) + 1, n * P:(n + 1) * P], yc[:, 2 * n:2 * n + 2].rearrange("p h d -> p (h d)"))
                m.then_inc(S("ynT_out"), 1)

            small_products(0)
            for l in range(1, LEVELS):
                inverse_first(0, l)
                inverse_second(0, l)
            apply_inverse(0)
            small_products(1)
            steps = [lambda: chunk_inputs(0, 0), lambda: chunk_state(0, 0), lambda: chunk_inputs(0, 1),
                     lambda: chunk_state(0, 1), lambda: tile_outputs(0)]
            for l in range(1, LEVELS):
                inverse_first(1, l)
                steps[l - 1]()
                inverse_second(1, l)
            turned = [False]

            def q_half(i):
                n = 7 + i // 2
                if i % 2 == 0:
                    landed(n, n % RING)
                    if n >= 9:
                        pe.wait_ge(S("proj_read"), n - 1)
                    else:
                        pe.wait_ge(S("ya_out"), 1)
                half(n, i % 2, n % 2)

            turn_outputs(0)
            apply_inverse(1, lambda: None)
            chunk_inputs_steps = [lambda: chunk_inputs(1, 0), lambda: chunk_state(1, 0), lambda: chunk_inputs(1, 1),
                                  lambda: chunk_state(1, 1), lambda: tile_outputs(1)]
            for i, step in enumerate(chunk_inputs_steps):
                q_half(i)
                step()
            for i in range(5, 8):
                q_half(i)
            turn_outputs(1)
            for i in range(8, 12):
                q_half(i)

            pe.wait_ge(S("ya_out"), NT)
            pe.wait_ge(S("proj_read"), 13)
            with pe.Fori(0, 2) as i:
                for j in range(RING):
                    n, slot = 13 + RING * i + j, (13 + j) % RING
                    landed(n, slot)
                    pe.wait_ge(S("proj_read"), n - RING + 1)
                    for c in range(2):
                        half(n, c, slot, slot)
            with pe.Fori(0, 2) as i:
                for j in range(RING):
                    n, slot = 19 + RING * i + j, (19 + j) % RING
                    landed(n, slot)
                    pe.wait_ge(S("proj_read"), n - RING + 1)
                    w = ring[slot].rearrange("p (k c) -> p k c", k=KD)
                    for t in range(NT):
                        for k in range(KD):
                            m = mm(ps[:, slot, t * T:(t + 1) * T], hT[:, k, t * P:(t + 1) * P], w[:, k],
                                   start=k == 0, stop=k == KD - 1)
                    m.then_inc(S("unit_used"), 1)

            def scores(n):
                if n == 0:
                    pe.wait_ge(S("proj_read"), 25)
                else:
                    pe.wait_ge(S("scores_read"), 12 * n)
                for g in range(NG_ATT):
                    c = g * NPAIR + n
                    m = mm(ps[:, g].rearrange("p (h t) -> p h t", h=2), qT[:, c, P:T], kz[:, c], start=True, stop=True)
                    m = mm(ps[:, 3 + g // 2, (g % 2) * T:(g % 2 + 1) * T].rearrange("p (h t) -> p h t", h=2),
                           qT[:, c, 0:P], kz[:, c, :, 0:P], start=True, stop=True)
                m.then_inc(S("scores_out"), 1)

            gate_mms = [0]

            def gate_columns(upto):
                while gate_mms[0] < upto:
                    u, i = divmod(gate_mms[0], 2 * KD)
                    n = 25 + u
                    if i == 0:
                        landed(n, n % RING)
                        pe.wait_ge(S("proj_read"), n)
                    c, k = divmod(i, KD)
                    w = ring[n % RING].rearrange("p (k c) -> p k c", k=KD)
                    m = mm(ps[:, 6, c * T:(c + 1) * T], w[:, k, c * P:(c + 1) * P], hT[:, k], start=k == 0, stop=k == KD - 1)
                    if i == 2 * KD - 1:
                        m.then_inc(S("unit_used"), 1)
                    gate_mms[0] += 1

            total = 8 * 2 * KD
            scores(0)
            gate_columns(16)
            for n in range(NPAIR):
                if n + 1 < NPAIR:
                    scores(n + 1)
                for h in range(2):
                    hd = 2 * n + h
                    pe.wait_ge(S("probs_ready"), 2 * hd + 2)
                    for g in range(NG_ATT):
                        i = hd * NG_ATT + g
                        if i:
                            pe.wait_ge(S("PT_ready"), i)
                        src = Ssb[:, n % 2, h]
                        tr(ps[:, 5, 0:P], src[:, g * P:(g + 1) * P])
                        tr(ps[:, 5, P:2 * P], src[:, 384 + g * T:384 + g * T + P])
                        tr(ps[:, 5, 2 * P:3 * P], src[:, 384 + g * T + P:384 + (g + 1) * T]).then_inc(S("PT_out"), 1)
                        gate_columns(16 + (total - 16) * (i + 1) // (6 * NPAIR))
                        if g == 0 and h == 0 and n >= 1:
                            pe.wait_ge(S("yb_read"), n)
                        pe.wait_ge(S("PT_ready"), i + 1)
                        rows = slice(h * HD, (h + 1) * HD)
                        vc = slice(g * RW + hd * HD, g * RW + (hd + 1) * HD)
                        mm(ps[rows, 7, 0:T], vtok[:, 0, vc], PT[:, i % 2, 0:T], start=g == 0, stop=False,
                           skip_group_check=True)
                        m = mm(ps[rows, 7, P:T], vtok[:, 1, vc], PT[:, i % 2, T:T + P], start=False, stop=g == 2,
                               skip_group_check=True)
                        m.then_inc(S("PV_done"), 1)

            pe.wait_ge(S("yb_read"), NPAIR)
            for j in range(4):
                n = 33 + j
                landed(n, n % RING)
                if j >= 2:
                    pe.wait_ge(S("merged"), j - 1)
                w = ring[n % RING].rearrange("p (b k c) -> p b k c", b=2, k=NPAIR)
                for b, y in enumerate((yaT, ybT)):
                    for c in range(2):
                        for k in range(NPAIR):
                            m = mm(ps[:, 2 * (j % 2) + b, c * T:(c + 1) * T], w[:, b, k, c * P:(c + 1) * P], y[:, k],
                                   start=k == 0, stop=k == NPAIR - 1)
                m.then_inc(S("unit_used"), 1)

            for u in range(4):
                n = 37 + u
                landed(n, n % RING)
                w = ring[n % RING].rearrange("p (k c) -> p k c", k=2)
                pe.wait_ge(S("merged"), u + 1)
                for k in range(2):
                    kk = 2 * u + k
                    for t in range(NT):
                        for hf in range(2):
                            m = mm(ps[:, 4 + 2 * t + hf], mT[:, kk, t * P:(t + 1) * P], w[:, k, hf * 512:(hf + 1) * 512],
                                   start=kk == 0, stop=kk == KD - 1)
                m.then_inc(S("unit_used"), 1)
            for t in range(NT):
                pe.wait_ge(S("h2_ready"), t + 1)
                for hf in range(2):
                    for k in range(4):
                        m = tr(ps[:, 2 * t + hf, k * P:(k + 1) * P], h2[:, t, (4 * hf + k) * P:(4 * hf + k + 1) * P])
                    m.then_inc(S("h2T_out"), 1)
            pe.wait_ge(S("ld_wr"), 16)
            for t in range(NT):
                pe.wait_ge(S("h2T_ready"), 2 * t + 2)
                for k in range(KD):
                    m = mm(ps[:, 4 + t, 0:36], h2T[:, k, t * P:(t + 1) * P], wr[:, k], start=k == 0, stop=k == KD - 1)
                m.then_inc(S("logits_out"), 1)
            pe.wait_ge(S("mask_ready"), 2)
            mm(ps[:, 6, 0:E], C("before"), rmask[:, 0], start=True, stop=True)
            mm(ps[:, 6, E:2 * E], C("ones"), rmask[:, 0], start=True, stop=False)
            mm(ps[:, 6, E:2 * E], C("before"), rmask[:, 1], start=False, stop=True)
            mm(ps[:, 6, 2 * E:3 * E], C("ones"), rmask[:, 0], start=True, stop=False)
            mm(ps[:, 6, 2 * E:3 * E], C("ones"), rmask[:, 1], start=False, stop=True).then_inc(S("pos_out"), 1)

            pe.wait_ge(S("passes_ready"), 1)
            passes = pe.value_load(npass_i[0:1, 0:1], min_val=1, max_val=NPASS)
            pe.wait_ge(S("zero_ready"), 1)
            for j in range(4):
                mm(ps[:, j], zero[:, 0:P], zero, start=True, stop=False, skip_group_check=True)
            for name in ("ysb0_ready", "ysb1_ready", "batch_done", "gu_used"):
                pe.sem_inc(S(name), 1)
            with pe.Fori(0, passes) as b:
                with pe.Fori(0, NBATCH // 2) as i:
                    for q in range(2):
                        trip = b * (NBATCH // 2) + i
                        done = 2 * trip + q
                        if q == 0:
                            pe.wait_ge(S("sel_ready"), 2 * b + 2)
                        pe.wait_ge(S("ysb0_ready"), done + 1)
                        pe.wait_ge(S("ysb1_ready"), done + 1)
                        for k in range(KD):
                            for t in range(NT):
                                m = mm(ps[:, 4 + k // 4, (k % 4) * P:(k % 4 + 1) * P], h2[:, t, k * P:(k + 1) * P],
                                       sel[:, t, bass.ds(i * (2 * P) + q * P, P)], start=t == 0, stop=t == NT - 1)
                            if k % 4 == 3:
                                m.then_inc(S("gath_out"), 1)
                        for e in range(BATCH):
                            pe.wait_ge(S(f"gu_landed{q}{e}"), 16 * trip + 16)
                        pe.wait_ge(S("gath0_ready"), done + 1)
                        pe.wait_ge(S("gath1_ready"), done + 1)
                        for k in range(KD):
                            for e in range(BATCH):
                                m = mm(ps[e * SLOTS:(e + 1) * SLOTS, 6], hg[:, k, e * SLOTS:(e + 1) * SLOTS],
                                       gu_w[q][e][:, k], start=k == 0, stop=k == KD - 1)
                        m.then_inc(S("gu_used"), 1)
                        pe.wait_ge(S("selw_ready"), done + 1)
                        for t in range(NT):
                            m = tr(ps[:, 7, t * P:(t + 1) * P], selw[:, t])
                        m.then_inc(S("selwT_out"), 1)
                        pe.wait_ge(S("act_ready"), done + 1)
                        for f in range(F // P):
                            m = tr(ps[:, 7, T + f * P:T + (f + 1) * P], act[:, f * P:(f + 1) * P])
                        m.then_inc(S("actT_out"), 1)
                        for e in range(BATCH):
                            pe.wait_ge(S(f"dn_landed{e}"), 32 * trip + 16 * q + 16)
                        pe.wait_ge(S("actT_ready"), done + 1)
                        for hf in range(2):
                            for f in range(F // P):
                                for e in range(BATCH):
                                    m = mm(ps[e * SLOTS:(e + 1) * SLOTS, 4 + hf], actT[:, f, e * SLOTS:(e + 1) * SLOTS],
                                           dn_w[e][:, f, hf * 512:(hf + 1) * 512], start=f == 0, stop=f == F // P - 1)
                            m.then_inc(S("dn_out"), 1)
                        pe.wait_ge(S("selwT_ready"), done + 1)
                        for hf in range(2):
                            pe.wait_ge(S(f"ysb{hf}_ready"), done + 2)
                            for t in range(NT):
                                m = mm(ps[:, 2 * t + hf], selwT[:, t], ysb[:, hf * 512:(hf + 1) * 512],
                                       start=False, stop=False, skip_group_check=True)
                        m.then_inc(S("batch_done"), 1)
            for j in range(4):
                m = mm(ps[:, j], zero[:, 0:P], zero, start=False, stop=True, skip_group_check=True)
            m.then_inc(S("moe_done"), 1)

            pe.wait_ge(S("ld_wpp"), 16)
            pe.wait_ge(S("ld_pT"), 16)
            for t in range(NT):
                for hf in range(2):
                    for k in range(2):
                        m = mm(ps[:, 4 + 2 * t + hf], pT_sb[:, k, t * P:(t + 1) * P], wpp_sb[:, k, hf * 512:(hf + 1) * 512],
                               start=k == 0, stop=k == 1)
            for t in range(NT):
                pe.wait_ge(S("h3_ready"), t + 1)
                pe.wait_ge(S("x2_ready"), 2)
                for hf in range(2):
                    for k in range(4):
                        m = tr(ps[:, 2 * t + hf, k * P:(k + 1) * P], h3[:, t, (4 * hf + k) * P:(4 * hf + k + 1) * P])
                    m.then_inc(S("h3T_out"), 1)
            pe.wait_ge(S("ld_wpg"), 16)
            pe.wait_ge(S("h3T_ready"), 4)
            for t in range(NT):
                for hf in range(2):
                    for k in range(KD):
                        m = mm(ps[:, 2 * t + hf], h3T[:, k, t * P:(t + 1) * P], wpg_sb[:, k, hf * 512:(hf + 1) * 512],
                               start=k == 0, stop=k == KD - 1)
                m.then_inc(S("gate_out"), 1)

        @block.scalar
        def _(a):
            do = Chain(a, "act")
            A = nc.scalar.activation
            eps = C("eps")

            def copy(o, i, scale=1.0):
                return A(o, i, ACT.Copy, scale=scale)

            a.wait_ge(S("ld_xT"), 16)
            A(sq, xT_sb, ACT.Square).then_inc(S("sq_ready"), 1)
            a.wait_ge(S("ld_cst"), 16)
            a.wait_ge(S("ld_cvec"), 16)
            a.wait_ge(S("ssq_done"), 1)
            A(rstd_bc, ps[:, 7, 0:T], ACT.Sqrt, scale=1.0 / D, bias=eps[:, 0:1]).then_inc(S("rms_ready"), 1)
            a.wait_ge(S("zeroed"), 1)

            def take_unit(n):
                a.wait_ge(S("unit_used"), n + 1)
                if n:
                    a.wait_ge(S("z_ready"), n)
                copy(shift[:, :, 1:T + 1], ps[:, n % RING].rearrange("p (c t) -> p c t", c=2)).then_inc(S("proj_read"), 1)

            take_unit(0)
            a.wait_ge(S("z_ready"), 1)
            A(lin[0:W_LORA, 0], lin[0:W_LORA, 0], ACT.Tanh).then_inc(S("lora_in"), 1)
            A(lin[:, 1], lin[:, 1], ACT.Sigmoid).then_inc(S("lora_in"), 1)
            take_unit(1)
            for kind, dst, name in ((0, swT, "w0"), (1, aT_, "a0")):
                a.wait_ge(S("lora_out"), kind + 1)
                for c in range(NPAIR):
                    ins = A(dst[:, c], ps[:, 3 + 2 * kind + c // 2, (c % 2) * T:(c % 2 + 1) * T], ACT.Sigmoid, bias=V(name, c))
                    if c == NPAIR - 1:
                        ins.then_inc(S("lora_read"), 1)
                    else:
                        do(ins)
            a.wait_ge(S("lora_out"), 3)
            copy(gT.rearrange("p n t -> p (n t)"), ps[:, 3:5].rearrange("p b t -> p (b t)")).then_inc(S("lora_read"), 1)
            take_unit(2)
            take_unit(3)
            a.wait_ge(S("cum_ready"), 1)
            A(wincT, cumT, ACT.Exp, scale=-DECAY).then_inc(S("winc_ready"), 1)
            A(winvT, cumT, ACT.Exp, scale=DECAY).then_inc(S("winv_ready"), 1)
            a.wait_ge(S("cumx_ready"), 1)
            A(wexT, wexT, ACT.Exp, scale=-DECAY).then_inc(S("wex_ready"), 1)
            take_unit(4)
            a.wait_ge(S("headsum"), 1)
            A(alT.rearrange("p n t -> p (n t)"), ps[:, 5:7].rearrange("p b t -> p (b t)"), ACT.Sqrt, bias=eps[:, 2:3])\
                .then_inc(S("kknorm"), 1)
            take_unit(5)
            take_unit(6)
            for i, dst in enumerate((Vtok, Btok, Ktok, Atok)):
                for t in range(NT):
                    j = NT * i + t
                    a.wait_ge(S("tok_out"), j + 1)
                    copy(dst[:, t], ps[:, (7, 0, 1, 2)[j % 4]]).then_inc(S("tok_read"), 1)

            def take_M(t):
                for g in range(2):
                    if t:
                        a.wait_ge(S("mlev_ready"), 2 * (LEVELS - 1) * t)
                        a.wait_ge(S("X_ready"), 2 * (LEVELS - 1) * t)
                    a.wait_ge(S("M_out"), 2 * t + g + 1)
                    copy(M_sb[:, 4 * g:4 * g + 4].rearrange("p h t -> p (h t)"), ps[:, 6 + g]).then_inc(S("M_ready"), 1)

            def take_first(t, l):
                for g in range(2):
                    a.wait_ge(S("T1_out"), 2 * (LEVELS - 1) * t + 2 * (l - 1) + g + 1)
                    copy(T1_sb[:, 4 * g:4 * g + 4].rearrange("p h t -> p (h t)"), ps[:, 2 + g]).then_inc(S("T1_ready"), 1)

            def take_inverse(t):
                a.wait_ge(S("NV_out"), t + 1)
                copy(NV, ps[:, 2]).then_inc(S("NV_ready"), 1)
                a.wait_ge(S("XAT_out"), t + 1)
                copy(XAT2[t].rearrange("p n t -> p (n t)"), ps[:, 3]).then_inc(S("XAT_ready"), 1)
                a.wait_ge(S("XNV_out"), t + 1)
                copy(XNV2[t], ps[:, 4]).then_inc(S("XNV_ready"), 1)

            def deviation(t):
                a.wait_ge(S("var_ready"), t + 1)
                A(stat_a[:, 0:8], stat_a[:, 0:8], ACT.Sqrt, scale=1.0 / HD, bias=eps[:, 1:2]).then_inc(S("sd_ready"), 1)

            def take_q(n):
                a.wait_ge(S("unit_used"), n + 1)
                copy(qT[:, 2 * (n - 7):2 * (n - 7) + 2], ps[:, n % 2].rearrange("p (c t) -> p c t", c=2),
                     scale=HD ** -0.5).then_inc(S("proj_read"), 1)

            take_M(0)
            for l in range(1, LEVELS):
                take_first(0, l)
            take_inverse(0)
            take_M(1)
            for l in range(1, LEVELS):
                take_first(1, l)
            deviation(0)
            take_inverse(1)
            a.wait_ge(S("mats_out"), 16)
            for n in range(7, 10):
                take_q(n)
            deviation(1)
            for n in range(10, 13):
                take_q(n)

            a.wait_ge(S("kz_zeroed"), 2)
            with a.Fori(0, 2) as i:
                for j in range(RING):
                    a.wait_ge(S("unit_used"), 13 + RING * i + j + 1)
                    for h in range(2):
                        rows = slice(h * HD, (h + 1) * HD)
                        ins = copy(kz[rows, bass.ds(2 * RING * i + 2 * j, 2), h],
                                   ps[rows, (13 + j) % RING].rearrange("p (c t) -> p c t", c=2))
                        ins.then_inc(S("proj_read") if h else S("kz_half"), 1)
            with a.Fori(0, 2) as i:
                for j in range(RING):
                    a.wait_ge(S("unit_used"), 19 + RING * i + j + 1)
                    copy(vtok[:, :, bass.ds((RING * i + j) * T, T)], ps[:, (19 + j) % RING].rearrange("p (c t) -> p c t", c=2)
                         ).then_inc(S("proj_read"), 1)

            def exps(n):
                for h in range(2):
                    for b in range(2):
                        i = 4 * n + 2 * h + b
                        v = Ssb[:, n % 2, h, 0:384] if b == 0 else Ssb[:, n % 2, h, 384:1152]
                        a.wait_ge(S("max_ready"), i + 1)
                        A(v, v, ACT.Exp, bias=st_max[:, i:i + 1], accum_out=stat_a[:, i:i + 1]).then_inc(S("exp_ready"), 1)

            def take_gates(u):
                a.wait_ge(S("unit_used"), 26 + u)
                A(gates[:, u // 2, u % 2], ps[:, 6], ACT.Sigmoid).then_inc(S("proj_read"), 1)

            gates_taken = 0
            exps(0)
            for n in range(NPAIR):
                if n + 1 < NPAIR:
                    exps(n + 1)
                for i in range(6 * n, 6 * n + 6):
                    a.wait_ge(S("PT_out"), i + 1)
                    if i >= 2:
                        a.wait_ge(S("PV_done"), i - 1)
                    copy(PT[:, i % 2], ps[:, 5, 0:384]).then_inc(S("PT_ready"), 1)
                    while gates_taken < 8 and 16 * (gates_taken + 1) <= 16 + 112 * (i + 1) // (6 * NPAIR):
                        take_gates(gates_taken)
                        gates_taken += 1
                a.wait_ge(S("PV_done"), 6 * n + 6)
                copy(ybT[:, n], ps[:, 7, 0:T]).then_inc(S("yb_read"), 1)
            def sd(src, i, junk):
                do(A(junk, src, ACT.Square, accum_out=stat_a[:, 16 + i:17 + i]))
                A(stat_a[:, i:i + 1], stat_a[:, 16 + i:17 + i], ACT.Sqrt, scale=1.0 / D, bias=eps[:, 0:1])\
                    .then_inc(S("rms_ready"), 1)

            junk = hg.rearrange("p k t -> p (k t)")
            for t in range(NT):
                a.wait_ge(S("x1_ready"), t + 1)
                sd(x1[:, t], t, junk)
            for i in range(4):
                a.wait_ge(S("h2T_out"), i + 1)
                t, hf = i // 2, i % 2
                copy(h2T[:, 4 * hf:4 * hf + 4, t * P:(t + 1) * P], ps[:, i].rearrange("p (k t) -> p k t", k=4))\
                    .then_inc(S("h2T_ready"), 1)
            for t in range(NT):
                a.wait_ge(S("route_max"), t + 1)
                A(rt[:, t, 0:EG], rt[:, t, 0:EG], ACT.Exp, bias=stat[:, 16 + t:17 + t], accum_out=stat_a[:, 4 + t:5 + t])\
                    .then_inc(S("route_exp"), 1)
                a.wait_ge(S("route_second"), t + 1)
                A(stat_a[:, 6 + t:7 + t], stat[:, 20 + t:21 + t], ACT.Exp).then_inc(S("route_exp"), 1)
            a.wait_ge(S("passes_ready"), 1)
            passes = a.value_load(npass_i[0:1, 0:1], min_val=1, max_val=NPASS)
            with a.Fori(0, passes) as b:
                with a.Fori(0, NBATCH // 2) as i:
                    for q in range(2):
                        done = 2 * (b * (NBATCH // 2) + i) + q
                        a.wait_ge(S("gath_out"), 2 * done + 1)
                        copy(hg[:, 0:4].rearrange("p k t -> p (k t)"), ps[:, 4]).then_inc(S("gath0_ready"), 1)
                        a.wait_ge(S("gu_used"), done + 2)
                        A(silu, ps[:, 6, 0:F], ACT.Silu).then_inc(S("silu_ready"), 1)
                        a.wait_ge(S("actT_out"), done + 1)
                        copy(actT.rearrange("p f t -> p (f t)"), ps[:, 7, T:2 * T]).then_inc(S("actT_ready"), 1)
                        a.wait_ge(S("batch_done"), done + 1)
                        a.wait_ge(S("dn_out"), 2 * done + 1)
                        copy(ysb[:, 0:512], ps[:, 4]).then_inc(S("ysb0_ready"), 1)

            for t in range(NT):
                a.wait_ge(S("x2_ready"), t + 1)
                sd(x1[:, t], 8 + t, junk)
            for i in range(4):
                a.wait_ge(S("h3T_out"), i + 1)
                t, hf = i // 2, i % 2
                copy(h3T[:, 4 * hf:4 * hf + 4, t * P:(t + 1) * P], ps[:, i].rearrange("p (k t) -> p k t", k=4))\
                    .then_inc(S("h3T_ready"), 1)
            for t in range(NT):
                a.wait_ge(S("gate_out"), t + 1)
                A(gate[:, t], ps[:, 2 * t:2 * t + 2].rearrange("p b n -> p (b n)"), ACT.Sigmoid).then_inc(S("gate_ready"), 1)
            for t in range(NT):
                a.wait_ge(S("x3_ready"), t + 1)
                sd(x1[:, t], 10 + t, junk)

        @block.gpsimd
        def _(g_):
            do = Chain(g_, "pool")
            Pg = nc.gpsimd
            do(Pg.memset(shift[:, :, 0:1], 0.0))
            Pg.memset(Th.rearrange("p a n t -> p (a n t)"), 0.0).then_inc(S("zeroed"), 1)
            g_.wait_ge(S("hT_ready"), 1)
            do(Pg.memset(arz.rearrange("p n a h t -> p (n a h t)"), 0.0))
            for kind, (src, ready) in enumerate(((alT, "al_ready"), (rhoT, "rho_ready"))):
                g_.wait_ge(S(ready), 1)
                for h in range(2):
                    rows = slice(h * HD, (h + 1) * HD)
                    do(Pg.tensor_copy(arz[rows, :, kind, h], src[rows]))
            g_.sem_inc(S("arz_ready"), 1)
            g_.wait_ge(S("ld_crw"), 16)
            g_.wait_ge(S("tok_out"), 8)
            for t in range(NT):
                for l in range(1, LEVELS):
                    for g in range(2):
                        n = 2 * (LEVELS - 1) * t + 2 * (l - 1) + g
                        if l == 1:
                            g_.wait_ge(S("M_ready"), 2 * t + g + 1)
                        if n >= 4:
                            g_.wait_ge(S("T1_out"), n - 3)
                        Pg.tensor_tensor(mlev[:, l % 2, 4 * g:4 * g + 4], M_sb[:, 4 * g:4 * g + 4],
                                         C("level")[:, l * P:(l + 1) * P].unsqueeze(1).broadcast_to([P, 4, P]), ALU.mult)\
                            .then_inc(S("mlev_ready"), 1)
            g_.wait_ge(S("merged"), 4)
            Pg.memset(zero, 0.0).then_inc(S("zero_ready"), 1)

        @block.vector
        def _(v):
            do = Chain(v, "dve")
            N = nc.vector
            tt, ts, stt = N.tensor_tensor, N.tensor_scalar, N.scalar_tensor_tensor

            def bc(x, n):
                return x.unsqueeze(2).broadcast_to([x.shape[0], x.shape[1], n])

            def bc1(x, n):
                return x.unsqueeze(1).broadcast_to([x.shape[0], n, x.shape[1]])

            v.wait_ge(S("rms_ready"), 1)
            do(N.reciprocal(rstd_bc, rstd_bc))
            for k in range(KD):
                ins = stt(hT[:, k], xT_sb[:, k], V("norm_mix", k), rstd_bc, ALU.mult, ALU.mult)
                do(ins, "hT_ready" if k == KD - 1 else None)
            zdst = [lin, kT[:, 0:2], kT[:, 2:4], rT[:, 0:2], rT[:, 2:4], vT[:, 0:2], vT[:, 2:4]]

            def shifted(n):
                v.wait_ge(S("proj_read"), n + 1)
                do(tt(dlt, shift[:, :, 0:T], shift[:, :, 1:T + 1], ALU.subtract))
                do(stt(zdst[n][:, 0], dlt[:, 0], V("mu", 2 * n), shift[:, 0, 1:T + 1], ALU.mult, ALU.add))
                do(stt(zdst[n][:, 1], dlt[:, 1], V("mu", 2 * n + 1), shift[:, 1, 1:T + 1], ALU.mult, ALU.add), "z_ready")

            flat = lambda x: x.rearrange("p n t -> p (n t)")
            shifted(0)
            shifted(1)
            shifted(2)
            for c in range(NPAIR):
                do(ts(kkT[:, c], kT[:, c], V("k_k", c), None, ALU.mult))
            do(tt(bT, kkT, kkT, ALU.mult), "kksq_ready")
            v.wait_ge(S("ld_crw"), 16)
            v.wait_ge(S("lora_read"), 1)
            do(N.tensor_tensor_scan(flat(cumT), C("reset"), flat(swT), 0.0, ALU.mult, ALU.add), "cum_ready")
            do(tt(wexT, cumT, swT, ALU.subtract), "cumx_ready")
            shifted(3)
            v.wait_ge(S("lora_read"), 2)
            for c in range(NPAIR):
                do(ts(kaT[:, c], aT_[:, c], 1.0, V("k_a", c), ALU.subtract, ALU.mult))
            do(stt(kaT, kaT, 1.0, kT, ALU.add, ALU.mult))
            shifted(4)
            for c in range(NPAIR):
                do(stt(rhoT[:, c], rT[:, c], V("r_k", c), kaT[:, c], ALU.mult, ALU.mult),
                   "rk_ready" if c == NPAIR - 1 else None)
            v.wait_ge(S("kknorm"), 1)
            do(N.reciprocal(alT, alT), "headsum_read")
            do(tt(kkT, kkT, alT, ALU.mult))
            shifted(5)
            do(tt(bT, kkT, aT_, ALU.mult))
            v.wait_ge(S("winv_ready"), 1)
            do(tt(bT, bT, winvT, ALU.mult), "b_ready")
            do(tt(kaT, kaT, winvT, ALU.mult), "ka_ready")
            v.wait_ge(S("wex_ready"), 1)
            do(stt(alT, wexT, -1.0, kkT, ALU.mult, ALU.mult), "al_ready")
            v.wait_ge(S("headsum"), 2)
            v.wait_ge(S("winc_ready"), 1)
            do(tt(rhoT, rT, wincT, ALU.mult), "rho_ready")
            shifted(6)
            do(tt(bonus, ps[:, 3:5].rearrange("p b (c t) -> p (b c) t", c=2), vT, ALU.mult), "headsum_read")

            def keep_small_products(t):
                for n in range(NPAIR):
                    for i in range(2):
                        v.wait_ge(S("mats_out"), 8 * t + 2 * n + i + 1)
                        if t == 0 and n == 0 and i == 0:
                            v.wait_ge(S("tok_out"), 8)
                            v.wait_ge(S("arz_ready"), 1)
                        do(tt(mats(t, n, i), ps[:, 2 + 2 * (n % 2) + i], C("causal"), ALU.mult), "mats_read")
                for g in range(2):
                    hh = slice(4 * g, 4 * g + 4)
                    v.wait_ge(S("M_ready"), 2 * t + g + 1)
                    if t:
                        v.wait_ge(S("XNV_ready"), t)
                    for n in range(2):
                        do(tt(Z_sb[:, 4 * g + 2 * n:4 * g + 2 * n + 2],
                              mats(t, 2 * g + n, 0)[:, 0:2 * P].rearrange("p (h t) -> p h t", h=2), bc1(C("level0T"), 2), ALU.mult))
                    do(tt(X_sb[:, hh], M_sb[:, hh], bc1(C("level")[:, 0:P], 4), ALU.mult))
                    do(tt(Z_sb[:, hh], Z_sb[:, hh], bc1(ident, 4), ALU.add), "Z_ready")
                    do(tt(X_sb[:, hh], X_sb[:, hh], bc1(ident, 4), ALU.add), "X_ready")

            def double(t, l):
                for g in range(2):
                    hh = slice(4 * g, 4 * g + 4)
                    v.wait_ge(S("D_out"), 2 * (LEVELS - 1) * t + 2 * (l - 1) + g + 1)
                    do(tt(Z_sb[:, hh], Z_sb[:, hh], ps[:, 4 + g].rearrange("p (h t) -> p h t", h=4), ALU.add), "Z_ready")
                    if l < LEVELS - 1:
                        v.wait_ge(S("DT_out"), 2 * (LEVELS - 2) * t + 2 * (l - 1) + g + 1)
                        do(tt(X_sb[:, hh], X_sb[:, hh], ps[:, 6 + g].rearrange("p (h t) -> p h t", h=4), ALU.add), "X_ready")

            def keep_inputs(t, c):
                cc, rows = 2 * t + c, slice(c * CH, (c + 1) * CH)
                if cc == 0:
                    v.wait_ge(S("zeroed"), 1)
                    v.sem_inc(S("state_ready"), 1)
                    do.n["state_ready"] = 1
                v.wait_ge(S("XNV_ready"), t + 1)
                v.wait_ge(S("U_out"), cc + 1)
                do(tt(U_sb[rows], ps[rows, 2 * t], XNV2[t][rows], ALU.add), "U_ready")

            def next_state(t, c):
                cc = 2 * t + c
                v.wait_ge(S("dT_out"), cc + 1)
                for h in range(2):
                    hr = slice(h * HD, (h + 1) * HD)
                    do(tt(Th[hr, cc + 1, :, hr], ps[hr, 2 * t + 1].rearrange("p (n t) -> p n t", n=NPAIR)[:, :, hr],
                          Th[hr, cc, :, hr], ALU.add))
                for h in range(2):
                    hr = slice(h * HD, (h + 1) * HD)
                    do(tt(Th[hr, cc + 1, :, hr], Th[hr, cc + 1, :, hr], bc(wincT[hr, :, (cc + 1) * CH - 1], HD), ALU.mult),
                       "state_ready" if h else None)

            def normed(t):
                v.wait_ge(S("Y_out"), t + 1)
                y8 = ps[:, 2 * t].rearrange("p (h d) -> p h d", h=NH)
                do(N.tensor_reduce(stat[:, 0:8], y8, AX, ALU.add))
                do(ts(stat[:, 0:8], stat[:, 0:8], -1.0 / HD, None, ALU.mult))
                do(tt(yc, y8, bc(stat[:, 0:8], HD), ALU.add))
                do(tt(ysq, yc, yc, ALU.mult))
                do(N.tensor_reduce(stat_a[:, 0:8], ysq, AX, ALU.add), "var_ready")
                v.wait_ge(S("sd_ready"), t + 1)
                do(N.reciprocal(stat[:, 8:16], stat_a[:, 0:8]))
                do(tt(yc, yc, bc(stat[:, 8:16], HD), ALU.mult), "yn_ready")

            def gated(t):
                v.wait_ge(S("ynT_out"), t + 1)
                cols = slice(t * P, (t + 1) * P)
                for n in range(NPAIR):
                    do(ts(tmpT[:, n], ps[:, 2 * t + 1, n * P:(n + 1) * P], V("ln_w", n), V("ln_b", n), ALU.mult, ALU.add))
                do(tt(tmpT, tmpT, bonus[:, :, cols], ALU.add))
                do(tt(yaT[:, :, cols], tmpT, gT[:, :, cols], ALU.mult), "ya_out")

            keep_small_products(0)
            for l in range(1, LEVELS):
                double(0, l)
            keep_small_products(1)
            steps = [lambda: keep_inputs(0, 0), lambda: next_state(0, 0), lambda: keep_inputs(0, 1),
                     lambda: next_state(0, 1), lambda: None]
            for l in range(1, LEVELS):
                steps[l - 1]()
                double(1, l)
            normed(0)
            gated(0)
            for c in range(2):
                keep_inputs(1, c)
                next_state(1, c)
            normed(1)
            gated(1)

            do(N.memset(kz[0:HD, :, 1], 0.0), "kz_zeroed")
            do(N.memset(kz[HD:P, :, 0], 0.0), "kz_zeroed")
            v.wait_ge(S("ld_neg"), 16)

            def score(n):
                v.wait_ge(S("scores_out"), n + 1)
                if n >= 2:
                    v.wait_ge(S("PT_out"), 6 * (n - 1))
                for h in range(2):
                    for b in range(2):
                        i = 4 * n + 2 * h + b
                        base, w = (0, P) if b == 0 else (384, T)
                        for g in range(NG_ATT):
                            if b:
                                src = ps[:, g, h * T:(h + 1) * T]
                                bias = neg_sb[:, g, P:384]
                            else:
                                at = (g % 2) * T + h * P
                                src = ps[:, 3 + g // 2, at:at + P]
                                bias = neg_sb[:, g, 0:P]
                            do(stt(Ssb[:, n % 2, h, base + g * w:base + (g + 1) * w], bias, SLOPES[g * 8 + 2 * n + h], src,
                                   ALU.mult, ALU.add), "scores_read")
                        do(N.tensor_reduce(st_max[:, i:i + 1], Ssb[:, n % 2, h, base:base + 3 * w], AX, ALU.max, negate=True),
                           "max_ready")

            def normalise(n):
                for h in range(2):
                    for b in range(2):
                        i = 4 * n + 2 * h + b
                        sl = Ssb[:, n % 2, h, 0:384] if b == 0 else Ssb[:, n % 2, h, 384:1152]
                        v.wait_ge(S("exp_ready"), i + 1)
                        do(N.reciprocal(stat[:, 16 + i:17 + i], stat_a[:, i:i + 1]))
                        do(ts(sl, sl, stat[:, 16 + i:17 + i], None, ALU.mult), "probs_ready")

            score(0)
            normalise(0)
            for n in range(1, NPAIR):
                score(n)
                normalise(n)
            for j in range(4):
                v.wait_ge(S("unit_used"), 34 + j)
                v.wait_ge(S("proj_read"), 33)
                do(tt(ma, gates[:, j, 0], ps[:, 2 * (j % 2)], ALU.mult))
                do(tt(mb, gates[:, j, 1], ps[:, 2 * (j % 2) + 1], ALU.mult))
                do(tt(mT[:, 2 * j:2 * j + 2], ma.rearrange("p (c t) -> p c t", c=2), mb.rearrange("p (c t) -> p c t", c=2),
                      ALU.add), "merged")
            two = lambda b: ps[:, b:b + 2].rearrange("p b n -> p (b n)")
            v.wait_ge(S("unit_used"), 41)
            v.wait_ge(S("ld_x"), 16)
            for t in range(NT):
                do(tt(x1[:, t], two(4 + 2 * t), xt_sb[:, t], ALU.add), "x1_ready")
            v.wait_ge(S("ld_gmoe"), 16)
            for t in range(NT):
                v.wait_ge(S("rms_ready"), 2 + t)
                do(N.reciprocal(stat[:, t:t + 1], stat_a[:, t:t + 1]))
                do(stt(h2[:, t], x1[:, t], stat[:, t:t + 1], gmoe, ALU.mult, ALU.mult), "h2_ready")

            def first_max(dst, logits, keys, top, scratch):
                do(ts(scratch, logits, top, None, ALU.is_equal))
                do(tt(scratch, scratch, keys, ALU.mult))
                do(N.tensor_reduce(stat[:, 24:25], scratch, AX, ALU.max))
                do(ts(dst, scratch, stat[:, 24:25], None, ALU.is_equal))

            for t in range(NT):
                L = rt[:, t]
                m1, m2, nd, gw, w1, w2 = [stat[:, c + t:c + t + 1] for c in (26, 28, 20, 30, 32, 34)]
                gm = stat[:, 40:40 + EG]
                pen = stat[:, 44:44 + EG]
                other = comb[:, t]
                e32 = posm[:, t]
                v.wait_ge(S("logits_out"), t + 1)
                do(N.tensor_copy(L, ps[:, 4 + t, 0:36]))
                do(N.tensor_reduce(stat[:, 22:23], L[:, 0:EG], AX, ALU.max))
                do(ts(stat[:, 48:52], L[:, 0:EG], stat[:, 22:23], None, ALU.is_equal))
                do(tt(stat[:, 48:52], stat[:, 48:52], C("key_g"), ALU.mult))
                do(N.tensor_reduce(stat[:, 24:25], stat[:, 48:52], AX, ALU.max))
                do(ts(gm, stat[:, 48:52], stat[:, 24:25], None, ALU.is_equal))
                do(ts(pen, gm, 1.0, -FAR, ALU.subtract, ALU.mult))
                do(tt(L[:, EG:36].rearrange("p (g e) -> p g e", g=EG), L[:, EG:36].rearrange("p (g e) -> p g e", g=EG),
                      bc(pen, E // EG), ALU.add))
                do(ts(stat[:, 16 + t:17 + t], stat[:, 22:23], -1.0, None, ALU.mult), "route_max")
                ex = L[:, EG:36]
                do(N.tensor_reduce(m1, ex, AX, ALU.max))
                first_max(rmask[:, t], ex, C("key_e"), m1, e32)
                do(stt(ex, rmask[:, t], 3.0 * FAR, ex, ALU.mult, ALU.add))
                do(N.tensor_reduce(m2, ex, AX, ALU.max))
                first_max(other, ex, C("key_e"), m2, e32)
                do(tt(nd, m2, m1, ALU.subtract), "route_second")
                v.wait_ge(S("route_exp"), 2 * t + 2)
                do(N.reciprocal(gw, stat_a[:, 4 + t:5 + t]))
                do(ts(w1, stat_a[:, 6 + t:7 + t], 1.0, None, ALU.add))
                do(N.reciprocal(w1, w1))
                do(tt(w2, stat_a[:, 6 + t:7 + t], w1, ALU.mult))
                do(tt(w1, w1, gw, ALU.mult))
                do(tt(w2, w2, gw, ALU.mult))
                do(ts(e32, other, w2, None, ALU.mult))
                do(tt(ex, rmask[:, t], other, ALU.add))
                do(stt(other, rmask[:, t], w1, e32, ALU.mult, ALU.add))
                do(N.tensor_copy(rmask[:, t], ex), "mask_ready")
            v.wait_ge(S("pos_out"), 1)
            for t in range(NT):
                do(ts(posm[:, t], rmask[:, t], -4096.0, 4096.0, ALU.mult, ALU.add))
                do(tt(posm[:, t], posm[:, t], ps[:, 6, t * E:(t + 1) * E], ALU.add))
            do(N.tensor_reduce(stat[:, 0:1], ps[:, 6, 2 * E:3 * E], AX, ALU.max))
            do(ts(stat[:, 48:48 + NPASS], C("full"), stat[:, 0:1], None, ALU.is_lt))
            do(N.tensor_reduce(stat[:, 1:2], stat[:, 48:48 + NPASS], AX, ALU.add))
            do(N.tensor_copy(npass_i[0:1, 0:1], stat[0:1, 1:2]), "passes_ready")
            passes = v.value_load(npass_i[0:1, 0:1], min_val=1, max_val=NPASS)
            e4 = lambda x: x.rearrange("p (e s) -> p e s", s=SLOTS)
            with v.Fori(0, passes) as b:
                v.wait_ge(S("batch_done"), NBATCH * b + 1)
                for t in range(NT):
                    tt(e4(sel[:, t]), C("slot")[:, bass.ds(SLOTS * b, SLOTS)].unsqueeze(1).broadcast_to([P, E, SLOTS]),
                       bc(posm[:, t], SLOTS), ALU.is_equal).then_inc(S("sel_ready"), 1)
                with v.Fori(0, NBATCH // 2) as i:
                    for q in range(2):
                        done = 2 * (b * (NBATCH // 2) + i) + q
                        if q == 0:
                            v.wait_ge(S("sel_ready"), 2 * b + 2)
                        for t in range(NT):
                            ins = tt(e4(selw[:, t]), e4(sel[:, t, bass.ds(i * 2 * P + q * P, P)]),
                                     bc(comb[:, t, bass.ds(i * 2 * BATCH + q * BATCH, BATCH)], SLOTS), ALU.mult)
                            ins.then_inc(S("selw_ready"), 1)
                        v.wait_ge(S("gath_out"), 2 * done + 2)
                        N.tensor_copy(hg[:, 4:8].rearrange("p k t -> p (k t)"), ps[:, 5]).then_inc(S("gath1_ready"), 1)
                        v.wait_ge(S("batch_done"), done + 1)
                        v.wait_ge(S("selwT_out"), done + 1)
                        N.tensor_copy(selwT.rearrange("p a t -> p (a t)"), ps[:, 7, 0:T]).then_inc(S("selwT_ready"), 1)
                        v.wait_ge(S("silu_ready"), done + 1)
                        tt(act, silu, ps[:, 6, F:2 * F], ALU.mult).then_inc(S("act_ready"), 1)
                        v.wait_ge(S("dn_out"), 2 * done + 2)
                        N.tensor_copy(ysb[:, 512:1024], ps[:, 5]).then_inc(S("ysb1_ready"), 1)
            v.wait_ge(S("moe_done"), 1)
            for t in range(NT):
                do(tt(x1[:, t], x1[:, t], two(2 * t), ALU.add), "x2_ready")
            v.wait_ge(S("ld_gple"), 16)
            for t in range(NT):
                v.wait_ge(S("rms_ready"), 4 + t)
                do(N.reciprocal(stat[:, 8 + t:9 + t], stat_a[:, 8 + t:9 + t]))
                do(stt(h3[:, t], x1[:, t], stat[:, 8 + t:9 + t], gple, ALU.mult, ALU.mult), "h3_ready")
            for t in range(NT):
                v.wait_ge(S("gate_ready"), t + 1)
                do(tt(gate[:, t], gate[:, t], two(4 + 2 * t), ALU.mult))
                do(tt(x1[:, t], x1[:, t], gate[:, t], ALU.add), "x3_ready")
            v.wait_ge(S("ld_gfin"), 16)
            for t in range(NT):
                v.wait_ge(S("rms_ready"), 6 + t)
                do(N.reciprocal(stat[:, 10 + t:11 + t], stat_a[:, 10 + t:11 + t]))
                do(stt(x1[:, t], x1[:, t], stat[:, 10 + t:11 + t], gfin, ALU.mult, ALU.mult), "out_ready")


def _constants(np):
    f = np.float32
    i = np.arange(P)
    c = np.zeros((P, N_CRW), f)

    def put(name, a):
        at, n = CST[name]
        c[:, at:at + n] = a

    s, t = i[:, None], i[None, :]
    same = (s // CH) == (t // CH)
    put("ident", np.eye(P))
    put("ones", 1.0)
    put("before", s < t)
    put("slot", np.arange(T))
    put("key_g", np.arange(EG, 0, -1))
    put("key_e", np.arange(E, 0, -1))
    put("full", np.arange(NPASS) * SLOTS)
    put("eps", np.array([EPS, GN_EPS, 1e-12, 0.0]))
    put("block", (s // HD) == (t // HD))
    put("causal", np.concatenate([(s < t) & same] * 2 + [(s <= t) & same] * 2, 1))
    lev = [((s // (2 * b)) == (t // (2 * b))) & ((s // b) % 2 == 1) & ((t // b) % 2 == 0) for b in (2 ** l for l in range(LEVELS))]
    put("level", np.concatenate(lev, 1))
    put("level0T", lev[0].T)
    put("reset", np.tile((np.arange(T) % CH != 0), NPAIR))
    neg = np.zeros((P, NG_ATT, 384), f)
    for g, (window, d) in enumerate(((128, 1), (512, 4), (2048, 16))):
        for b in range(2):
            keys = np.arange(P * (b + 1))
            dist = (b * P + i)[:, None] - keys[None, :]
            ok = (dist >= 0) & (dist % d == 0) & (dist <= window)
            neg[:, g, (0 if b == 0 else P):(P if b == 0 else 384)] = np.where(ok, -dist, FAR)
    return c[:, :N_CST].copy(), c[:, N_CST:].copy(), neg


def kernel(**inp):
    import numpy as np
    import concourse.bacc as bacc
    from concourse.bass_utils import run_bass_kernel_spmd as run

    w = {k: np.asarray(v) for k, v in inp.items()}
    con = np.ascontiguousarray

    def kp(a):
        return con(a.reshape(-1, P, a.shape[-1]).transpose(1, 0, 2))

    def col(a):
        return a.reshape(-1, P).T

    x = w["x"][0]
    win = w["w_in"][0]
    RC = 3 * RW + 256
    AC = 3 * NG_ATT * RW
    units = []

    def cols(at, n):
        for c in range(0, n, T):
            units.append(kp(win[:, at + c:at + c + T]).reshape(P, UNIT))

    cols(3 * RW, 256)
    cols(RW, RW)
    cols(0, RW)
    cols(2 * RW, RW)
    cols(RC, AC)
    pa, pb = w["w_proj_a"][0], w["w_proj_b"][0]
    for m in range(4):
        cols(RC + AC + m * T, T)
        cols(RC + AC + D + m * T, T)
    for m in range(4):
        units.append(np.concatenate([kp(pa[:, m * T:(m + 1) * T]).reshape(P, -1), kp(pb[:, m * T:(m + 1) * T]).reshape(P, -1)], 1))
    wo = kp(w["w_out"][0])
    for u in range(4):
        units.append(wo[:, 2 * u:2 * u + 2].reshape(P, UNIT))
    mu = w["rwkv_mu"][0]
    mu = np.concatenate([mu[3 * RW:], mu[RW:2 * RW], mu[:RW], mu[2 * RW:3 * RW]])
    cvec = np.concatenate([col(w["norm_mix"][0]), col(mu)] + [col(w[n][0].reshape(-1)) for n in (
        "rwkv_w0", "rwkv_a0", "rwkv_k_k", "rwkv_k_a", "rwkv_r_k", "rwkv_ln_w", "rwkv_ln_b")], 1)
    lora = np.zeros((P, 2, RW), np.float32)
    lora[:64, 0] = w["rwkv_w2"][0]
    lora[64:, 1] = w["rwkv_a2"][0]
    gains = np.stack([np.broadcast_to(g, (P, D)) for g in (w["norm_moe"][0], w["norm_ple"][0], w["norm_final"])])
    wr = np.concatenate([w["w_router_group"][0], w["w_router_expert"][0].transpose(1, 0, 2).reshape(D, E)], 1)
    gu = np.concatenate([w["w_exp_gate"][0], w["w_exp_up"][0]], -1).reshape(E, KD, P, 2 * F).transpose(0, 2, 1, 3)
    dn = w["w_exp_down"][0].reshape(E, F // P, P, D).transpose(0, 2, 1, 3)
    cst, crw, neg = _constants(np)
    arrays = {
        "xT": kp(x.T), "xtok": kp(x), "pT": kp(w["p"][0, 0].T), "cst": cst, "crw": crw, "neg": neg, "cvec": cvec,
        "lora": lora, "g2": w["rwkv_g2"][0], "stream": np.stack(units), "gain3": gains, "router": kp(wr),
        "wgu": gu, "wd": dn, "wpg": kp(w["w_ple_gate"][0]), "wpp": kp(w["w_ple_proj"][0]),
    }
    nc = bacc.Bacc("TRN2", target_bir_lowering=False, num_devices=1)
    args = []
    for name, a in arrays.items():
        arrays[name] = con(a)
        args.append(nc.dram_tensor(name, a.shape, F32, kind="ExternalInput").ap())
    o = nc.dram_tensor("out", (1, T, D), F32, kind="ExternalOutput").ap()
    program(nc, *args, o)
    r = run(nc, [arrays], core_ids=[0])
    return r.results[0]["out"]
```

```python
import concourse.bass as bass
from concourse import mybir
from contextlib import ExitStack

F32 = mybir.dt.float32
F32R = mybir.dt.float32r
I32 = mybir.dt.int32
ACT = mybir.ActivationFunctionType
ALU = mybir.AluOpType
AX = mybir.AxisListType.X

P = 128
D = 1024
T = 256
KD = D // P
NT = T // P
RW = 512
NPAIR = RW // P
HD = 64
W_LORA = 64
NH = 8
CH = 64
NG_ATT = 3
E = 32
EG = 4
F = 256
SLOTS = 32
BATCH = P // SLOTS
NBATCH = E // BATCH
NPASS = T // SLOTS
UNIT = 2048
RING = 3
SMALL = 320
XPARTS = 4
WPG_PIECES = 4
LEVELS = 6
Q_UNIT, K_UNIT, V_UNIT, GATE_UNIT, MERGE_UNIT, OUT_UNIT, UNITS = 7, 13, 19, 25, 33, 37, 41
DECAY = 0.6065306597126334
EPS = 1e-6
GN_EPS = 64e-5
FAR = -1.0e30

CST = {}
CVEC = {}


def _columns(table, spec, at=0):
    for name, n in spec:
        table[name] = (at, n)
        at += n
    return at


N_CST = _columns(CST, [("ident", P), ("ones", P), ("before", P), ("slot", T), ("key_g", EG), ("key_e", E),
                       ("full", NPASS), ("eps", 4)])
N_CRW = _columns(CST, [("block", P), ("causal", 4 * P), ("level", LEVELS * P), ("level0T", P), ("reset", NPAIR * T)], N_CST)
N_CVEC = _columns(CVEC, [("norm_mix", KD), ("mu", 14), ("w0", NPAIR), ("a0", NPAIR), ("k_k", NPAIR), ("k_a", NPAIR),
                         ("r_k", NPAIR), ("ln_w", NPAIR), ("ln_b", NPAIR)])
SLOPES = [2.0 ** (-8.0 * (i + 1) / 24) for i in range(24)]


def program(nc, xT, xtok, pT, cst, crw, neg, cvec, lora, g2, stream, gain3, router, wgu, wd, wpg, wpp, out):
    ctx = ExitStack()
    with ctx:
        def sem(name):
            return ctx.enter_context(nc.semaphore(name))

        COLS = 53000
        GU0, GU1, DN, HIGH = 0, 16384, 32768, 40960
        with ExitStack() as early:
            part = lambda name: early.enter_context(nc.sbuf_tensor(name, [P, UNIT], F32R))
            parts = [part(f"part{i}") for i in range(2 + 2 * RING)]
            mixed_parts = [part(f"mixed_part{i}") for i in range(2)]
            y_parts = [part(f"y_part{i}") for i in range(2)]
            h3_parts = [part(f"h3_part{i}") for i in range(2)]
            early.enter_context(nc.sbuf_tensor("skipped", [P, 2 * UNIT], F32))
            late_parts = [part(f"late_part{i}") for i in range(4)]
            early.enter_context(nc.sbuf_tensor("skipped_too", [P, N_CST + N_CVEC + SMALL + NT * D], F32))
            last_parts = [part(f"last_part{i}") for i in range(4)]
        with ExitStack() as early:
            at = DN + 4 * UNIT + N_CST + N_CVEC + SMALL + 2 * NT * D + N_CRW - N_CST
            early.enter_context(nc.sbuf_tensor("skipped_for_q", [P, at], F32))
            q_low_part = early.enter_context(nc.sbuf_tensor("q_low_part", [P, UNIT], F32R))
        mem = ctx.enter_context(nc.sbuf_tensor("mem", [P, COLS], F32))
        npass_i = ctx.enter_context(nc.sbuf_tensor("npass_i", [1, 1], I32))
        ps = ctx.enter_context(nc.psum_tensor("ps", [P, 8, 512], F32))

        def region(lo, hi):
            at = [lo]

            def take(*dims):
                n = 1
                for d in dims:
                    n *= d
                v = mem[:, at[0]:at[0] + n]
                at[0] += n
                assert at[0] <= hi, (at[0], hi)
                names = "abcd"[:len(dims)]
                if len(dims) > 1:
                    v = v.rearrange(f"p ({' '.join(names)}) -> p {' '.join(names)}",
                                    **{m: d for m, d in zip(names[1:], dims[1:])})
                return v
            return take

        take = region(GU0, DN)
        gu_w = [[take(KD, 2 * F) for _ in range(BATCH)] for _ in range(2)]
        take = region(DN, HIGH)
        dn_w = [take(F // P, D) for _ in range(BATCH)]
        ring_at = DN - RING * UNIT
        ring = [mem[:, ring_at + i * UNIT:ring_at + (i + 1) * UNIT] for i in range(RING)]

        take = region(HIGH, COLS)
        c_all = take(N_CST)
        cv = take(N_CVEC)
        small = take(SMALL)
        high_pre = HIGH + N_CST + N_CVEC + SMALL
        x1 = take(NT, D)
        h2 = take(NT, D)
        sel = take(NT, E * SLOTS)
        hg = take(KD, P)
        selw = take(NT, P)
        silu = take(F)
        act = take(F)
        actT = take(F // P, P)
        ysb = take(D)
        selwT = take(NT, P)
        zero = take(P)
        gple = take(D)
        take = region(HIGH + N_CST + N_CVEC, high_pre)
        rmask = take(NT, E)
        comb = take(NT, E)
        posm = take(NT, E)
        stat = take(64)
        stat_a = take(32)
        st_max = stat[:, 0:16]

        take = region(high_pre, COLS)
        hT = take(KD, T)
        yaT = take(NPAIR, T)
        ybT = take(NPAIR, T)
        crw_sb = take(N_CRW - N_CST)
        lora_sb = take(2, RW)
        g2_sb = take(RW)
        lin = take(2, T)
        mats_more = [take(2, 512) for _ in range(2)]
        take = region(GU0, GU1)
        prep = take(8, NPAIR, T)
        rT, kT, aT_, kkT, swT, cumT, wexT, winvT = [prep[:, i] for i in range(8)]
        mats0 = prep[:, 0:4].rearrange("p s n t -> p (s n t)").rearrange("p (n b c) -> p n b c", n=NPAIR, b=2)
        M_sb, X_sb, Z_sb, T1_sb = [prep[:, 4 + i].rearrange("p n t -> p (n t)").rearrange("p (h t) -> p h t", h=NH)
                                   for i in range(4)]
        vT = take(NPAIR, T)
        gT = take(NPAIR, T)
        bonus = take(NPAIR, T)
        wincT = take(NPAIR, T)
        bT = take(NPAIR, T)
        kaT = take(NPAIR, T)
        rhoT = take(NPAIR, T)
        mats_more.append(take(2, 512))
        mats_more.append(vT.rearrange("p n t -> p (n t)").rearrange("p (b c) -> p b c", b=2))
        take = region(GU1, ring_at)
        arz = take(NPAIR, 2, 2, T)
        mlev = take(2, NH, P)
        alT = mlev[:, 0].rearrange("p h t -> p (h t)").rearrange("p (n t) -> p n t", n=NPAIR)
        tok = take(4, NT, RW)
        Atok, Btok, Ktok, Vtok = [tok[:, i] for i in range(4)]
        take = region(DN, HIGH)
        NV = take(RW)
        XNV2 = [take(RW) for _ in range(NT)]
        XAT2 = [take(NPAIR, P) for _ in range(NT)]
        U_sb = take(RW)
        Th = take(5, NPAIR, P)
        yc = take(NH, HD)
        ysq = take(NH, HD)
        shift = take(2, T + 1)
        tmpT = take(NPAIR, P)
        dlt = ysq.rearrange("p h d -> p (h d)").rearrange("p (c t) -> p c t", c=2)

        def mats(t, n, i):
            return mats0[:, n, i] if t == 0 else mats_more[n][:, i]

        part_kt = lambda i: parts[i].rearrange("p (k c) -> p k c", k=KD)
        hT_parts = [part_kt(0), part_kt(1)]
        w_parts = [[part_kt(2 + 2 * slot + i) for i in range(2)] for slot in range(RING)]
        mT_parts = [m.rearrange("p (k t) -> p k t", k=KD) for m in mixed_parts]
        yT_parts = [y.rearrange("p (b k t) -> p b k t", b=2, k=NPAIR) for y in y_parts]

        def unit_parts(n):
            at = 2 * ((n - MERGE_UNIT) % 2)
            if n < K_UNIT:
                return (parts[2][:, :], parts[3][:, :]) if (n - Q_UNIT) % 2 else (parts[6][:, :], q_low_part[:, :])
            if n < MERGE_UNIT + 2:
                slot = part_slot(n)
                return parts[2 + 2 * slot][:, :], parts[3 + 2 * slot][:, :]
            if n < UNITS - 2:
                return late_parts[at][:, :], late_parts[at + 1][:, :]
            return last_parts[at][:, :], last_parts[at + 1][:, :]

        def part_slot(n):
            return n % RING if n < GATE_UNIT + 2 else (n - GATE_UNIT) % 2

        def low_ready(n):
            if n < K_UNIT:
                return "pool_low", n - Q_UNIT + 1
            if n < GATE_UNIT + 2:
                return "w_low", n - K_UNIT + 1
            if n < OUT_UNIT:
                return "pool_low", K_UNIT - Q_UNIT + n - GATE_UNIT - 1
            return "w_low", GATE_UNIT + 2 - K_UNIT + n - OUT_UNIT + 1

        PRODUCTS = ((0, 0), (1, 0), (0, 1))

        take = region(GU0, ring_at)
        xT_sb = take(KD, T)
        sq = take(KD, T)
        rstd_bc = take(T)
        take = region(GU1, ring_at)
        qT = take(NG_ATT * NPAIR, T)
        kz = take(NG_ATT * NPAIR, 2, T)
        take = region(DN, HIGH)
        vtok = take(NT, NG_ATT * RW)
        Ssb = take(2, 2, NG_ATT * 384)
        take = region(high_pre + 4096, COLS)
        neg_sb = take(NG_ATT, 384)
        PT = take(2, 384)
        gates = take(4, 2, 2 * T)
        take = region(GU1, ring_at)
        take(2 * UNIT)
        h2T = take(KD, T)
        gmoe = take(D)
        wr = take(KD, 36)
        take = region(GU1 + 4 * UNIT, ring_at)
        xt_sb = take(NT, D)
        ma, mb = x1[:, 0, 0:512], x1[:, 0, 512:1024]
        rt = silu[:, 0:NT * 36].rearrange("p (t n) -> p t n", t=NT)
        take = region(GU0, GU1)
        wpg_sb = take(KD, D)
        wpp_sb = take(T // P, D)
        pT_sb = take(T // P, T)
        gfin = take(D)
        gate = take(NT, D)
        h3 = h2
        h3T_parts = [x.rearrange("p (k t) -> p k t", k=KD) for x in h3_parts]

        def wpg_parts(j):
            return [x.rearrange("p (k f) -> p k f", k=KD // WPG_PIECES)
                    for x in (mixed_parts, y_parts, late_parts[0:2], late_parts[2:4])[j]]

        def wpg_low(j):
            if j < 2:
                return "pool_low", low_ready(OUT_UNIT - 1)[1] + j + 1
            return "w_low", low_ready(UNITS - 1)[1] + j - 1

        def C(name):
            at, n = CST[name]
            return c_all[:, at:at + n] if at < N_CST else crw_sb[:, at - N_CST:at - N_CST + n]

        def V(name, i):
            at = CVEC[name][0] + i
            return cv[:, at:at + 1]

        ident = C("ident")

        sems = {}

        def S(name):
            if name not in sems:
                sems[name] = ctx.enter_context(nc.semaphore("s_" + name))
            return sems[name]

        GATE_MMS = 2 * KD * len(PRODUCTS)

        gate_ends = [6 * NPAIR * (u + 1) // (MERGE_UNIT - GATE_UNIT - 1) for u in range(MERGE_UNIT - GATE_UNIT - 1)]

        def gates_due(i):
            u = sum(e <= i for e in gate_ends)
            first = gate_ends[u - 1] if u else 0
            return GATE_MMS * (u + 1) + GATE_MMS * (i + 1 - first) // (gate_ends[u] - first)

        class Chain:

            def __init__(self, eng, own):
                self.eng, self.own, self.n = eng, own, {}

            def __call__(self, ins, signal=None):
                name = signal or self.own
                self.n[name] = self.n.get(name, 0) + 1
                ins.then_inc(S(name), 1)
                self.eng.wait_ge(S(name), self.n[name])

        block = ctx.enter_context(nc.Block())
        W0 = N_CRW - N_CST

        @block.sync
        def _(sp):
            for j in range(XPARTS):
                ks = slice(j * KD // XPARTS, (j + 1) * KD // XPARTS)
                sp.dma_start(xT_sb[:, ks], xT[:, ks]).then_inc(S(f"ld_xT{j}"), 16)
                if j == 0:
                    sp.dma_start(c_all, cst).then_inc(S("ld_cst"), 16)
            sp.dma_start(cv, cvec).then_inc(S("ld_cvec"), 16)

            def unit(n, slot, first=False):
                if not isinstance(n, int):
                    sp.wait_ge(S("w_low"), n - RING - K_UNIT + 1)
                elif n - RING >= Q_UNIT:
                    name, value = low_ready(n - RING)
                    sp.wait_ge(S(name), value)
                elif not first:
                    sp.wait_ge(S("unit_used"), n - RING + 1)
                sp.dma_start(ring[slot], stream[bass.ds(n, 1)].rearrange("a p n -> p (a n)")).then_inc(
                    S(f"unit_landed{slot}"), 16)

            for n in range(RING):
                unit(n, n, first=True)
            sp.dma_start(crw_sb, crw).then_inc(S("ld_crw"), 16)
            sp.dma_start(lora_sb, lora).then_inc(S("ld_lora"), 16)
            sp.dma_start(g2_sb, g2).then_inc(S("ld_lora"), 16)
            for n in range(RING, 13):
                unit(n, n % RING)

            def load_gate_up(trip, i, q, fresh, experts=range(BATCH), halves=range(2)):
                for kh, e in [(kh, e) for kh in halves for e in experts]:
                    which = i * (2 * BATCH) + q * BATCH + e
                    ks = slice(kh * KD // 2, (kh + 1) * KD // 2)
                    if not fresh and e == 0:
                        sp.wait_ge(S("gu_used" if kh else "gu_half_used"), 2 * trip + q)
                    sp.dma_start(gu_w[q][e][:, ks], wgu[bass.ds(which, 1)].rearrange("a p k f -> p (a k) f")[:, ks]).then_inc(
                        S(f"gu_landed{q}{kh}"), 16)

            def load_down(trip, i, q, fresh, experts=range(BATCH)):
                for e in experts:
                    which = i * (2 * BATCH) + q * BATCH + e
                    if not fresh and e == 0:
                        sp.wait_ge(S("dn_out"), 2 * (2 * trip + q))
                    sp.dma_start(dn_w[e], wd[bass.ds(which, 1)].rearrange("a p k f -> p (a k) f")).then_inc(
                        S(f"dn_landed{e}"), 16)

            def load(trip, i, q, fresh):
                load_gate_up(trip, i, q, fresh)
                load_down(trip, i, q, fresh)

            for n in range(K_UNIT, K_UNIT + RING):
                unit(n, n % RING)
            with sp.Fori(1, 4) as i:
                for j in range(RING):
                    unit(K_UNIT + RING * i + j, (K_UNIT + j) % RING)
            sp.wait_ge(S("ya_out"), NT)
            sp.dma_start(neg_sb, neg).then_inc(S("ld_neg"), 16)
            for n in range(GATE_UNIT, MERGE_UNIT + RING):
                if n == GATE_UNIT + 6:
                    sp.wait_ge(S("unit_used"), GATE_UNIT + 2)
                    load_gate_up(0, 0, 0, True, (3,))
                if n == GATE_UNIT + 9:
                    sp.wait_ge(S("scores_out"), NPAIR)
                    sp.dma_start(xt_sb, xtok).then_inc(S("ld_x"), 16)
                unit(n, n % RING)
            unit(36, 36 % RING)
            sp.wait_ge(S("unit_used"), MERGE_UNIT)
            load_gate_up(0, 0, 0, True, (0,))
            unit(37, 37 % RING)
            sp.wait_ge(S("unit_used"), MERGE_UNIT + 1)
            load_gate_up(0, 0, 0, True, (1,))
            unit(38, 38 % RING)
            sp.wait_ge(S("unit_used"), MERGE_UNIT + 2)
            unit(39, 39 % RING)
            load_gate_up(0, 0, 0, True, (2,))
            sp.wait_ge(S("unit_used"), OUT_UNIT)
            unit(40, 40 % RING)
            sp.dma_start(gmoe, gain3[0]).then_inc(S("ld_gmoe"), 16)
            sp.dma_start(wr, router).then_inc(S("ld_wr"), 16)
            sp.wait_ge(S("unit_used"), UNITS - 3)
            load_down(0, 0, 0, True, (0, 1))
            sp.wait_ge(S("unit_used"), UNITS - 2)
            load_down(0, 0, 0, True, (2, 3))
            name, value = low_ready(UNITS - 1)
            sp.wait_ge(S(name), value)
            load_gate_up(0, 0, 1, True, (3,))
            sp.wait_ge(S("unit_used"), UNITS)
            load_gate_up(0, 0, 1, True, (0,))
            sp.wait_ge(S("x1_ready"), NT)
            load_gate_up(0, 0, 1, True, (2,))
            sp.wait_ge(S("logits_out"), 1)
            sp.dma_start(gple, gain3[1]).then_inc(S("ld_gple"), 16)
            load_gate_up(0, 0, 1, True, (1,))
            load_gate_up(1, 1, 0, False, halves=(0,))
            load_down(0, 0, 1, False)
            load_gate_up(1, 1, 0, False, halves=(1,))
            load_down(1, 1, 0, False)
            load(1, 1, 1, False)
            with sp.Fori(2, NBATCH // 2) as i:
                load(i, i, 0, False)
                load(i, i, 1, False)
            passes = sp.value_load(npass_i[0:1, 0:1], min_val=1, max_val=NPASS)
            with sp.If(passes > 1):
                with sp.Fori(1, passes) as b:
                    with sp.Fori(0, NBATCH // 2) as i:
                        load(b * (NBATCH // 2) + i, i, 0, False)
                        load(b * (NBATCH // 2) + i, i, 1, False)
            sp.wait_ge(S("gu_used"), passes * NBATCH)
            sp.dma_start(wpp_sb, wpp).then_inc(S("ld_wpp"), 16)
            sp.dma_start(pT_sb, pT).then_inc(S("ld_pT"), 16)
            for j in range(WPG_PIECES):
                ks = slice(j * KD // WPG_PIECES, (j + 1) * KD // WPG_PIECES)
                sp.dma_start(wpg_sb[:, ks], wpg[:, ks]).then_inc(S(f"ld_wpg{j}"), 16)
            sp.dma_start(gfin, gain3[2]).then_inc(S("ld_gfin"), 16)
            for t in range(NT):
                for hf in range(2):
                    cols = slice(hf * 512, (hf + 1) * 512)
                    sp.wait_ge(S("out_ready"), 2 * t + hf + 1)
                    sp.dma_start(out[0, t * P:(t + 1) * P, cols], x1[:, t, cols]).then_inc(S("out_stored"), 16)
            sp.wait_ge(S("out_stored"), 16 * 2 * NT)

        @block.tensor
        def _(pe):
            mm = nc.tensor.matmul

            def tr(o, i):
                return nc.tensor.transpose(o, i, ident)

            pe.wait_ge(S("ld_cst"), 16)
            for k in range(KD):
                if k % (KD // XPARTS) == 0:
                    pe.wait_ge(S("sq_ready"), k // (KD // XPARTS) + 1)
                m = mm(ps[:, 7, 0:T], C("ones"), sq[:, k], start=k == 0, stop=k == KD - 1)
            m.then_inc(S("ssq_done"), 1)

            def landed(n, slot):
                pe.wait_ge(S(f"unit_landed{slot}"), 16 * (n // RING) + 16)

            def half(n, c, bank, w_slot=None, first=False):
                w = ring[n % RING if w_slot is None else w_slot].rearrange("p (k c) -> p k c", k=KD)
                for k in range(KD):
                    if first and c == 0:
                        pe.wait_ge(S("hT_ready"), k + 1)
                    m = mm(ps[:, bank, c * T:(c + 1) * T], w[:, k, c * P:(c + 1) * P], hT[:, k],
                           start=k == 0, stop=k == KD - 1)
                if c:
                    m.then_inc(S("unit_used"), 1)

            def project(n):
                landed(n, n % RING)
                if n >= RING:
                    pe.wait_ge(S("proj_read"), n - RING + 1)
                for c in range(2):
                    half(n, c, n % RING, first=n == 0)

            def headsum(src, bank):
                for c in range(2):
                    m = mm(ps[:, bank + c], C("block"), src[:, 2 * c:2 * c + 2].rearrange("p n t -> p (n t)"),
                           start=True, stop=True)
                m.then_inc(S("headsum"), 1)

            project(0)
            project(1)
            pe.wait_ge(S("ld_lora"), 32)
            pe.wait_ge(S("lora_in"), 2)
            for kind in range(3):
                if kind == 2:
                    pe.wait_ge(S("lora_read"), 1)
                for c in range(NPAIR):
                    w = g2_sb if kind == 2 else lora_sb[:, kind]
                    m = mm(ps[:, (3, 5, 3)[kind] + c // 2, (c % 2) * T:(c % 2 + 1) * T], w[:, c * P:(c + 1) * P],
                           lin[:, 1] if kind == 2 else lin[:, 0], start=True, stop=True)
                m.then_inc(S("lora_out"), 1)
            project(2)
            project(3)
            project(4)
            pe.wait_ge(S("ld_crw"), 16)
            pe.wait_ge(S("kksq_ready"), 1)
            pe.wait_ge(S("lora_read"), 2)
            headsum(bT, 5)
            project(5)
            pe.wait_ge(S("rk_ready"), 1)
            pe.wait_ge(S("lora_read"), 3)
            headsum(rhoT, 3)
            project(6)

            for i, (src, ready) in enumerate(((bT, "b_ready"), (kaT, "ka_ready"), (alT, "al_ready"), (vT, "z_ready"))):
                pe.wait_ge(S(ready), 7 if i == 3 else 1)
                for t in range(NT):
                    j = NT * i + t
                    if j == 1:
                        pe.wait_ge(S("proj_read"), 7)
                    if j == 3:
                        pe.wait_ge(S("kknorm"), 1)
                    if j >= 4:
                        pe.wait_ge(S("tok_read"), j - 3)
                    for c in range(NPAIR):
                        m = tr(ps[:, (7, 0, 1, 6)[j % 4], c * P:(c + 1) * P], src[:, c, t * P:(t + 1) * P])
                    m.then_inc(S("tok_out"), 1)

            pe.wait_ge(S("arz_pool"), 1)
            pe.wait_ge(S("arz_act"), 3)

            def small_products(t):
                tt = slice(t * P, (t + 1) * P)
                if t == 0:
                    pe.wait_ge(S("headsum_read"), 2)
                else:
                    pe.wait_ge(S("XAT_ready"), t)
                    pe.wait_ge(S("XNV_ready"), t)
                for n in range(NPAIR):
                    for i, src in enumerate((bT, kaT)):
                        if n >= 2:
                            pe.wait_ge(S("mats_read"), 8 * t + 2 * (n - 2) + i + 1)
                        mm(ps[:, 2 + 2 * (n % 2) + i].rearrange("p (a t) -> p a t", a=4), src[:, n, tt],
                           arz[:, n].rearrange("p a b t -> p (a b) t")[:, :, tt], start=True, stop=True)\
                            .then_inc(S("mats_out"), 1)
                    if n >= 2:
                        g = n - 2
                        pe.wait_ge(S("mats_read"), 8 * t + 4 * g + 4)
                        pe.wait_ge(S("tok_read"), 8)
                        for h in range(4):
                            m = tr(ps[:, 6 + g, h * P:(h + 1) * P], mats(t, 2 * g + h // 2, 0)[:, (h % 2) * P:(h % 2 + 1) * P])
                        m.then_inc(S("M_out"), 1)

            def inverse_first(t, l):
                for g in range(2):
                    pe.wait_ge(S("mlev_ready"), (LEVELS - 1) * 2 * t + 2 * (l - 1) + g + 1)
                    pe.wait_ge(S("Z_ready"), LEVELS * 2 * t + 2 * (l - 1) + g + 1)
                    if l == 1:
                        pe.wait_ge(S("mats_read"), 8 * t + 8)
                    for h in range(4 * g, 4 * g + 4):
                        m = mm(ps[:, 2 + g, (h % 4) * P:(h % 4 + 1) * P], mlev[:, l % 2, h], Z_sb[:, h], start=True, stop=True)
                    m.then_inc(S("T1_out"), 1)

            def inverse_second(t, l):
                for g in range(2):
                    pe.wait_ge(S("T1_ready"), (LEVELS - 1) * 2 * t + 2 * (l - 1) + g + 1)
                    pe.wait_ge(S("X_ready"), (LEVELS - 1) * 2 * t + 2 * (l - 1) + g + 1)
                    for h in range(4 * g, 4 * g + 4):
                        m = mm(ps[:, 4 + g, (h % 4) * P:(h % 4 + 1) * P], X_sb[:, h], T1_sb[:, h], start=True, stop=True)
                    m.then_inc(S("D_out"), 1)
                    if l < LEVELS - 1:
                        for h in range(4 * g, 4 * g + 4):
                            m = mm(ps[:, 6 + g, (h % 4) * P:(h % 4 + 1) * P], T1_sb[:, h], X_sb[:, h], start=True, stop=True)
                        m.then_inc(S("DT_out"), 1)

            def apply_inverse(t, between=lambda: None):
                pe.wait_ge(S("Z_ready"), LEVELS * 2 * (t + 1))
                for h in range(NH):
                    m = mm(ps[:, 2, h * HD:(h + 1) * HD], mats(t, h // 2, 1)[:, (h % 2) * P:(h % 2 + 1) * P],
                           Vtok[:, t, h * HD:(h + 1) * HD], start=True, stop=True)
                m.then_inc(S("NV_out"), 1)
                for h in range(NH):
                    m = mm(ps[(h % 2) * HD:(h % 2 + 1) * HD, 3, (h // 2) * P:(h // 2 + 1) * P],
                           Atok[:, t, h * HD:(h + 1) * HD], Z_sb[:, h], start=True, stop=True)
                m.then_inc(S("XAT_out"), 1)
                between()
                pe.wait_ge(S("NV_ready"), t + 1)
                for h in range(NH):
                    m = mm(ps[:, 4, h * HD:(h + 1) * HD], Z_sb[:, h], NV[:, h * HD:(h + 1) * HD], start=True, stop=True)
                m.then_inc(S("XNV_out"), 1)

            def chain_bank(t):
                return 0 if t == 0 else 2

            def chunk_inputs(t, c):
                cc, rows = 2 * t + c, slice(c * CH, (c + 1) * CH)
                pe.wait_ge(S("XAT_ready"), t + 1)
                pe.wait_ge(S("state_ready"), 1 + cc)
                for n in range(NPAIR):
                    m = mm(ps[rows, chain_bank(t), n * P:(n + 1) * P], XAT2[t][:, n, rows], Th[:, cc, n], start=True, stop=True)
                m.then_inc(S("U_out"), 1)

            def chunk_state(t, c):
                cc, rows = 2 * t + c, slice(c * CH, (c + 1) * CH)
                pe.wait_ge(S("U_ready"), cc + 1)
                for n in range(NPAIR):
                    o = ps[:, chain_bank(t) + 1, n * P:(n + 1) * P]
                    mm(o, Ktok[rows, t, n * P:(n + 1) * P], Vtok[rows, t, n * P:(n + 1) * P], start=True, stop=False)
                    m = mm(o, Btok[rows, t, n * P:(n + 1) * P], U_sb[rows, n * P:(n + 1) * P], start=False, stop=True)
                m.then_inc(S("dT_out"), 1)

            def tile_outputs(t):
                bank = chain_bank(t)
                for c in range(2):
                    rows = slice(c * CH, (c + 1) * CH)
                    for n in range(NPAIR):
                        mm(ps[rows, bank, n * P:(n + 1) * P], rhoT[:, n, t * P + c * CH:t * P + (c + 1) * CH],
                           Th[:, 2 * t + c, n], start=n == 0, stop=False, skip_group_check=True)
                for h in range(NH):
                    cols = slice(h * HD, (h + 1) * HD)
                    hh = slice(2 * P + (h % 2) * P, 2 * P + (h % 2 + 1) * P)
                    mm(ps[:, bank, cols], mats(t, h // 2, 0)[:, hh], U_sb[:, cols], start=False, stop=False, skip_group_check=True)
                    m = mm(ps[:, bank, cols], mats(t, h // 2, 1)[:, hh], Vtok[:, t, cols], start=False,
                           stop=h == NH - 1, skip_group_check=True)
                m.then_inc(S("Y_out"), 1)

            def turn_outputs(t):
                pe.wait_ge(S("yn_ready"), t + 1)
                for n in range(NPAIR):
                    m = tr(ps[:, chain_bank(t) + 1, n * P:(n + 1) * P], yc[:, 2 * n:2 * n + 2].rearrange("p h d -> p (h d)"))
                m.then_inc(S("ynT_out"), 1)

            small_products(0)
            for l in range(1, LEVELS):
                inverse_first(0, l)
                inverse_second(0, l)
            apply_inverse(0)
            small_products(1)
            steps = [lambda: chunk_inputs(0, 0), lambda: chunk_state(0, 0), lambda: chunk_inputs(0, 1),
                     lambda: chunk_state(0, 1), lambda: tile_outputs(0)]
            for l in range(1, LEVELS):
                inverse_first(1, l)
                steps[l - 1]()
                inverse_second(1, l)
            def q_half(i):
                n, c = Q_UNIT + i // 2, i % 2
                if c == 0:
                    name, value = low_ready(n)
                    pe.wait_ge(S(name), value)
                    pe.wait_ge(S("hT_low"), 1)
                    if n >= Q_UNIT + 2:
                        pe.wait_ge(S("proj_read"), n - 1)
                w = [x.rearrange("p (k c) -> p k c", k=KD) for x in unit_parts(n)]
                for k in range(KD):
                    for wp, hp in PRODUCTS:
                        m = mm(ps[:, 6 + n % 2, c * T:(c + 1) * T], w[wp][:, k, c * P:(c + 1) * P], hT_parts[hp][:, k],
                               start=k + wp + hp == 0, stop=k == KD - 1 and hp == 1)
                if c:
                    m.then_inc(S("unit_used"), 1)

            apply_inverse(1)
            turn_outputs(0)
            chunk_inputs_steps = [lambda: chunk_inputs(1, 0), lambda: chunk_state(1, 0), lambda: chunk_inputs(1, 1),
                                  lambda: chunk_state(1, 1), lambda: tile_outputs(1)]
            for i, step in enumerate(chunk_inputs_steps):
                step()
                q_half(i)
            for i in range(5, 8):
                q_half(i)
            turn_outputs(1)
            for i in range(8, 12):
                q_half(i)

            pe.wait_ge(S("ya_out"), NT)
            with pe.Fori(0, 2) as i:
                for j in range(RING):
                    n, slot = K_UNIT + RING * i + j, (K_UNIT + j) % RING
                    pe.wait_ge(S("w_low"), RING * i + j + 1)
                    pe.wait_ge(S("proj_read"), n - RING + 1)
                    for c in range(2):
                        for k in range(KD):
                            for wp, hp in PRODUCTS:
                                m = mm(ps[:, slot, c * T:(c + 1) * T], w_parts[slot][wp][:, k, c * P:(c + 1) * P],
                                       hT_parts[hp][:, k], start=k + wp + hp == 0, stop=k == KD - 1 and hp == 1)
                    m.then_inc(S("unit_used"), 1)
            with pe.Fori(0, 2) as i:
                for j in range(RING):
                    n, slot = V_UNIT + RING * i + j, (V_UNIT + j) % RING
                    pe.wait_ge(S("w_low"), V_UNIT - K_UNIT + RING * i + j + 1)
                    pe.wait_ge(S("proj_read"), n - RING + 1)
                    for t in range(NT):
                        for k in range(KD):
                            for wp, hp in PRODUCTS:
                                m = mm(ps[:, slot, t * T:(t + 1) * T], hT_parts[hp][:, k, t * P:(t + 1) * P],
                                       w_parts[slot][wp][:, k], start=k + wp + hp == 0, stop=k == KD - 1 and hp == 1)
                    m.then_inc(S("unit_used"), 1)

            def scores(n):
                if n == 0:
                    pe.wait_ge(S("proj_read"), 25)
                else:
                    pe.wait_ge(S("scores_read"), 12 * n)
                for g in range(NG_ATT):
                    c = g * NPAIR + n
                    m = mm(ps[:, g].rearrange("p (h t) -> p h t", h=2), qT[:, c, P:T], kz[:, c], start=True, stop=True)
                    m = mm(ps[:, 3 + g // 2, (g % 2) * T:(g % 2 + 1) * T].rearrange("p (h t) -> p h t", h=2),
                           qT[:, c, 0:P], kz[:, c, :, 0:P], start=True, stop=True)
                m.then_inc(S("scores_out"), 1)

            gate_mms = [0]

            def gate_columns(upto):
                while gate_mms[0] < upto:
                    u, i = divmod(gate_mms[0], GATE_MMS)
                    n = GATE_UNIT + u
                    if i == 0:
                        name, value = low_ready(n)
                        pe.wait_ge(S(name), value)
                        pe.wait_ge(S("proj_read"), n)
                    ck, p = divmod(i, len(PRODUCTS))
                    c, k = divmod(ck, KD)
                    wp, hp = PRODUCTS[p]
                    m = mm(ps[:, 6, c * T:(c + 1) * T], w_parts[part_slot(n)][wp][:, k, c * P:(c + 1) * P], hT_parts[hp][:, k],
                           start=k + p == 0, stop=k == KD - 1 and p == len(PRODUCTS) - 1)
                    if i == GATE_MMS - 1:
                        m.then_inc(S("unit_used"), 1)
                    gate_mms[0] += 1

            scores(0)
            gate_columns(GATE_MMS)
            for n in range(NPAIR):
                if n + 1 < NPAIR:
                    scores(n + 1)
                for h in range(2):
                    hd = 2 * n + h
                    pe.wait_ge(S("probs_ready"), 2 * hd + 2)
                    for g in range(NG_ATT):
                        i = hd * NG_ATT + g
                        if i:
                            pe.wait_ge(S("PT_ready"), i)
                        src = Ssb[:, n % 2, h]
                        tr(ps[:, 5, 0:P], src[:, g * P:(g + 1) * P])
                        tr(ps[:, 5, P:2 * P], src[:, 384 + g * T:384 + g * T + P])
                        tr(ps[:, 5, 2 * P:3 * P], src[:, 384 + g * T + P:384 + (g + 1) * T]).then_inc(S("PT_out"), 1)
                        gate_columns(gates_due(i))
                        if g == 0 and h == 0 and n >= 1:
                            pe.wait_ge(S("yb_read"), n)
                        pe.wait_ge(S("PT_ready"), i + 1)
                        rows = slice(h * HD, (h + 1) * HD)
                        vc = slice(g * RW + hd * HD, g * RW + (hd + 1) * HD)
                        mm(ps[rows, 7, 0:T], vtok[:, 0, vc], PT[:, i % 2, 0:T], start=g == 0, stop=False,
                           skip_group_check=True)
                        m = mm(ps[rows, 7, P:T], vtok[:, 1, vc], PT[:, i % 2, T:T + P], start=False, stop=g == 2,
                               skip_group_check=True)
                        m.then_inc(S("PV_done"), 1)

            for j in range(4):
                n = MERGE_UNIT + j
                name, value = low_ready(n)
                pe.wait_ge(S(name), value)
                if j >= 2:
                    pe.wait_ge(S("merged"), j - 1)
                w = [x.rearrange("p (b k c) -> p b k c", b=2, k=NPAIR) for x in unit_parts(n)]
                for b in range(2):
                    if j == 0:
                        pe.wait_ge(S("y_low"), 3 if b else 1)
                    for c in range(2):
                        for k in range(NPAIR):
                            for wp, yp in PRODUCTS:
                                m = mm(ps[:, 2 * (j % 2) + b, c * T:(c + 1) * T], w[wp][:, b, k, c * P:(c + 1) * P],
                                       yT_parts[yp][:, b, k], start=k + wp + yp == 0, stop=k == NPAIR - 1 and yp == 1)
                m.then_inc(S("unit_used"), 1)

            for u in range(4):
                n = OUT_UNIT + u
                name, value = low_ready(n)
                pe.wait_ge(S(name), value)
                w = [x.rearrange("p (k c) -> p k c", k=2) for x in unit_parts(n)]
                pe.wait_ge(S("m_low"), u + 1)
                for t in range(NT):
                    for k in range(2):
                        kk = 2 * u + k
                        for hf in range(2):
                            for wp, yp in PRODUCTS:
                                m = mm(ps[:, 4 + 2 * t + hf], mT_parts[yp][:, kk, t * P:(t + 1) * P],
                                       w[wp][:, k, hf * 512:(hf + 1) * 512], start=kk + wp + yp == 0,
                                       stop=kk == KD - 1 and yp == 1)
                    m.then_inc(S("mixed_out" if t == 0 else "unit_used"), 1)
            for t in range(NT):
                pe.wait_ge(S("h2_ready"), t + 1)
                for hf in range(2):
                    for k in range(4):
                        m = tr(ps[:, 2 * t + hf, k * P:(k + 1) * P], h2[:, t, (4 * hf + k) * P:(4 * hf + k + 1) * P])
                    m.then_inc(S("h2T_out"), 1)
            pe.wait_ge(S("ld_wr"), 16)
            for t in range(NT):
                pe.wait_ge(S("h2T_kept" if t else "h2T_ready"), 2)
                for k in range(KD):
                    m = mm(ps[:, 4 + t, 0:36], h2T[:, k, t * P:(t + 1) * P], wr[:, k], start=k == 0, stop=k == KD - 1)
            m.then_inc(S("logits_out"), 1)
            pe.wait_ge(S("zero_ready"), 1)
            for j in range(4):
                mm(ps[:, j], zero, c_all[:, 0:512], start=True, stop=False, skip_group_check=True)
            pe.wait_ge(S("mask_ready"), 1)
            chosen = rt[:, :, EG:36]
            mm(ps[:, 6, 0:E], C("before"), chosen[:, 0], start=True, stop=True)
            mm(ps[:, 6, E:2 * E], C("ones"), chosen[:, 0], start=True, stop=False)
            mm(ps[:, 6, E:2 * E], C("before"), chosen[:, 1], start=False, stop=True)
            mm(ps[:, 6, 2 * E:3 * E], C("ones"), chosen[:, 0], start=True, stop=False)
            mm(ps[:, 6, 2 * E:3 * E], C("ones"), chosen[:, 1], start=False, stop=True).then_inc(S("pos_out"), 1)

            pe.wait_ge(S("passes_ready"), 1)
            passes = pe.value_load(npass_i[0:1, 0:1], min_val=1, max_val=NPASS)
            for name in ("ysb0_ready", "ysb1_ready", "batch_done", "gu_used", "gu_half_used"):
                pe.sem_inc(S(name), 1)
            with pe.Fori(0, passes) as b:
                with pe.Fori(0, NBATCH // 2) as i:
                    for q in range(2):
                        trip = b * (NBATCH // 2) + i
                        done = 2 * trip + q
                        if q == 0:
                            pe.wait_ge(S("sel_ready"), (NBATCH // 2) * b + i + 1)
                        pe.wait_ge(S("ysb0_ready"), done + 1)
                        pe.wait_ge(S("ysb1_ready"), done + 1)
                        for k in range(KD):
                            for t in range(NT):
                                m = mm(ps[:, 4 + k // 4, (k % 4) * P:(k % 4 + 1) * P], h2[:, t, k * P:(k + 1) * P],
                                       sel[:, t, bass.ds(i * (2 * P) + q * P, P)], start=t == 0, stop=t == NT - 1)
                            if k % 4 == 3:
                                m.then_inc(S("gath_out"), 1)
                        for k in range(KD):
                            if k % (KD // 2) == 0:
                                kh = k // (KD // 2)
                                pe.wait_ge(S(f"gu_landed{q}{kh}"), 16 * BATCH * (trip + 1))
                                pe.wait_ge(S(f"gath{kh}_ready"), done + 1)
                            if k == KD // 2:
                                m.then_inc(S("gu_half_used"), 1)
                            for e in range(BATCH):
                                m = mm(ps[e * SLOTS:(e + 1) * SLOTS, 6], hg[:, k, e * SLOTS:(e + 1) * SLOTS],
                                       gu_w[q][e][:, k], start=k == 0, stop=k == KD - 1)
                        m.then_inc(S("gu_used"), 1)
                        pe.wait_ge(S("selw_ready"), done + 1)
                        for t in range(NT):
                            m = tr(ps[:, 7, t * P:(t + 1) * P], selw[:, t])
                        m.then_inc(S("selwT_out"), 1)
                        pe.wait_ge(S("act_ready"), done + 1)
                        for f in range(F // P):
                            m = tr(ps[:, 7, T + f * P:T + (f + 1) * P], act[:, f * P:(f + 1) * P])
                        m.then_inc(S("actT_out"), 1)
                        for e in range(BATCH):
                            pe.wait_ge(S(f"dn_landed{e}"), 32 * trip + 16 * q + 16)
                        pe.wait_ge(S("actT_ready"), done + 1)
                        for hf in range(2):
                            for f in range(F // P):
                                for e in range(BATCH):
                                    m = mm(ps[e * SLOTS:(e + 1) * SLOTS, 4 + hf], actT[:, f, e * SLOTS:(e + 1) * SLOTS],
                                           dn_w[e][:, f, hf * 512:(hf + 1) * 512], start=f == 0, stop=f == F // P - 1)
                            m.then_inc(S("dn_out"), 1)
                        pe.wait_ge(S("selwT_ready"), done + 1)
                        for hf in range(2):
                            pe.wait_ge(S(f"ysb{hf}_ready"), done + 2)
                            for t in range(NT):
                                m = mm(ps[:, 2 * t + hf], selwT[:, t], ysb[:, hf * 512:(hf + 1) * 512],
                                       start=False, stop=False, skip_group_check=True)
                        m.then_inc(S("batch_done"), 1)
            for j in range(4):
                m = mm(ps[:, j, 0:1], zero, c_all[:, 0:1], start=False, stop=True, skip_group_check=True)
            m.then_inc(S("moe_done"), 1)

            pe.wait_ge(S("ld_wpp"), 16)
            pe.wait_ge(S("ld_pT"), 16)
            for t in range(NT):
                for hf in range(2):
                    for k in range(2):
                        m = mm(ps[:, 4 + 2 * t + hf], pT_sb[:, k, t * P:(t + 1) * P], wpp_sb[:, k, hf * 512:(hf + 1) * 512],
                               start=k == 0, stop=k == 1)
            for t in range(NT):
                pe.wait_ge(S("h3_ready"), t + 1)
                pe.wait_ge(S("x2_ready"), 2)
                for hf in range(2):
                    for k in range(4):
                        m = tr(ps[:, 2 * t + hf, k * P:(k + 1) * P], h3[:, t, (4 * hf + k) * P:(4 * hf + k + 1) * P])
                    m.then_inc(S("h3T_out"), 1)
            for t in range(NT):
                pe.wait_ge(S("h3T_ready"), 2 * t + 2)
                pe.wait_ge(S("h3T_low"), 2 * t + 2)
                order = [(j, hf) for j in range(WPG_PIECES) for hf in range(2)]
                if t:
                    order.sort(key=lambda x: x[1])
                for j, hf in order:
                    name, value = wpg_low(j)
                    pe.wait_ge(S(name), value)
                    w = wpg_parts(j)
                    for kk in range(KD // WPG_PIECES):
                        k = j * KD // WPG_PIECES + kk
                        for wp, hp in PRODUCTS:
                            m = mm(ps[:, 2 * t + hf], h3T_parts[hp][:, k, t * P:(t + 1) * P], w[wp][:, kk, hf * 512:(hf + 1) * 512],
                                   start=k + wp + hp == 0, stop=k == KD - 1 and hp == 1)
                    if j == WPG_PIECES - 1:
                        m.then_inc(S("gate_out"), 1)

        @block.scalar
        def _(a):
            do = Chain(a, "act")
            A = nc.scalar.activation
            eps = C("eps")

            def copy(o, i, scale=1.0):
                return A(o, i, ACT.Copy, scale=scale)

            for j in range(XPARTS):
                a.wait_ge(S(f"ld_xT{j}"), 16)
                ks = slice(j * KD // XPARTS, (j + 1) * KD // XPARTS)
                A(sq[:, ks], xT_sb[:, ks], ACT.Square).then_inc(S("sq_ready"), 1)
                if j == 1:
                    a.wait_ge(S("ld_cst"), 16)
                    do(A(stat_a[:, 24:25], eps[:, 0:1], ACT.Sqrt))
            a.wait_ge(S("ld_cst"), 16)
            a.wait_ge(S("ld_cvec"), 16)
            a.wait_ge(S("ssq_done"), 1)
            A(rstd_bc, ps[:, 7, 0:T], ACT.Sqrt, scale=1.0 / D, bias=eps[:, 0:1]).then_inc(S("rms_ready"), 1)
            a.wait_ge(S("zeroed"), 1)

            def take_unit(n):
                a.wait_ge(S("unit_used"), n + 1)
                if n:
                    a.wait_ge(S("z_ready"), n)
                copy(shift[:, :, 1:T + 1], ps[:, n % RING].rearrange("p (c t) -> p c t", c=2)).then_inc(S("proj_read"), 1)

            take_unit(0)
            a.wait_ge(S("z_ready"), 1)
            A(lin[0:W_LORA, 0], lin[0:W_LORA, 0], ACT.Tanh).then_inc(S("lora_in"), 1)
            A(lin[:, 1], lin[:, 1], ACT.Sigmoid).then_inc(S("lora_in"), 1)
            take_unit(1)
            for kind, dst, name in ((0, swT, "w0"), (1, aT_, "a0")):
                a.wait_ge(S("lora_out"), kind + 1)
                for c in range(NPAIR):
                    ins = A(dst[:, c], ps[:, 3 + 2 * kind + c // 2, (c % 2) * T:(c % 2 + 1) * T], ACT.Sigmoid, bias=V(name, c))
                    if c == NPAIR - 1:
                        ins.then_inc(S("lora_read"), 1)
                    else:
                        do(ins)
            a.wait_ge(S("lora_out"), 3)
            copy(gT.rearrange("p n t -> p (n t)"), ps[:, 3:5].rearrange("p b t -> p (b t)")).then_inc(S("lora_read"), 1)
            take_unit(2)
            take_unit(3)
            a.wait_ge(S("cum_ready"), 1)
            A(wincT, cumT, ACT.Exp, scale=-DECAY).then_inc(S("winc_ready"), 1)
            A(winvT, cumT, ACT.Exp, scale=DECAY).then_inc(S("winv_ready"), 1)
            a.wait_ge(S("cumx_ready"), 1)
            A(wexT, wexT, ACT.Exp, scale=-DECAY).then_inc(S("wex_ready"), 1)
            take_unit(4)
            a.wait_ge(S("headsum"), 1)
            A(alT.rearrange("p n t -> p (n t)"), ps[:, 5:7].rearrange("p b t -> p (b t)"), ACT.Sqrt, bias=eps[:, 2:3])\
                .then_inc(S("kknorm"), 1)
            take_unit(5)
            take_unit(6)
            for i, dst in enumerate((Btok, Ktok, Atok, Vtok)):
                if i == 2:
                    a.wait_ge(S("arz_zeroed"), 1)
                    a.wait_ge(S("al_ready"), 1)
                    copy(arz[HD:P, :, 0, 1], alT[HD:P]).then_inc(S("arz_act"), 1)
                    a.wait_ge(S("rho_ready"), 1)
                    for h in range(2):
                        copy(arz[h * HD:(h + 1) * HD, :, 1, h], rhoT[h * HD:(h + 1) * HD]).then_inc(S("arz_act"), 1)
                for t in range(NT):
                    j = NT * i + t
                    a.wait_ge(S("tok_out"), j + 1)
                    copy(dst[:, t], ps[:, (7, 0, 1, 6)[j % 4]]).then_inc(S("tok_read"), 1)

            def take_M(t):
                for g in range(2):
                    if t:
                        a.wait_ge(S("mlev_ready"), 2 * (LEVELS - 1) * t)
                        a.wait_ge(S("X_ready"), 2 * (LEVELS - 1) * t)
                    a.wait_ge(S("M_out"), 2 * t + g + 1)
                    copy(M_sb[:, 4 * g:4 * g + 4].rearrange("p h t -> p (h t)"), ps[:, 6 + g]).then_inc(S("M_ready"), 1)

            def take_first(t, l):
                for g in range(2):
                    a.wait_ge(S("T1_out"), 2 * (LEVELS - 1) * t + 2 * (l - 1) + g + 1)
                    copy(T1_sb[:, 4 * g:4 * g + 4].rearrange("p h t -> p (h t)"), ps[:, 2 + g]).then_inc(S("T1_ready"), 1)

            def take_inverse(t, between=lambda: None):
                a.wait_ge(S("NV_out"), t + 1)
                copy(NV, ps[:, 2]).then_inc(S("NV_ready"), 1)
                a.wait_ge(S("XAT_out"), t + 1)
                copy(XAT2[t].rearrange("p n t -> p (n t)"), ps[:, 3]).then_inc(S("XAT_ready"), 1)
                between()
                a.wait_ge(S("XNV_out"), t + 1)
                copy(XNV2[t], ps[:, 4]).then_inc(S("XNV_ready"), 1)

            def deviation(t):
                a.wait_ge(S("var_ready"), t + 1)
                A(stat_a[:, 0:8], stat_a[:, 0:8], ACT.Sqrt, scale=1.0 / HD, bias=eps[:, 1:2]).then_inc(S("sd_ready"), 1)

            def take_q(n):
                a.wait_ge(S("unit_used"), n + 1)
                copy(qT[:, 2 * (n - Q_UNIT):2 * (n - Q_UNIT) + 2], ps[:, 6 + n % 2].rearrange("p (c t) -> p c t", c=2),
                     scale=HD ** -0.5).then_inc(S("proj_read"), 1)

            take_M(0)
            for l in range(1, LEVELS):
                take_first(0, l)
            take_inverse(0)
            take_M(1)
            def high_part(n, slot, to=None):
                a.wait_ge(S(f"unit_landed{slot}"), 16 * (n // RING) + 16)
                copy(w_parts[slot if to is None else to][0], ring[slot].rearrange("p (k c) -> p k c", k=KD)).then_inc(S("w_high"), 1)

            def late_high(n):
                a.wait_ge(S(f"unit_landed{n % RING}"), 16 * (n // RING) + 16)
                copy(unit_parts(n)[0], ring[n % RING]).then_inc(S("w_high"), 1)

            for l in range(1, LEVELS):
                take_first(1, l)
                if l == LEVELS - 2:
                    a.wait_ge(S("mats_out"), 16)
                    late_high(Q_UNIT)
            a.wait_ge(S("Y_out"), 1)
            copy(hT_parts[0], hT).then_inc(S("hT_high"), 1)
            take_inverse(1, lambda: deviation(0))
            late_high(Q_UNIT + 1)
            for n in range(Q_UNIT, Q_UNIT + 3):
                take_q(n)
                late_high(n + 2)
            deviation(1)
            take_q(Q_UNIT + 3)
            late_high(Q_UNIT + 5)
            a.wait_ge(S("ya_out"), NT)
            high_part(K_UNIT, K_UNIT % RING)
            take_q(Q_UNIT + 4)
            high_part(K_UNIT + 1, (K_UNIT + 1) % RING)
            take_q(Q_UNIT + 5)

            a.wait_ge(S("kz_zeroed"), 2)
            with a.Fori(0, 2) as i:
                for j in range(RING):
                    a.wait_ge(S("unit_used"), K_UNIT + RING * i + j)
                    high_part(K_UNIT + RING * i + j + 2, (K_UNIT + j + 2) % RING)
                    a.wait_ge(S("unit_used"), K_UNIT + RING * i + j + 1)
                    for h in range(2):
                        rows = slice(h * HD, (h + 1) * HD)
                        ins = copy(kz[rows, bass.ds(2 * RING * i + 2 * j, 2), h],
                                   ps[rows, (13 + j) % RING].rearrange("p (c t) -> p c t", c=2))
                        ins.then_inc(S("proj_read") if h else S("kz_half"), 1)
            with a.Fori(0, 2) as i:
                for j in range(RING):
                    a.wait_ge(S("unit_used"), V_UNIT + RING * i + j)
                    high_part(V_UNIT + RING * i + j + 2, (V_UNIT + j + 2) % RING)
                    a.wait_ge(S("unit_used"), V_UNIT + RING * i + j + 1)
                    copy(vtok[:, :, bass.ds((RING * i + j) * T, T)], ps[:, (19 + j) % RING].rearrange("p (c t) -> p c t", c=2)
                         ).then_inc(S("proj_read"), 1)

            def exp_of(n, j):
                h, b = divmod(j, 2)
                i = 4 * n + j
                v = Ssb[:, n % 2, h, 0:384] if b == 0 else Ssb[:, n % 2, h, 384:1152]
                a.wait_ge(S("max_ready"), i + 1)
                A(v, v, ACT.Exp, bias=st_max[:, i:i + 1], accum_out=stat_a[:, i:i + 1]).then_inc(S("exp_ready"), 1)

            def take_gates(u):
                a.wait_ge(S("unit_used"), 26 + u)
                copy(gates[:, u // 2, u % 2], ps[:, 6]).then_inc(S("proj_read"), 1)
                n = GATE_UNIT + u + 2
                high_part(n, n % RING, part_slot(n))

            for j in range(4):
                exp_of(0, j)
                if j == 1:
                    take_gates(0)
            gates_taken = 1
            for n in range(NPAIR):
                for i in range(6 * n, 6 * n + 6):
                    a.wait_ge(S("PT_out"), i + 1)
                    if i >= 2:
                        a.wait_ge(S("PV_done"), i - 1)
                    copy(PT[:, i % 2], ps[:, 5, 0:384]).then_inc(S("PT_ready"), 1)
                    while gates_taken < 8 and GATE_MMS * (gates_taken + 1) <= gates_due(i):
                        take_gates(gates_taken)
                        gates_taken += 1
                    if n + 1 < NPAIR and i < 6 * n + 4:
                        exp_of(n + 1, i - 6 * n)
                    if i == 6 * NPAIR - 6:
                        a.wait_ge(S("scores_out"), NPAIR)
                        copy(yT_parts[0][:, 0], yaT).then_inc(S("y_high"), 1)
                    if i == 6 * NPAIR - 5:
                        a.wait_ge(S("yb_read"), NPAIR - 1)
                        copy(yT_parts[0][:, 1, 0:NPAIR - 1], ybT[:, 0:NPAIR - 1]).then_inc(S("y_high"), 1)
                a.wait_ge(S("PV_done"), 6 * n + 6)
                copy(ybT[:, n], ps[:, 7, 0:T]).then_inc(S("yb_read"), 1)
            copy(yT_parts[0][:, 1, NPAIR - 1], ps[:, 7, 0:T]).then_inc(S("y_high"), 1)

            def open_gates(j):
                both = gates[:, j].rearrange("p b t -> p (b t)")
                A(both, both, ACT.Sigmoid).then_inc(S("gates_ready"), 1)

            def merged_high(j):
                a.wait_ge(S("merged"), j + 1)
                copy(mT_parts[0][:, 2 * j:2 * j + 2], ma.rearrange("p (c t) -> p c t", c=2)).then_inc(S("m_high"), 1)

            late_high(MERGE_UNIT + 2)
            a.wait_ge(S("proj_read"), MERGE_UNIT)
            open_gates(0)
            late_high(MERGE_UNIT + 3)
            for j in range(1, 4):
                open_gates(j)
            merged_high(0)
            merged_high(1)
            for u in range(4):
                a.wait_ge(S("unit_used"), OUT_UNIT + u - 1)
                if u == 2:
                    a.wait_ge(S("merged"), 4)
                    a.wait_ge(S("y_low"), 3)
                late_high(OUT_UNIT + u)
                if u < 2:
                    merged_high(2 + u)

            def sd(src, i, junk):
                do(A(junk, src, ACT.Square, accum_out=stat_a[:, 16 + i:17 + i]))
                A(stat_a[:, i:i + 1], stat_a[:, 16 + i:17 + i], ACT.Sqrt, scale=1.0 / D, bias=eps[:, 0:1])\
                    .then_inc(S("rms_ready"), 1)

            junk = hg.rearrange("p k t -> p (k t)")
            do(A(stat_a[:, 24:25], eps[:, 0:1], ACT.Sqrt))
            for t in range(NT):
                a.wait_ge(S("x1_ready"), t + 1)
                sd(x1[:, t], t, h2[:, t])
            for hf in range(2):
                a.wait_ge(S("h2T_out"), hf + 1)
                copy(h2T[:, 4 * hf:4 * hf + 4, 0:P], ps[:, hf].rearrange("p (k t) -> p k t", k=4)).then_inc(S("h2T_ready"), 1)
            a.wait_ge(S("route_max"), 1)
            for t in range(NT):
                A(rt[:, t, 0:EG], rt[:, t, 0:EG], ACT.Exp, bias=stat[:, 16 + t:17 + t], accum_out=stat_a[:, 4 + t:5 + t])\
                    .then_inc(S("route_exp"), 1)
            a.wait_ge(S("route_second"), 1)
            A(stat_a[:, 6:8], stat[:, 20:22], ACT.Exp).then_inc(S("route_exp"), 1)
            a.wait_ge(S("passes_ready"), 1)
            passes = a.value_load(npass_i[0:1, 0:1], min_val=1, max_val=NPASS)
            with a.Fori(0, passes) as b:
                with a.Fori(0, NBATCH // 2) as i:
                    for q in range(2):
                        done = 2 * (b * (NBATCH // 2) + i) + q
                        a.wait_ge(S("gath_out"), 2 * done + 1)
                        copy(hg[:, 0:4].rearrange("p k t -> p (k t)"), ps[:, 4]).then_inc(S("gath0_ready"), 1)
                        a.wait_ge(S("gu_used"), done + 2)
                        A(silu, ps[:, 6, 0:F], ACT.Silu).then_inc(S("silu_ready"), 1)
                        a.wait_ge(S("actT_out"), done + 1)
                        copy(actT.rearrange("p f t -> p (f t)"), ps[:, 7, T:2 * T]).then_inc(S("actT_ready"), 1)
                        a.wait_ge(S("batch_done"), done + 1)
                        a.wait_ge(S("dn_out"), 2 * done + 1)
                        copy(ysb[:, 0:512], ps[:, 4]).then_inc(S("ysb0_ready"), 1)

            def wpg_high(j):
                per = KD // WPG_PIECES
                a.wait_ge(S(f"ld_wpg{j}"), 16)
                copy(wpg_parts(j)[0], wpg_sb[:, per * j:per * (j + 1)]).then_inc(S("w_high"), 1)

            a.wait_ge(S("gu_used"), passes * NBATCH + 1)
            wpg_high(0)
            do(A(stat_a[:, 24:25], eps[:, 0:1], ACT.Sqrt))
            for t in range(NT):
                a.wait_ge(S("x2_ready"), t + 1)
                sd(x1[:, t], 8 + t, junk)
            for j in range(1, WPG_PIECES):
                wpg_high(j)
                if j < 3:
                    for i in range(2 * (j - 1), 2 * j):
                        a.wait_ge(S("h3T_out"), i + 1)
                        t, hf = i // 2, i % 2
                        copy(h3T_parts[0][:, 4 * hf:4 * hf + 4, t * P:(t + 1) * P], ps[:, i].rearrange("p (k t) -> p k t", k=4))\
                            .then_inc(S("h3T_ready"), 1)
            for t in range(NT):
                def open_half(hf):
                    a.wait_ge(S("gate_out"), 2 * t + hf + 1)
                    A(gate[:, t, hf * 512:(hf + 1) * 512], ps[:, 2 * t + hf], ACT.Sigmoid).then_inc(S("gate_ready"), 1)

                def square_half(hf):
                    cols = slice(hf * 512, (hf + 1) * 512)
                    a.wait_ge(S("x3_ready"), 2 * t + hf + 1)
                    A(junk[:, cols], x1[:, t, cols], ACT.Square, accum_out=stat_a[:, 20 + 2 * t + hf:21 + 2 * t + hf])\
                        .then_inc(S("half_ssq"), 1)

                open_half(0)
                if t == NT - 1:
                    square_half(0)
                open_half(1)
                do(A(stat_a[:, 24:25], eps[:, 0:1], ACT.Sqrt))
                if t < NT - 1:
                    square_half(0)
                square_half(1)
                a.wait_ge(S("ssq_ready"), t + 1)
                A(stat_a[:, 10 + t:11 + t], stat_a[:, 28 + t:29 + t], ACT.Sqrt, scale=1.0 / D, bias=eps[:, 0:1])\
                    .then_inc(S("rms_ready"), 1)

        @block.gpsimd
        def _(g_):
            do = Chain(g_, "pool")
            Pg = nc.gpsimd
            do(Pg.memset(shift[:, :, 0:1], 0.0))
            Pg.memset(Th.rearrange("p a n t -> p (a n t)"), 0.0).then_inc(S("zeroed"), 1)
            g_.wait_ge(S("hT_ready"), KD)
            do(Pg.memset(arz.rearrange("p n a h t -> p (n a h t)"), 0.0), "arz_zeroed")
            g_.wait_ge(S("al_ready"), 1)
            Pg.tensor_copy(arz[0:HD, :, 0, 0], alT[0:HD]).then_inc(S("arz_pool"), 1)
            g_.wait_ge(S("ld_crw"), 16)
            g_.wait_ge(S("tok_out"), 8)
            for t in range(NT):
                for l in range(1, LEVELS):
                    for g in range(2):
                        n = 2 * (LEVELS - 1) * t + 2 * (l - 1) + g
                        if l == 1:
                            g_.wait_ge(S("M_ready"), 2 * t + g + 1)
                        if n >= 4:
                            g_.wait_ge(S("T1_out"), n - 3)
                        Pg.tensor_tensor(mlev[:, l % 2, 4 * g:4 * g + 4], M_sb[:, 4 * g:4 * g + 4],
                                         C("level")[:, l * P:(l + 1) * P].unsqueeze(1).broadcast_to([P, 4, P]), ALU.mult)\
                            .then_inc(S("mlev_ready"), 1)
            for n in range(Q_UNIT, K_UNIT):
                if n == Q_UNIT + 1:
                    g_.wait_ge(S("hT_high"), 1)
                    Pg.tensor_tensor(hT_parts[1], hT, hT_parts[0].bitcast(F32), ALU.subtract).then_inc(S("hT_low"), 1)
                g_.wait_ge(S("w_high"), n - Q_UNIT + 1)
                high, low = unit_parts(n)
                Pg.tensor_tensor(low, ring[n % RING], high.bitcast(F32), ALU.subtract).then_inc(S("pool_low"), 1)
            for n in range(GATE_UNIT + 2, MERGE_UNIT):
                slot = part_slot(n)
                g_.wait_ge(S("w_high"), n - Q_UNIT + 1)
                Pg.tensor_tensor(w_parts[slot][1], ring[n % RING].rearrange("p (k c) -> p k c", k=KD),
                                 w_parts[slot][0].bitcast(F32), ALU.subtract).then_inc(S("pool_low"), 1)
            for n in range(MERGE_UNIT, OUT_UNIT):
                g_.wait_ge(S("w_high"), n - Q_UNIT + 1)
                high, low = unit_parts(n)
                Pg.tensor_tensor(low, ring[n % RING], high.bitcast(F32), ALU.subtract).then_inc(S("pool_low"), 1)
            g_.wait_ge(S("unit_used"), UNITS)
            Pg.memset(zero, 0.0).then_inc(S("zero_ready"), 1)
            for j in range(2):
                per = KD // WPG_PIECES
                g_.wait_ge(S("w_high"), UNITS - Q_UNIT + j + 1)
                high, low = wpg_parts(j)
                Pg.tensor_tensor(low, wpg_sb[:, per * j:per * (j + 1)], high.bitcast(F32), ALU.subtract)\
                    .then_inc(S("pool_low"), 1)

        @block.vector
        def _(v):
            do = Chain(v, "dve")
            N = nc.vector
            tt, ts, stt = N.tensor_tensor, N.tensor_scalar, N.scalar_tensor_tensor

            def bc(x, n):
                return x.unsqueeze(2).broadcast_to([x.shape[0], x.shape[1], n])

            def bc1(x, n):
                return x.unsqueeze(1).broadcast_to([x.shape[0], n, x.shape[1]])

            v.wait_ge(S("rms_ready"), 1)
            do(N.reciprocal(rstd_bc, rstd_bc))
            for k in range(KD):
                ins = stt(hT[:, k], xT_sb[:, k], V("norm_mix", k), rstd_bc, ALU.mult, ALU.mult)
                ins.then_inc(S("hT_ready"), 1)
            v.wait_ge(S("hT_ready"), KD)
            zdst = [lin, kT[:, 0:2], kT[:, 2:4], rT[:, 0:2], rT[:, 2:4], vT[:, 0:2], vT[:, 2:4]]

            def shifted(n):
                v.wait_ge(S("proj_read"), n + 1)
                do(tt(dlt, shift[:, :, 0:T], shift[:, :, 1:T + 1], ALU.subtract))
                do(stt(zdst[n][:, 0], dlt[:, 0], V("mu", 2 * n), shift[:, 0, 1:T + 1], ALU.mult, ALU.add))
                do(stt(zdst[n][:, 1], dlt[:, 1], V("mu", 2 * n + 1), shift[:, 1, 1:T + 1], ALU.mult, ALU.add), "z_ready")

            flat = lambda x: x.rearrange("p n t -> p (n t)")
            shifted(0)
            shifted(1)
            shifted(2)
            for c in range(NPAIR):
                do(ts(kkT[:, c], kT[:, c], V("k_k", c), None, ALU.mult))
            do(tt(bT, kkT, kkT, ALU.mult), "kksq_ready")
            v.wait_ge(S("ld_crw"), 16)
            v.wait_ge(S("lora_read"), 1)
            do(N.tensor_tensor_scan(flat(cumT), C("reset"), flat(swT), 0.0, ALU.mult, ALU.add), "cum_ready")
            do(tt(wexT, cumT, swT, ALU.subtract), "cumx_ready")
            shifted(3)
            v.wait_ge(S("lora_read"), 2)
            for c in range(NPAIR):
                do(ts(kaT[:, c], aT_[:, c], 1.0, V("k_a", c), ALU.subtract, ALU.mult))
            do(stt(kaT, kaT, 1.0, kT, ALU.add, ALU.mult))
            shifted(4)
            for c in range(NPAIR):
                do(stt(rhoT[:, c], rT[:, c], V("r_k", c), kaT[:, c], ALU.mult, ALU.mult),
                   "rk_ready" if c == NPAIR - 1 else None)
            v.wait_ge(S("kknorm"), 1)
            do(N.reciprocal(alT, alT), "headsum_read")
            do(tt(kkT, kkT, alT, ALU.mult))
            shifted(5)
            do(tt(bT, kkT, aT_, ALU.mult))
            v.wait_ge(S("winv_ready"), 1)
            do(tt(bT, bT, winvT, ALU.mult), "b_ready")
            do(tt(kaT, kaT, winvT, ALU.mult), "ka_ready")
            v.wait_ge(S("wex_ready"), 1)
            do(stt(alT, wexT, -1.0, kkT, ALU.mult, ALU.mult), "al_ready")
            v.wait_ge(S("headsum"), 2)
            v.wait_ge(S("winc_ready"), 1)
            do(tt(rhoT, rT, wincT, ALU.mult), "rho_ready")
            shifted(6)
            do(tt(bonus, ps[:, 3:5].rearrange("p b (c t) -> p (b c) t", c=2), vT, ALU.mult), "headsum_read")

            def first_level(t, g):
                hh = slice(4 * g, 4 * g + 4)
                if t:
                    v.wait_ge(S("XNV_ready"), t)
                for n in range(2):
                    do(tt(Z_sb[:, 4 * g + 2 * n:4 * g + 2 * n + 2],
                          mats(t, 2 * g + n, 0)[:, 0:2 * P].rearrange("p (h t) -> p h t", h=2), bc1(C("level0T"), 2), ALU.mult))
                do(tt(Z_sb[:, hh], Z_sb[:, hh], bc1(ident, 4), ALU.add), "Z_ready")

            def keep_small_products(t):
                for n in range(NPAIR):
                    for i in range(2):
                        v.wait_ge(S("mats_out"), 8 * t + 2 * n + i + 1)
                        if t == 0 and n == 0 and i == 0:
                            v.wait_ge(S("tok_out"), 8)
                            v.wait_ge(S("arz_act"), 3)
                            v.wait_ge(S("arz_pool"), 1)
                        do(tt(mats(t, n, i), ps[:, 2 + 2 * (n % 2) + i], C("causal"), ALU.mult), "mats_read")
                    if n == 2 or n == 3:
                        first_level(t, n - 2)
                for g in range(2):
                    hh = slice(4 * g, 4 * g + 4)
                    v.wait_ge(S("M_ready"), 2 * t + g + 1)
                    do(tt(X_sb[:, hh], M_sb[:, hh], bc1(C("level")[:, 0:P], 4), ALU.mult))
                    do(tt(X_sb[:, hh], X_sb[:, hh], bc1(ident, 4), ALU.add), "X_ready")

            def double(t, l):
                for g in range(2):
                    hh = slice(4 * g, 4 * g + 4)
                    v.wait_ge(S("D_out"), 2 * (LEVELS - 1) * t + 2 * (l - 1) + g + 1)
                    do(tt(Z_sb[:, hh], Z_sb[:, hh], ps[:, 4 + g].rearrange("p (h t) -> p h t", h=4), ALU.add), "Z_ready")
                    if l < LEVELS - 1:
                        v.wait_ge(S("DT_out"), 2 * (LEVELS - 2) * t + 2 * (l - 1) + g + 1)
                        do(tt(X_sb[:, hh], X_sb[:, hh], ps[:, 6 + g].rearrange("p (h t) -> p h t", h=4), ALU.add), "X_ready")

            def keep_inputs(t, c):
                cc, rows = 2 * t + c, slice(c * CH, (c + 1) * CH)
                if cc == 0:
                    v.wait_ge(S("zeroed"), 1)
                    v.sem_inc(S("state_ready"), 1)
                    do.n["state_ready"] = 1
                v.wait_ge(S("XNV_ready"), t + 1)
                v.wait_ge(S("U_out"), cc + 1)
                do(tt(U_sb[rows], ps[rows, 2 * t], XNV2[t][rows], ALU.add), "U_ready")

            def next_state(t, c):
                cc = 2 * t + c
                v.wait_ge(S("dT_out"), cc + 1)
                for h in range(2):
                    hr = slice(h * HD, (h + 1) * HD)
                    do(tt(Th[hr, cc + 1, :, hr], ps[hr, 2 * t + 1].rearrange("p (n t) -> p n t", n=NPAIR)[:, :, hr],
                          Th[hr, cc, :, hr], ALU.add))
                for h in range(2):
                    hr = slice(h * HD, (h + 1) * HD)
                    do(tt(Th[hr, cc + 1, :, hr], Th[hr, cc + 1, :, hr], bc(wincT[hr, :, (cc + 1) * CH - 1], HD), ALU.mult),
                       "state_ready" if h else None)

            def normed(t):
                v.wait_ge(S("Y_out"), t + 1)
                y8 = ps[:, 2 * t].rearrange("p (h d) -> p h d", h=NH)
                do(N.tensor_reduce(stat[:, 0:8], y8, AX, ALU.add))
                do(ts(stat[:, 0:8], stat[:, 0:8], -1.0 / HD, None, ALU.mult))
                do(tt(yc, y8, bc(stat[:, 0:8], HD), ALU.add))
                do(tt(ysq, yc, yc, ALU.mult))
                do(N.tensor_reduce(stat_a[:, 0:8], ysq, AX, ALU.add), "var_ready")
                v.wait_ge(S("sd_ready"), t + 1)
                do(N.reciprocal(stat[:, 8:16], stat_a[:, 0:8]))
                do(tt(yc, yc, bc(stat[:, 8:16], HD), ALU.mult), "yn_ready")

            def gated(t):
                v.wait_ge(S("ynT_out"), t + 1)
                cols = slice(t * P, (t + 1) * P)
                for n in range(NPAIR):
                    do(ts(tmpT[:, n], ps[:, 2 * t + 1, n * P:(n + 1) * P], V("ln_w", n), V("ln_b", n), ALU.mult, ALU.add))
                do(tt(tmpT, tmpT, bonus[:, :, cols], ALU.add))
                do(tt(yaT[:, :, cols], tmpT, gT[:, :, cols], ALU.mult), "ya_out")

            keep_small_products(0)
            for l in range(1, LEVELS):
                double(0, l)
            keep_small_products(1)
            steps = [lambda: keep_inputs(0, 0), lambda: next_state(0, 0), lambda: keep_inputs(0, 1),
                     lambda: next_state(0, 1), lambda: None]
            for l in range(1, LEVELS):
                steps[l - 1]()
                double(1, l)
            normed(0)
            gated(0)
            for c in range(2):
                keep_inputs(1, c)
                next_state(1, c)
            normed(1)
            gated(1)

            def low_part(n, slot):
                v.wait_ge(S("w_high"), n - Q_UNIT + 1)
                tt(w_parts[slot][1], ring[slot].rearrange("p (k c) -> p k c", k=KD), w_parts[slot][0].bitcast(F32), ALU.subtract)\
                    .then_inc(S("w_low"), 1)

            low_part(K_UNIT, K_UNIT % RING)
            do(N.memset(kz[0:HD, :, 1], 0.0), "kz_zeroed")
            do(N.memset(kz[HD:P, :, 0], 0.0), "kz_zeroed")
            low_part(K_UNIT + 1, (K_UNIT + 1) % RING)
            with v.Fori(0, 4) as i:
                for j in range(RING):
                    low_part(K_UNIT + RING * i + j + 2, (K_UNIT + j + 2) % RING)
            v.wait_ge(S("ld_neg"), 16)

            def score(n):
                v.wait_ge(S("scores_out"), n + 1)
                if n >= 2:
                    v.wait_ge(S("PT_out"), 6 * (n - 1))
                for h in range(2):
                    for b in range(2):
                        i = 4 * n + 2 * h + b
                        base, w = (0, P) if b == 0 else (384, T)
                        for g in range(NG_ATT):
                            if b:
                                src = ps[:, g, h * T:(h + 1) * T]
                                bias = neg_sb[:, g, P:384]
                            else:
                                at = (g % 2) * T + h * P
                                src = ps[:, 3 + g // 2, at:at + P]
                                bias = neg_sb[:, g, 0:P]
                            do(stt(Ssb[:, n % 2, h, base + g * w:base + (g + 1) * w], bias, SLOPES[g * 8 + 2 * n + h], src,
                                   ALU.mult, ALU.add), "scores_read")
                        do(N.tensor_reduce(st_max[:, i:i + 1], Ssb[:, n % 2, h, base:base + 3 * w], AX, ALU.max, negate=True),
                           "max_ready")

            def normalise(n):
                for h in range(2):
                    for b in range(2):
                        i = 4 * n + 2 * h + b
                        sl = Ssb[:, n % 2, h, 0:384] if b == 0 else Ssb[:, n % 2, h, 384:1152]
                        v.wait_ge(S("exp_ready"), i + 1)
                        do(N.reciprocal(stat[:, 16 + i:17 + i], stat_a[:, i:i + 1]))
                        do(ts(sl, sl, stat[:, 16 + i:17 + i], None, ALU.mult), "probs_ready")

            score(0)
            normalise(0)
            for n in range(1, NPAIR):
                score(n)
                normalise(n)
            for b, ks in ((0, slice(0, NPAIR)), (1, slice(0, NPAIR - 1)), (1, slice(NPAIR - 1, NPAIR))):
                v.wait_ge(S("y_high"), 1 if b == 0 else 3 if ks.start else 2)
                if ks.start:
                    v.wait_ge(S("yb_read"), NPAIR)
                do(tt(yT_parts[1][:, b, ks], (yaT, ybT)[b][:, ks], yT_parts[0][:, b, ks].bitcast(F32), ALU.subtract), "y_low")

            def late_low(n):
                v.wait_ge(S("w_high"), n - Q_UNIT + 1)
                high, low = unit_parts(n)
                tt(low, ring[n % RING], high.bitcast(F32), ALU.subtract).then_inc(S("w_low"), 1)

            def merge(j):
                v.wait_ge(S("unit_used"), MERGE_UNIT + j + 1)
                v.wait_ge(S("gates_ready"), j + 1)
                do(tt(ma, gates[:, j, 0], ps[:, 2 * (j % 2)], ALU.mult))
                do(tt(mb, gates[:, j, 1], ps[:, 2 * (j % 2) + 1], ALU.mult))
                do(tt(ma, ma, mb, ALU.add), "merged")

            def merged_low(j):
                v.wait_ge(S("m_high"), j + 1)
                do(tt(mT_parts[1][:, 2 * j:2 * j + 2], ma.rearrange("p (c t) -> p c t", c=2),
                      mT_parts[0][:, 2 * j:2 * j + 2].bitcast(F32), ALU.subtract), "m_low")

            for j in range(4):
                merge(j)
                if j >= 2:
                    late_low(OUT_UNIT + j - 2)
                merged_low(j)
            late_low(OUT_UNIT + 2)
            late_low(OUT_UNIT + 3)
            two = lambda b: ps[:, b:b + 2].rearrange("p b n -> p (b n)")
            v.wait_ge(S("ld_x"), 16)
            v.wait_ge(S("ld_gmoe"), 16)
            for t in range(NT):
                v.wait_ge(S("unit_used" if t else "mixed_out"), 41 if t else 4)
                do(tt(x1[:, t], two(4 + 2 * t), xt_sb[:, t], ALU.add), "x1_ready")
            for t in range(NT):
                v.wait_ge(S("rms_ready"), 2 + t)
                do(N.reciprocal(stat[:, t:t + 1], stat_a[:, t:t + 1]))
                do(stt(h2[:, t], x1[:, t], stat[:, t:t + 1], gmoe, ALU.mult, ALU.mult), "h2_ready")

            def keep_h2T(t):
                for hf in range(2):
                    v.wait_ge(S("h2T_out"), 2 * t + hf + 1)
                    do(N.tensor_copy(h2T[:, 4 * hf:4 * hf + 4, t * P:(t + 1) * P],
                                     ps[:, 2 * t + hf].rearrange("p (k t) -> p k t", k=4)), "h2T_kept")

            keep_h2T(1)
            group, ex = rt[:, :, 0:EG], rt[:, :, EG:36]

            def first_max(dst, logits, keys, top):
                n = logits.shape[2]
                do(N.tensor_reduce(top, logits, AX, ALU.max))
                do(tt(dst, logits, bc(top, n), ALU.is_equal))
                do(tt(dst, dst, bc1(keys, NT), ALU.mult))
                do(N.tensor_reduce(stat[:, 24:26], dst, AX, ALU.max))
                do(tt(dst, dst, bc(stat[:, 24:26], n), ALU.is_equal))

            m1, m2, gw, w1, w2, top = [stat[:, c:c + NT] for c in (26, 28, 30, 32, 34, 22)]
            gm = stat[:, 40:40 + NT * EG].rearrange("p (t g) -> p t g", t=NT)
            v.wait_ge(S("logits_out"), 1)
            do(N.tensor_copy(rt, ps[:, 4:6, 0:36]))
            first_max(gm, group, C("key_g"), top)
            do(ts(stat[:, 16:18], top, -1.0, None, ALU.mult), "route_max")
            do(ts(gm, gm, 1.0, -FAR, ALU.subtract, ALU.mult))
            for t in range(NT):
                by_group = ex[:, t].rearrange("p (g e) -> p g e", g=EG)
                do(tt(by_group, by_group, bc(gm[:, t], E // EG), ALU.add))
            first_max(rmask, ex, C("key_e"), m1)
            do(stt(ex, rmask, 3.0 * FAR, ex, ALU.mult, ALU.add))
            first_max(comb, ex, C("key_e"), m2)
            do(tt(stat[:, 20:22], m2, m1, ALU.subtract), "route_second")
            do(tt(ex, rmask, comb, ALU.add), "mask_ready")
            v.wait_ge(S("route_exp"), 3)
            do(N.reciprocal(gw, stat_a[:, 4:6]))
            do(ts(w1, stat_a[:, 6:8], 1.0, None, ALU.add))
            do(N.reciprocal(w1, w1))
            do(tt(w1, w1, gw, ALU.mult))
            do(tt(w2, stat_a[:, 6:8], w1, ALU.mult))
            do(tt(posm, comb, bc(w2, E), ALU.mult))
            do(tt(comb, rmask, bc(w1, E), ALU.mult))
            do(tt(comb, comb, posm, ALU.add))
            v.wait_ge(S("pos_out"), 1)
            do(ts(posm, ex, -4096.0, 4096.0, ALU.mult, ALU.add))
            do(tt(posm, posm, ps[:, 6, 0:NT * E].rearrange("p (t e) -> p t e", t=NT), ALU.add))
            do(N.tensor_reduce(stat[:, 0:1], ps[:, 6, 2 * E:3 * E], AX, ALU.max))
            do(ts(stat[:, 48:48 + NPASS], C("full"), stat[:, 0:1], None, ALU.is_lt))
            do(N.tensor_reduce(stat[:, 1:2], stat[:, 48:48 + NPASS], AX, ALU.add))
            do(N.tensor_copy(npass_i[0:1, 0:1], stat[0:1, 1:2]), "passes_ready")
            passes = v.value_load(npass_i[0:1, 0:1], min_val=1, max_val=NPASS)
            e4 = lambda x: x.rearrange("p (e s) -> p e s", s=SLOTS)
            with v.Fori(0, passes) as b:
                v.wait_ge(S("batch_done"), NBATCH * b + 1)
                for i in range(NBATCH // 2):
                    es = slice(2 * BATCH * i, 2 * BATCH * (i + 1))
                    tt(sel[:, :, 2 * P * i:2 * P * (i + 1)].rearrange("p t (e s) -> p t e s", s=SLOTS),
                       C("slot")[:, bass.ds(SLOTS * b, SLOTS)].unsqueeze(1).unsqueeze(1).broadcast_to([P, NT, 2 * BATCH, SLOTS]),
                       posm[:, :, es].unsqueeze(3).broadcast_to([P, NT, 2 * BATCH, SLOTS]), ALU.is_equal)\
                        .then_inc(S("sel_ready"), 1)
                with v.Fori(0, NBATCH // 2) as i:
                    for q in range(2):
                        done = 2 * (b * (NBATCH // 2) + i) + q
                        if q == 0:
                            v.wait_ge(S("sel_ready"), (NBATCH // 2) * b + i + 1)
                        for t in range(NT):
                            ins = tt(e4(selw[:, t]), e4(sel[:, t, bass.ds(i * 2 * P + q * P, P)]),
                                     bc(comb[:, t, bass.ds(i * 2 * BATCH + q * BATCH, BATCH)], SLOTS), ALU.mult)
                            ins.then_inc(S("selw_ready"), 1)
                        v.wait_ge(S("gath_out"), 2 * done + 2)
                        N.tensor_copy(hg[:, 4:8].rearrange("p k t -> p (k t)"), ps[:, 5]).then_inc(S("gath1_ready"), 1)
                        v.wait_ge(S("batch_done"), done + 1)
                        v.wait_ge(S("selwT_out"), done + 1)
                        N.tensor_copy(selwT.rearrange("p a t -> p (a t)"), ps[:, 7, 0:T]).then_inc(S("selwT_ready"), 1)
                        v.wait_ge(S("silu_ready"), done + 1)
                        tt(act, silu, ps[:, 6, F:2 * F], ALU.mult).then_inc(S("act_ready"), 1)
                        v.wait_ge(S("dn_out"), 2 * done + 2)
                        N.tensor_copy(ysb[:, 512:1024], ps[:, 5]).then_inc(S("ysb1_ready"), 1)
            v.wait_ge(S("moe_done"), 1)
            v.wait_ge(S("ld_gple"), 16)
            for t in range(NT):
                do(tt(x1[:, t], x1[:, t], two(2 * t), ALU.add), "x2_ready")
            for t in range(NT):
                v.wait_ge(S("rms_ready"), 4 + t)
                do(N.reciprocal(stat[:, 8 + t:9 + t], stat_a[:, 8 + t:9 + t]))
                do(stt(h3[:, t], x1[:, t], stat[:, 8 + t:9 + t], gple, ALU.mult, ALU.mult), "h3_ready")

            def wpg_low_part(j):
                per = KD // WPG_PIECES
                v.wait_ge(S("w_high"), UNITS - Q_UNIT + j + 1)
                high, low = wpg_parts(j)
                tt(low, wpg_sb[:, per * j:per * (j + 1)], high.bitcast(F32), ALU.subtract).then_inc(S("w_low"), 1)

            def h3T_low_part(i):
                v.wait_ge(S("h3T_ready"), i + 1)
                t, hf = i // 2, i % 2
                at = slice(4 * hf, 4 * hf + 4), slice(t * P, (t + 1) * P)
                do(tt(h3T_parts[1][:, at[0], at[1]], ps[:, i].rearrange("p (k t) -> p k t", k=4),
                      h3T_parts[0][:, at[0], at[1]].bitcast(F32), ALU.subtract), "h3T_low")

            h3T_low_part(0)
            h3T_low_part(1)
            wpg_low_part(2)
            h3T_low_part(2)
            h3T_low_part(3)
            wpg_low_part(3)
            v.wait_ge(S("ld_gfin"), 16)
            for t in range(NT):
                for hf in range(2):
                    cols = slice(hf * 512, (hf + 1) * 512)
                    v.wait_ge(S("gate_ready"), 2 * t + hf + 1)
                    do(tt(gate[:, t, cols], gate[:, t, cols], ps[:, 4 + 2 * t + hf], ALU.mult))
                    do(tt(x1[:, t, cols], x1[:, t, cols], gate[:, t, cols], ALU.add), "x3_ready")
                v.wait_ge(S("half_ssq"), 2 * t + 2)
                do(tt(stat_a[:, 28 + t:29 + t], stat_a[:, 20 + 2 * t:21 + 2 * t], stat_a[:, 21 + 2 * t:22 + 2 * t], ALU.add),
                   "ssq_ready")
                v.wait_ge(S("rms_ready"), 6 + t)
                do(N.reciprocal(stat[:, 10 + t:11 + t], stat_a[:, 10 + t:11 + t]))
                for hf in range(2):
                    cols = slice(hf * 512, (hf + 1) * 512)
                    stt(x1[:, t, cols], x1[:, t, cols], stat[:, 10 + t:11 + t], gfin[:, cols], ALU.mult, ALU.mult)\
                        .then_inc(S("out_ready"), 1)


def _constants(np):
    f = np.float32
    i = np.arange(P)
    c = np.zeros((P, N_CRW), f)

    def put(name, a):
        at, n = CST[name]
        c[:, at:at + n] = a

    s, t = i[:, None], i[None, :]
    same = (s // CH) == (t // CH)
    put("ident", np.eye(P))
    put("ones", 1.0)
    put("before", s < t)
    put("slot", np.arange(T))
    put("key_g", np.arange(EG, 0, -1))
    put("key_e", np.arange(E, 0, -1))
    put("full", np.arange(NPASS) * SLOTS)
    put("eps", np.array([EPS, GN_EPS, 1e-12, 0.0]))
    put("block", (s // HD) == (t // HD))
    put("causal", np.concatenate([(s < t) & same] * 2 + [(s <= t) & same] * 2, 1))
    lev = [((s // (2 * b)) == (t // (2 * b))) & ((s // b) % 2 == 1) & ((t // b) % 2 == 0) for b in (2 ** l for l in range(LEVELS))]
    put("level", np.concatenate(lev, 1))
    put("level0T", lev[0].T)
    put("reset", np.tile((np.arange(T) % CH != 0), NPAIR))
    neg = np.zeros((P, NG_ATT, 384), f)
    for g, (window, d) in enumerate(((128, 1), (512, 4), (2048, 16))):
        for b in range(2):
            keys = np.arange(P * (b + 1))
            dist = (b * P + i)[:, None] - keys[None, :]
            ok = (dist >= 0) & (dist % d == 0) & (dist <= window)
            neg[:, g, (0 if b == 0 else P):(P if b == 0 else 384)] = np.where(ok, -dist, FAR)
    return c[:, :N_CST].copy(), c[:, N_CST:].copy(), neg


def kernel(**inp):
    import numpy as np
    import concourse.bacc as bacc
    from concourse.bass_utils import run_bass_kernel_spmd as run

    w = {k: np.asarray(v) for k, v in inp.items()}
    con = np.ascontiguousarray

    def kp(a):
        return con(a.reshape(-1, P, a.shape[-1]).transpose(1, 0, 2))

    def col(a):
        return a.reshape(-1, P).T

    x = w["x"][0]
    win = w["w_in"][0]
    RC = 3 * RW + 256
    AC = 3 * NG_ATT * RW
    units = []

    def cols(at, n):
        for c in range(0, n, T):
            units.append(kp(win[:, at + c:at + c + T]).reshape(P, UNIT))

    cols(3 * RW, 256)
    cols(RW, RW)
    cols(0, RW)
    cols(2 * RW, RW)
    cols(RC, AC)
    pa, pb = w["w_proj_a"][0], w["w_proj_b"][0]
    for m in range(4):
        cols(RC + AC + m * T, T)
        cols(RC + AC + D + m * T, T)
    for m in range(4):
        units.append(np.concatenate([kp(pa[:, m * T:(m + 1) * T]).reshape(P, -1), kp(pb[:, m * T:(m + 1) * T]).reshape(P, -1)], 1))
    wo = kp(w["w_out"][0])
    for u in range(4):
        units.append(wo[:, 2 * u:2 * u + 2].reshape(P, UNIT))
    mu = w["rwkv_mu"][0]
    mu = np.concatenate([mu[3 * RW:], mu[RW:2 * RW], mu[:RW], mu[2 * RW:3 * RW]])
    cvec = np.concatenate([col(w["norm_mix"][0]), col(mu)] + [col(w[n][0].reshape(-1)) for n in (
        "rwkv_w0", "rwkv_a0", "rwkv_k_k", "rwkv_k_a", "rwkv_r_k", "rwkv_ln_w", "rwkv_ln_b")], 1)
    lora = np.zeros((P, 2, RW), np.float32)
    lora[:64, 0] = w["rwkv_w2"][0]
    lora[64:, 1] = w["rwkv_a2"][0]
    gains = np.stack([np.broadcast_to(g, (P, D)) for g in (w["norm_moe"][0], w["norm_ple"][0], w["norm_final"])])
    wr = np.concatenate([w["w_router_group"][0], w["w_router_expert"][0].transpose(1, 0, 2).reshape(D, E)], 1)
    gu = np.concatenate([w["w_exp_gate"][0], w["w_exp_up"][0]], -1).reshape(E, KD, P, 2 * F).transpose(0, 2, 1, 3)
    dn = w["w_exp_down"][0].reshape(E, F // P, P, D).transpose(0, 2, 1, 3)
    cst, crw, neg = _constants(np)
    arrays = {
        "xT": kp(x.T), "xtok": kp(x), "pT": kp(w["p"][0, 0].T), "cst": cst, "crw": crw, "neg": neg, "cvec": cvec,
        "lora": lora, "g2": w["rwkv_g2"][0], "stream": np.stack(units), "gain3": gains, "router": kp(wr),
        "wgu": gu, "wd": dn, "wpg": kp(w["w_ple_gate"][0]), "wpp": kp(w["w_ple_proj"][0]),
    }
    nc = bacc.Bacc("TRN2", target_bir_lowering=False, num_devices=1)
    args = []
    for name, a in arrays.items():
        arrays[name] = con(a)
        args.append(nc.dram_tensor(name, a.shape, F32, kind="ExternalInput").ap())
    o = nc.dram_tensor("out", (1, T, D), F32, kind="ExternalOutput").ap()
    program(nc, *args, o)
    r = run(nc, [arrays], core_ids=[0])
    return r.results[0]["out"]
```
